# Optimizing a Trainium2 kernel written in Bass

```python
import jax, jax.numpy as jnp
from jax import lax
import numpy as np

D_MODEL = 1024
BATCH = 1
SEQ = 1024
DEPTH = 1
DEC_BATCH = 8
DEC_SEQ = 8
PAST_LEN = 1024
PAGE_SIZE = 128

ATT_HEAD_DIM = 64
ATT_GROUPS = ((128, 1), (512, 4), (2048, 16))
N_ATT_GROUPS = 3
ATT_HEADS_PER_GROUP = 4
ATT_HEADS = N_ATT_GROUPS * ATT_HEADS_PER_GROUP
ATT_WIDTH = ATT_HEADS * ATT_HEAD_DIM
ATT_OUT_WIDTH = ATT_HEADS_PER_GROUP * ATT_HEAD_DIM
ATT_BLOCK = 128
ALIBI_MAX_EXP = 8.0

HG_HEADS = 4
HG_DK = 128
HG_DV = 128
HG_KW = HG_HEADS * HG_DK
HG_VW = HG_HEADS * HG_DV
HG_CHUNK = 64

PEER_HEADS = 8
PEER_NKEYS = 128
PEER_EXPERTS = PEER_NKEYS * PEER_NKEYS
PEER_DHALF = 128
PEER_DQ = 2 * PEER_DHALF
PEER_TOPK = 16
PEER_BLOCK = 256

N_MOD = 6
NORM_EPS = 1e-6

IN_SPLITS = (ATT_WIDTH, ATT_WIDTH, ATT_WIDTH, HG_KW, HG_VW, HG_KW, HG_VW, D_MODEL, D_MODEL)
IN_COLS = sum(IN_SPLITS)

kernel_name = "hybrid_dilated_attn_hgrn2_peer_adaln_step"

F32 = jnp.float32

def rms_norm(x, g):
    xf = x.astype(F32)
    y = xf * lax.rsqrt(jnp.mean(xf * xf, axis=-1, keepdims=True) + NORM_EPS)
    return y.astype(x.dtype) * g

def alibi_slopes():
    return jnp.exp2(-ALIBI_MAX_EXP * jnp.arange(1, ATT_HEADS + 1, dtype=F32) / ATT_HEADS)

def dilated_attn_prompt(q, k, v, window, dil, slopes):
    B, S, H, Dh = q.shape
    n_taps = window // dil
    span = dil * ATT_BLOCK
    Sp = -(-S // span) * span
    L = Sp // dil
    nb = L // ATT_BLOCK

    def to_sub(a):
        a = jnp.pad(a, ((0, 0), (0, Sp - S), (0, 0), (0, 0)))
        a = a.reshape(B, L, dil, H, Dh).transpose(0, 2, 1, 3, 4)
        return a.reshape(B, dil, nb, ATT_BLOCK, H, Dh)

    def with_prev(a):
        prev = jnp.concatenate([jnp.zeros_like(a[:, :, :1]), a[:, :, :-1]], axis=2)
        return jnp.concatenate([prev, a], axis=3)

    def from_sub(a):
        rest = a.shape[5:]
        a = a.reshape((B, dil, L, H) + rest)
        a = jnp.moveaxis(a, 1, 2)
        return a.reshape((B, Sp, H) + rest)[:, :S]

    qb = to_sub(q)
    kk = with_prev(to_sub(k))
    vv = with_prev(to_sub(v))
    i = jnp.arange(ATT_BLOCK)[:, None]
    j = jnp.arange(2 * ATT_BLOCK)[None, :]
    delta = i + ATT_BLOCK - j
    key_sub = jnp.arange(nb)[:, None, None] * ATT_BLOCK + j[None] - ATT_BLOCK
    mask = (delta >= 0) & (delta <= n_taps) & (key_sub >= 0)
    bias = -slopes[:, None, None] * (delta * dil).astype(F32)[None]
    s = jnp.einsum('bgnqhd,bgnkhd->bgnhqk', qb, kk).astype(F32) * (Dh ** -0.5) + bias
    s = jnp.where(mask[:, None], s, -jnp.inf)
    lse = jax.nn.logsumexp(s, axis=-1)
    p = jnp.exp(s - lse[..., None]).astype(v.dtype)
    o = jnp.einsum('bgnhqk,bgnkhd->bgnqhd', p, vv)
    return from_sub(o), from_sub(jnp.swapaxes(lse, -1, -2))

def dilated_attn_sample(q, k, v, kbuf, vbuf, window, dil, slopes):
    Bd, T, H, Dh = q.shape
    W = kbuf.shape[1]
    n_taps = window // dil
    kall = jnp.concatenate([kbuf, k], axis=1)
    vall = jnp.concatenate([vbuf, v], axis=1)
    taps = jnp.arange(n_taps + 1)
    idx = W + jnp.arange(T)[:, None] - taps[None, :] * dil
    valid = idx >= 0
    idxc = jnp.clip(idx, 0, None)
    kg = jnp.take(kall, idxc, axis=1)
    vg = jnp.take(vall, idxc, axis=1)
    bias = -slopes[:, None] * (taps * dil).astype(F32)[None, :]
    s = jnp.einsum('bthd,btjhd->bthj', q, kg).astype(F32) * (Dh ** -0.5) + bias
    s = jnp.where(valid[:, None, :], s, -jnp.inf)
    lse = jax.nn.logsumexp(s, axis=-1)
    p = jnp.exp(s - lse[..., None]).astype(v.dtype)
    o = jnp.einsum('bthj,btjhd->bthd', p, vg)
    return o, lse, kall[:, T:], vall[:, T:]

def hgrn2_scan(q, k, v, log_f, s0):
    B, L, H, DK = q.shape
    DV = v.shape[-1]
    C = min(HG_CHUNK, L)
    Lp = -(-L // C) * C
    NC = Lp // C

    def chunks(a):
        a = jnp.pad(a.astype(F32), ((0, 0), (0, Lp - L), (0, 0), (0, 0)))
        return jnp.moveaxis(a.reshape(B, NC, C, H, a.shape[-1]), 1, 0)

    causal = jnp.tril(jnp.ones((C, C), dtype=bool))[None, :, :, None, None]

    def step(S, inp):
        qc, kc, vc, lfc = inp
        b = jnp.cumsum(lfc, axis=1)
        o_inter = jnp.einsum('bthk,bhkv->bthv', qc * jnp.exp(b), S)
        diff = b[:, :, None] - b[:, None, :]
        dec = jnp.exp(jnp.where(causal, diff, -jnp.inf))
        A = jnp.einsum('bthk,bshk,btshk->bhts', qc, kc, dec)
        o_intra = jnp.einsum('bhts,bshv->bthv', A, vc)
        bC = b[:, -1]
        kd = kc * jnp.exp(bC[:, None] - b)
        S_new = jnp.exp(bC)[..., None] * S + jnp.einsum('bshk,bshv->bhkv', kd, vc)
        return S_new, o_inter + o_intra

    S_fin, o = lax.scan(step, s0.astype(F32), (chunks(q), chunks(k), chunks(v), chunks(log_f)))
    o = jnp.moveaxis(o, 0, 1).reshape(B, Lp, H, DV)[:, :L]
    return o, S_fin.astype(s0.dtype)

def token_mixer(h, w_in, w_att_branch, w_hg_branch, w_out, lb, hg_norm_g, slopes, att_caches, s0):
    N, L, _ = h.shape
    proj = h @ w_in
    cuts = [int(c) for c in np.cumsum(IN_SPLITS)[:-1]]
    q, k, v, zf, zi, zq, zg, za, zh = jnp.split(proj, cuts, axis=-1)
    q = q.reshape(N, L, ATT_HEADS, ATT_HEAD_DIM)
    k = k.reshape(N, L, ATT_HEADS, ATT_HEAD_DIM)
    v = v.reshape(N, L, ATT_HEADS, ATT_HEAD_DIM)

    outs, lses, bufs = [], [], []
    for gi, (window, dil) in enumerate(ATT_GROUPS):
        hs = slice(gi * ATT_HEADS_PER_GROUP, (gi + 1) * ATT_HEADS_PER_GROUP)
        if att_caches is None:
            o, lse = dilated_attn_prompt(q[:, :, hs], k[:, :, hs], v[:, :, hs], window, dil, slopes[hs])
            keep = min(window, L)
            kb, vb = k[:, L - keep:, hs], v[:, L - keep:, hs]
        else:
            o, lse, kb, vb = dilated_attn_sample(q[:, :, hs], k[:, :, hs], v[:, :, hs],
                                                 att_caches[2 * gi], att_caches[2 * gi + 1],
                                                 window, dil, slopes[hs])
        outs.append(o)
        lses.append(lse)
        bufs.append(kb)
        bufs.append(vb)
    wg = jax.nn.softmax(jnp.stack(lses, axis=0), axis=0)
    att = jnp.einsum('gnlh,gnlhd->nlhd', wg.astype(h.dtype), jnp.stack(outs, axis=0))
    att = att.reshape(N, L, ATT_OUT_WIDTH)

    f = lb + (1.0 - lb) * jax.nn.sigmoid(zf.astype(F32))
    log_f = jnp.log(f).reshape(N, L, HG_HEADS, HG_DK)
    kh = (1.0 - f).reshape(N, L, HG_HEADS, HG_DK)
    o_h, s_fin = hgrn2_scan(zq.reshape(N, L, HG_HEADS, HG_DK), kh,
                            zi.reshape(N, L, HG_HEADS, HG_DV), log_f, s0)
    o_h = rms_norm(o_h.astype(h.dtype), hg_norm_g) * jax.nn.silu(zg.reshape(N, L, HG_HEADS, HG_DV))
    o_h = o_h.reshape(N, L, HG_VW)

    merged = jax.nn.sigmoid(za) * (att @ w_att_branch) + jax.nn.sigmoid(zh) * (o_h @ w_hg_branch)
    return merged @ w_out, bufs, s_fin

def peer(h, wq, subkeys, u_tab, v_tab):
    N, D = h.shape
    blk = min(PEER_BLOCK, N)
    Np = -(-N // blk) * blk
    hb = jnp.pad(h, ((0, Np - N), (0, 0))).reshape(Np // blk, blk, D)

    def one(xb):
        qry = (xb @ wq).reshape(blk, PEER_HEADS, 2, PEER_DHALF)
        sc = jnp.einsum('thpd,hpkd->thpk', qry, subkeys).astype(F32)
        s1, i1 = lax.top_k(sc[:, :, 0], PEER_TOPK)
        s2, i2 = lax.top_k(sc[:, :, 1], PEER_TOPK)
        cand = (s1[..., :, None] + s2[..., None, :]).reshape(blk, PEER_HEADS, PEER_TOPK * PEER_TOPK)
        sf, ci = lax.top_k(cand, PEER_TOPK)
        e1 = jnp.take_along_axis(i1, ci // PEER_TOPK, axis=-1)
        e2 = jnp.take_along_axis(i2, ci % PEER_TOPK, axis=-1)
        eid = e1 * PEER_NKEYS + e2
        g = jax.nn.softmax(sf, axis=-1)
        ug = jnp.take(u_tab, eid, axis=0)
        vg = jnp.take(v_tab, eid, axis=0)
        act = jax.nn.gelu(jnp.einsum('td,thkd->thk', xb, ug).astype(F32))
        return jnp.einsum('thk,thkd->td', (g * act).astype(xb.dtype), vg)

    return lax.map(one, hb).reshape(Np, D)[:N]

def layer(x, c, ada_w, ada_b, norm1_g, w_in, w_att_branch, w_hg_branch, w_out, lb, hg_norm_g,
          norm2_g, peer_wq, peer_subkeys, peer_u, peer_v, slopes, att_caches, s0):
    mod = jax.nn.silu(c) @ ada_w + ada_b
    sh1, sc1, g1, sh2, sc2, g2 = jnp.split(mod, N_MOD, axis=-1)
    h = rms_norm(x, norm1_g) * (1.0 + sc1[:, None]) + sh1[:, None]
    mix, bufs, s_fin = token_mixer(h, w_in, w_att_branch, w_hg_branch, w_out, lb, hg_norm_g,
                                   slopes, att_caches, s0)
    x = x + g1[:, None] * mix
    h2 = rms_norm(x, norm2_g) * (1.0 + sc2[:, None]) + sh2[:, None]
    N, L, D = x.shape
    ff = peer(h2.reshape(N * L, D), peer_wq, peer_subkeys, peer_u, peer_v).reshape(N, L, D)
    x = x + g2[:, None] * ff
    return x, bufs, s_fin

def setup_inputs(seed: int = 0) -> dict:
    key = jax.random.key(seed)
    ks = jax.random.split(key, 32)

    def nrm(k, shape, scale):
        return jax.random.normal(k, shape, F32) * scale

    def buf_shape(window):
        return (DEPTH, DEC_BATCH, min(window, PAST_LEN), ATT_HEADS_PER_GROUP, ATT_HEAD_DIM)

    D = D_MODEL
    return {
        "x_prompt": nrm(ks[0], (BATCH, SEQ, D), 1.0),
        "x_sample": nrm(ks[1], (DEC_BATCH, DEC_SEQ, D), 1.0),
        "cache_k0": nrm(ks[2], buf_shape(ATT_GROUPS[0][0]), 1.0),
        "cache_v0": nrm(ks[3], buf_shape(ATT_GROUPS[0][0]), 1.0),
        "cache_k1": nrm(ks[4], buf_shape(ATT_GROUPS[1][0]), 1.0),
        "cache_v1": nrm(ks[5], buf_shape(ATT_GROUPS[1][0]), 1.0),
        "cache_k2": nrm(ks[6], buf_shape(ATT_GROUPS[2][0]), 1.0),
        "cache_v2": nrm(ks[7], buf_shape(ATT_GROUPS[2][0]), 1.0),
        "state_hgrn": nrm(ks[8], (DEPTH, DEC_BATCH, HG_HEADS, HG_DK, HG_DV), 0.3),
        "c_prompt": nrm(ks[9], (BATCH, D), 1.0),
        "c_sample": nrm(ks[10], (DEC_BATCH, D), 1.0),
        "ada_w": nrm(ks[11], (DEPTH, D, N_MOD * D), 0.5 * D ** -0.5),
        "ada_b": nrm(ks[12], (DEPTH, N_MOD * D), 0.02),
        "norm1_g": 1.0 + nrm(ks[13], (DEPTH, D), 0.02),
        "w_in": nrm(ks[14], (DEPTH, D, IN_COLS), D ** -0.5),
        "w_att_branch": nrm(ks[15], (DEPTH, ATT_OUT_WIDTH, D), ATT_OUT_WIDTH ** -0.5),
        "w_hg_branch": nrm(ks[16], (DEPTH, HG_VW, D), HG_VW ** -0.5),
        "w_out": nrm(ks[17], (DEPTH, D, D), D ** -0.5),
        "hg_lower_bound": nrm(ks[18], (DEPTH + 1, HG_KW), 0.1),
        "hg_norm_g": 1.0 + nrm(ks[19], (DEPTH, HG_DV), 0.02),
        "norm2_g": 1.0 + nrm(ks[20], (DEPTH, D), 0.02),
        "peer_wq": nrm(ks[21], (DEPTH, D, PEER_HEADS * PEER_DQ), D ** -0.5),
        "peer_subkeys": nrm(ks[22], (DEPTH, PEER_HEADS, 2, PEER_NKEYS, PEER_DHALF), PEER_DHALF ** -0.5),
        "peer_u": nrm(ks[23], (DEPTH, PEER_EXPERTS, D), D ** -0.5),
        "peer_v": nrm(ks[24], (DEPTH, PEER_EXPERTS, D), 0.5),
        "final_norm_g": 1.0 + nrm(ks[25], (D,), 0.02),
    }

def reference(x_prompt, x_sample, cache_k0, cache_v0, cache_k1, cache_v1, cache_k2, cache_v2,
              state_hgrn, c_prompt, c_sample, ada_w, ada_b, norm1_g, w_in, w_att_branch,
              w_hg_branch, w_out, hg_lower_bound, hg_norm_g, norm2_g, peer_wq, peer_subkeys,
              peer_u, peer_v, final_norm_g):
    slopes = alibi_slopes()
    lbs = jnp.cumsum(jax.nn.softmax(hg_lower_bound.astype(F32), axis=0), axis=0)
    yp, ys = x_prompt, x_sample
    new_p = [[] for _ in range(7)]
    new_s = [[] for _ in range(7)]
    for l in range(DEPTH):
        wl = (ada_w[l], ada_b[l], norm1_g[l], w_in[l], w_att_branch[l], w_hg_branch[l], w_out[l],
              lbs[l], hg_norm_g[l], norm2_g[l], peer_wq[l], peer_subkeys[l], peer_u[l], peer_v[l], slopes)
        s0_p = jnp.zeros((yp.shape[0], HG_HEADS, HG_DK, HG_DV), F32)
        yp, bufs_p, st_p = layer(yp, c_prompt, *wl, None, s0_p)
        caches_l = (cache_k0[l], cache_v0[l], cache_k1[l], cache_v1[l], cache_k2[l], cache_v2[l])
        ys, bufs_s, st_s = layer(ys, c_sample, *wl, caches_l, state_hgrn[l])
        for i in range(6):
            new_p[i].append(bufs_p[i])
            new_s[i].append(bufs_s[i])
        new_p[6].append(st_p)
        new_s[6].append(st_s)
    y_prompt = rms_norm(yp, final_norm_g)
    y_sample = rms_norm(ys, final_norm_g)
    k0_p = jnp.stack(new_p[0]); v0_p = jnp.stack(new_p[1])
    k1_p = jnp.stack(new_p[2]); v1_p = jnp.stack(new_p[3])
    k2_p = jnp.stack(new_p[4]); v2_p = jnp.stack(new_p[5])
    hgrn_p = jnp.stack(new_p[6])
    k0_s = jnp.stack(new_s[0]); v0_s = jnp.stack(new_s[1])
    k1_s = jnp.stack(new_s[2]); v1_s = jnp.stack(new_s[3])
    k2_s = jnp.stack(new_s[4]); v2_s = jnp.stack(new_s[5])
    hgrn_s = jnp.stack(new_s[6])
    return (y_prompt, y_sample, k0_p, v0_p, k1_p, v1_p, k2_p, v2_p, hgrn_p,
            k0_s, v0_s, k1_s, v1_s, k2_s, v2_s, hgrn_s)


_drawn_inputs = setup_inputs


def setup_inputs(seed=0):
    import zlib

    import numpy as np

    out = dict(_drawn_inputs(seed))
    spreads = {}
    factors = {'norm1_g': 2.856, 'hg_norm_g': 8.0, 'norm2_g': 17.681, 'final_norm_g': 7.749}
    for name, (base, spread) in spreads.items():
        noise = np.random.default_rng([zlib.crc32(name.encode()), seed]).standard_normal(out[name].shape)
        drawn = base * np.exp(spread * noise) if base else spread * noise
        out[name] = __import__('jax').numpy.asarray(drawn.astype(out[name].dtype))
    for name, factor in factors.items():
        out[name] = (out[name] * factor).astype(out[name].dtype)
    return out
```

```python
from contextlib import ExitStack

import numpy as np

import concourse.bass as bass
from concourse import mybir

F32 = mybir.dt.float32
U32 = mybir.dt.uint32
ALU = mybir.AluOpType
ACT = mybir.ActivationFunctionType
AX = mybir.AxisListType.X

P = 128
D = 1024
KD = D // P
SEQ = 1024
NB, NT = 8, 8
NS = NB * NT
TOK = SEQ + NS
PT = SEQ // P
EPS = 1e-6
GROUPS = ((128, 1), (512, 4), (1024, 16))
HPG, DH = 4, 64
GW = HPG * DH
AW = len(GROUPS) * GW
HH, HK = 4, 128
HW = HH * HK
CH = 32
NCH = P // CH
HEADS, KEYS, TOPK, DHALF = 8, 128, 16, 128
PICKS = HEADS * TOPK
NEG = -1e30
REC = DH + 2
C_Q, C_K, C_V = 0, AW, 2 * AW
C_ZF, C_ZI = 3 * AW, 3 * AW + HW
C_ZQ = C_ZI + HW
C_ZG = C_ZQ + HW
C_ZA = C_ZG + HW
C_ZH = C_ZA + D
NATC = C_ZQ
TRC = 2 * HW + 2 * D
SLOPES = [float(x) for x in np.exp2(np.float32(-8.0) * np.arange(1, 13, dtype=np.float32) / np.float32(12))]
W_S = (P + NS, 512 + NS, 512 + NS)


def constants():
    i, j = np.arange(P)[:, None], np.arange(P)[None, :]
    out, at = [], {}

    def put(name, a):
        a = np.asarray(a, np.float32)
        full = np.zeros((P, a.shape[1]), np.float32)
        full[: a.shape[0]] = a
        at[name] = (sum(x.shape[1] for x in out), a.shape[1])
        out.append(full)

    put("ident", np.eye(P))
    put("ones", np.ones((P, P)))
    def band(dil):
        delta = i + P - np.arange(2 * P)[None, :]
        return np.where((delta >= 0) & (delta <= P), -delta * dil, NEG)
    first = band(1)
    first[:, :P] = NEG
    put("pen0", np.concatenate([first, band(1)], 1))
    put("pen1", band(4))
    put("pen2", np.where((i // 64 == j // 64) & (i % 64 >= j % 64), -(i % 64 - j % 64) * 16, NEG))
    for half in range(2):
        bb, t = i // 32, i % 8
        new = np.arange(NS)[None, :]
        for g, (w, dil) in enumerate(GROUPS):
            n = np.arange(min(w, 512))[None, :]
            kb, p = n // P, n % P
            idx = (n, p * 4 + kb, p % 64 * 16 + p // 64 * 4 + kb)[g]
            d_old = w + t - idx
            d_new = t - new % 8
            same = new // 8 == 4 * half + bb
            p_old = np.where((d_old % dil == 0) & (d_old <= P * dil), -d_old, NEG)
            p_new = np.where(same & (d_new >= 0) & (d_new % dil == 0), -d_new, NEG)
            put(f"pens{half}{g}", np.concatenate([p_old, p_new], 1))
    sl = np.array([[8.0 * SLOPES[4 * g + r % 32 // 8] for g in range(3)] for r in range(P)])
    put("slope_s", sl)
    put("headmask", (i % 32 // 8 == np.arange(4)[None, :]))
    def sums(n, ch):
        s, t = np.arange(n)[:, None], np.arange(n)[None, :]
        mid = ch // 2 - 1
        c = (s // ch == t // ch) * ((s % ch <= t % ch) * 1.0 - (s % ch <= mid))
        m = (s // ch == np.arange(n // ch)[None, :]) & (s % ch <= mid)
        return np.concatenate([c, m], 1), (s // ch == t // ch) & (s <= t)
    a, m = sums(P, CH)
    put("tri_p", a)
    put("causal_p", m)
    a, m = sums(NS, NT)
    put("tri_s", a)
    put("causal_s", m)
    put("seqmask", (np.arange(NS)[:, None] // 8 == np.arange(8)[None, :]))
    put("sel_p", np.concatenate([np.ones((1, P)), np.zeros((8, P))]))
    put("sel_s", np.arange(9)[:, None] == 1 + np.arange(NS)[None, :] // 8)
    put("iota16", np.broadcast_to(np.arange(16), (P, 16)))
    return np.concatenate(out, 1), at


CONST, AT = constants()

SCRATCH = {
    "modrep": ([P + NS, 6 * D], F32), "proj_n": ([TOK, NATC], F32), "proj_t": ([TRC, TOK], F32),
    "att_rec": ([3, TOK, HPG * REC], F32), "att_t": ([GW, TOK], F32), "oh_t": ([HW, TOK], F32),
    "mix_t": ([D, TOK], F32), "x1": ([TOK, D], F32), "h2": ([TOK, D], F32),
    "qry_t": ([2 * HEADS * DHALF, TOK], F32), "eid": ([TOK, PICKS], U32), "gate": ([TOK, PICKS], F32),
}


class Ordered:

    def __init__(self, eng, sem):
        self.eng, self.sem, self.base, self.n = eng, sem, 0, 0

    def turn(self, i, steps, start):
        self.base, self.n = i * steps + start, 0

    def __call__(self, ins):
        ins.then_inc(self.sem, 1)
        self.n += 1
        self.eng.wait_ge(self.sem, self.base + self.n)


class Program:
    def __init__(self, nc, t, ctx, scratch_kind):
        self.nc, self.t, self.ctx = nc, t, ctx
        self.sems = []
        self.const = ctx.enter_context(nc.sbuf_tensor("const", [P, CONST.shape[1]], F32))
        for name, (shape, dtype) in SCRATCH.items():
            kind = scratch_kind if isinstance(scratch_kind, str) else scratch_kind(name)
            t[name] = nc.dram_tensor(name, shape, dtype, kind=kind).ap()

    def c(self, name, rows=P):
        a, n = AT[name]
        return self.const[0:rows, a:a + n]

    def sem(self, name):
        handle = self.nc.alloc_semaphore(name=name)
        self.sems.append(handle)
        return handle

    def clear_semaphores(self):
        nc = self.nc
        nc.clear_and_free_semaphores(self.sems)
        nc.all_engine_barrier()
        self.sems = []


def load_constants(pr):
    nc = pr.nc
    loaded = pr.sem("const_loaded")
    with nc.Block("load_constants") as block:
        @block.sync
        def _(sp):
            sp.dma_start(pr.const[:, :], pr.t["const"]).then_inc(loaded, 16)
            sp.wait_ge(loaded, 16)


def conditioning(pr):
    nc, t = pr.nc, pr.t
    CW = 512
    turns = 6 * D // CW // 2
    s_in, s_sig, s_act, s_tr, s_ct = (pr.sem(f"ad_{n}") for n in ("in", "sig", "silu", "tr", "ct"))
    w_in = [pr.sem(f"ad_win{s}") for s in range(2)]
    s_mod, s_modsb, s_rep, s_repsb = (pr.sem(f"ad_{n}") for n in ("mod", "modsb", "rep", "repsb"))
    rep_free, s_stored = pr.sem("ad_repfree"), pr.sem("ad_stored")
    w_v = t["ada_w"][0].rearrange("(k p) n -> p k n", p=P)
    with ExitStack() as cx:
        sb = lambda name, shape: cx.enter_context(nc.sbuf_tensor(name, shape, F32))
        ps = lambda name, shape: cx.enter_context(nc.psum_tensor(name, shape, F32))
        c9, sg = sb("c9", [9, D]), sb("sg", [9, D])
        ct = sb("ct", [P, KD, 9])
        w = [sb(f"adw{s}", [P, KD, CW]) for s in range(2)]
        bias = [sb(f"adb{s}", [1, CW]) for s in range(2)]
        modsb = [sb(f"modsb{s}", [9, CW]) for s in range(2)]
        rep = [sb(f"rep{s}", [P, CW]) for s in range(2)]
        reps = [sb(f"reps{s}", [NS, CW]) for s in range(2)]
        p_tr = ps("p_tr", [P, KD, 16])
        p_mod = [ps(f"p_mod{s}", [9, CW]) for s in range(2)]
        p_rep = [ps(f"p_rep{s}", [P, CW]) for s in range(2)]
        p_reps = [ps(f"p_reps{s}", [NS, CW]) for s in range(2)]
        block = cx.enter_context(nc.Block("conditioning"))

        @block.sync
        def _(sp):
            sp.dma_start(c9[0:1, :], t["c_prompt"]).then_inc(s_in, 16)
            sp.dma_start(c9[1:9, :], t["c_sample"]).then_inc(s_in, 16)

            def load(s, col):
                sp.dma_start(w[s][:, :, :], w_v[:, :, bass.ds(col, CW)]).then_inc(w_in[s], 16)
                sp.dma_start(bias[s][:, :], t["ada_b"][:, bass.ds(col, CW)]).then_inc(w_in[s], 16)

            for s in range(2):
                load(s, s * CW)
            with sp.Fori(1, turns) as i:
                for s in range(2):
                    sp.wait_ge(s_mod, i * 2 + s - 1)
                    load(s, (i * 2 + s) * CW)

        @block.tensor
        def _(pe):
            pe.wait_ge(s_act, 1)
            for k in range(KD):
                tr = nc.tensor.transpose(p_tr[:, k, 0:9], c9[:, k * P:(k + 1) * P], pr.c("ident")[0:9, 0:9])
            tr.then_inc(s_tr, 1)
            pe.wait_ge(s_ct, 1)
            with pe.Fori(0, turns) as i:
                for s in range(2):
                    pe.wait_ge(w_in[s], i * 32 + 32)
                    for k in range(KD):
                        nc.tensor.matmul(p_mod[s][:, :], ct[:, k, :], w[s][:, k, :], start=(k == 0), stop=False)
                    nc.tensor.matmul(p_mod[s][:, :], pr.c("ones")[0:1, 0:9], bias[s][:, :],
                                     start=False, stop=True).then_inc(s_mod, 1)
                for s in range(2):
                    pe.wait_ge(s_modsb, i * 2 + s + 1)
                    nc.tensor.matmul(p_rep[s][:, :], pr.c("sel_p", 9), modsb[s][:, :], start=True, stop=True)
                    nc.tensor.matmul(p_reps[s][:, :], pr.c("sel_s", 9), modsb[s][:, :],
                                     start=True, stop=True).then_inc(s_rep, 1)

        @block.scalar
        def _(act):
            act.wait_ge(s_in, 32)
            nc.scalar.activation(sg[:, :], c9[:, :], ACT.Sigmoid).then_inc(s_sig, 1)
            act.sem_inc(rep_free, 2)
            with act.Fori(0, turns) as i:
                for s in range(2):
                    act.wait_ge(s_mod, i * 2 + s + 1)
                    nc.scalar.copy(modsb[s][:, :], p_mod[s][:, :]).then_inc(s_modsb, 1)
                for s in range(2):
                    act.wait_ge(s_rep, i * 2 + s + 1)
                    act.wait_ge(rep_free, i * 2 + s + 1)
                    nc.scalar.copy(rep[s][:, :], p_rep[s][:, :]).then_inc(s_repsb, 1)
                    nc.scalar.copy(reps[s][:, :], p_reps[s][:, :]).then_inc(s_repsb, 1)

        @block.vector
        def _(dve):
            dve.wait_ge(s_sig, 1)
            nc.vector.tensor_tensor(c9[:, :], c9[:, :], sg[:, :], ALU.mult).then_inc(s_act, 1)
            dve.wait_ge(s_tr, 1)
            nc.vector.tensor_copy(ct[:, :, :], p_tr[:, :, 0:9]).then_inc(s_ct, 1)

        @block.gpsimd
        def _(pool):
            with pool.Fori(0, turns) as i:
                for s in range(2):
                    col = (i * 2 + s) * CW
                    pool.wait_ge(s_repsb, (i * 2 + s) * 2 + 2)
                    pool.dma_start(t["modrep"][0:P, bass.ds(col, CW)], rep[s][:, :]).then_inc(s_stored, 16)
                    pool.dma_start(t["modrep"][P:P + NS, bass.ds(col, CW)], reps[s][:, :]).then_inc(s_stored, 16)
                    pool.wait_ge(s_stored, (i * 2 + s) * 32 + 32)
                    pool.sem_inc(rep_free, 1)


def norm_modulate(pr, tag, prompt_src, sample_src, gain, scale_ix, shift_ix, ht, keep=None):
    nc, t = pr.nc, pr.t
    x_in = [pr.sem(f"{tag}_xin{s}") for s in range(2)]
    (mod_in, gmod, sq, ms, ln, rstd, scaled, h_ready, turned, ht_done, kept, h_free) = (
        pr.sem(f"{tag}_{n}") for n in ("modin", "gmod", "sq", "ms", "ln", "rstd", "scaled", "hready",
                                       "turned", "htdone", "kept", "hfree"))
    nstep = pr.sem(f"{tag}_newton")
    with ExitStack() as cx:
        sb = lambda name, shape: cx.enter_context(nc.sbuf_tensor(f"{tag}_{name}", shape, F32))
        x = [sb(f"x{s}", [P, D]) for s in range(2)]
        h = [sb(f"h{s}", [P, D]) for s in range(2)]
        junk = sb("junk", [P, D])
        g_b = sb("g", [P, D])
        scl, shf = [sb(f"scl{r}", [P, D]) for r in range(2)], [sb(f"shf{r}", [P, D]) for r in range(2)]
        st = [sb(f"st{s}", [P, 6]) for s in range(2)]
        p_t = [cx.enter_context(nc.psum_tensor(f"{tag}_pt{s}", [P, KD, P], F32)) for s in range(2)]
        block = cx.enter_context(nc.Block(tag))

        @block.sync
        def _(sp):
            sp.dma_start(g_b[:, :], gain.partition_broadcast(P)).then_inc(mod_in, 16)
            for r, (a, n) in enumerate(((0, P), (P, NS))):
                for buf, ix in ((scl, scale_ix), (shf, shift_ix)):
                    sp.dma_start(buf[r][0:n, :], t["modrep"][a:a + n, ix * D:(ix + 1) * D]).then_inc(mod_in, 16)

            def load(n, s):
                sp.dma_start(x[s][:, :], prompt_src[bass.ds(n * P, P), :]).then_inc(x_in[s], 16)

            for s in range(2):
                load(s, s)
            with sp.Fori(1, PT // 2) as i:
                for s in range(2):
                    sp.wait_ge(scaled, i * 2 + s - 1)
                    load(i * 2 + s, s)
            sp.wait_ge(scaled, PT - 1)
            sp.dma_start(x[0][0:NS, :], sample_src).then_inc(x_in[0], 16)

        @block.scalar
        def _(act):
            def squares(n, s, turn, rows):
                act.wait_ge(x_in[s], turn * 16 + 16)
                nc.scalar.activation(junk[0:rows, :], x[s][0:rows, :], ACT.Square,
                                     accum_out=st[s][0:rows, 0:1]).then_inc(sq, 1)
                act.wait_ge(sq, n + 1)

            def root(n, s, rows):
                act.wait_ge(ms, n + 1)
                nc.scalar.activation(st[s][0:rows, 2:3], st[s][0:rows, 1:2], ACT.Ln).then_inc(ln, 1)
                act.wait_ge(ln, n + 1)
                nc.scalar.activation(st[s][0:rows, 3:4], st[s][0:rows, 2:3], ACT.Exp, scale=-0.5).then_inc(rstd, 1)

            def evacuate(n, s, rows):
                act.wait_ge(turned, n + 3)
                nc.scalar.copy(ht[:, :, bass.ds(n * P, rows)], p_t[s][:, :, 0:rows]).then_inc(ht_done, 1)

            act.sem_inc(ht_done, 2)
            with act.Fori(0, PT // 2) as i:
                for s in range(2):
                    squares(i * 2 + s, s, i, P)
                for s in range(2):
                    root(i * 2 + s, s, P)
                for s in range(2):
                    evacuate(i * 2 + s, s, P)
            squares(PT, 0, PT // 2, NS)
            root(PT, 0, NS)
            evacuate(PT, 0, NS)

        @block.vector
        def _(dve):
            dve.wait_ge(mod_in, 16 * 5)
            for r, n in ((0, P), (1, NS)):
                nc.vector.scalar_tensor_tensor(scl[r][0:n, :], scl[r][0:n, :], 1.0, g_b[0:n, :],
                                               ALU.add, ALU.mult).then_inc(gmod, 1)
            dve.wait_ge(gmod, 2)

            def mean(n, s, rows):
                dve.wait_ge(sq, n + 1)
                nc.vector.tensor_scalar(st[s][0:rows, 1:2], st[s][0:rows, 0:1], 1.0 / D, EPS,
                                        ALU.mult, ALU.add).then_inc(ms, 1)

            def modulate(n, s, rows, r):
                dve.wait_ge(rstd, n + 1)
                newton = Ordered(dve, nstep)
                newton.turn(n, 3, 0)
                y, f = st[s][0:rows, 3:4], st[s][0:rows, 4:5]
                newton(nc.vector.scalar_tensor_tensor(f, y, st[s][0:rows, 1:2], y, ALU.mult, ALU.mult))
                newton(nc.vector.tensor_scalar(f, f, -0.5, 1.5, ALU.mult, ALU.add))
                newton(nc.vector.tensor_tensor(st[s][0:rows, 5:6], y, f, ALU.mult))
                dve.wait_ge(turned, n + 1)
                if keep is not None:
                    dve.wait_ge(h_free, n + 1)
                nc.vector.scalar_tensor_tensor(h[s][0:rows, :], x[s][0:rows, :], st[s][0:rows, 5:6], scl[r][0:rows, :],
                                               ALU.mult, ALU.mult).then_inc(scaled, 1)
                dve.wait_ge(scaled, n + 1)
                nc.vector.tensor_tensor(h[s][0:rows, :], h[s][0:rows, :], shf[r][0:rows, :], ALU.add).then_inc(h_ready, 1)

            with dve.Fori(0, PT // 2) as i:
                for s in range(2):
                    mean(i * 2 + s, s, P)
                for s in range(2):
                    modulate(i * 2 + s, s, P, 0)
            mean(PT, 0, NS)
            modulate(PT, 0, NS, 1)

        @block.tensor
        def _(pe):
            pe.sem_inc(turned, 2)

            def turn(n, s, rows):
                pe.wait_ge(h_ready, n + 1)
                pe.wait_ge(ht_done, n + 1)
                for k in range(KD):
                    tr = nc.tensor.transpose(p_t[s][:, k, 0:rows], h[s][0:rows, k * P:(k + 1) * P],
                                             pr.c("ident")[0:rows, 0:rows])
                tr.then_inc(turned, 1)

            with pe.Fori(0, PT // 2) as i:
                for s in range(2):
                    turn(i * 2 + s, s, P)
            turn(PT, 0, NS)

        if keep is not None:
            @block.gpsimd
            def _(pool):
                pool.sem_inc(h_free, 2)

                def store(n, s, rows):
                    pool.wait_ge(h_ready, n + 1)
                    pool.dma_start(keep[bass.ds(n * P, rows), :], h[s][0:rows, :]).then_inc(kept, 16)
                    pool.wait_ge(kept, n * 16 + 16)
                    pool.sem_inc(h_free, 1)

                with pool.Fori(0, PT // 2) as i:
                    for s in range(2):
                        store(i * 2 + s, s, P)
                store(PT, 0, NS)


def project_features(pr, tag, ht, w_v, col0, cols, dst, row0, cw):
    nc = pr.nc
    ct, turns = cw // P, cols // cw // 2
    assert turns * 2 * cw == cols
    w_in = [pr.sem(f"{tag}_win{s}") for s in range(2)]
    product, evacuated, stored, st_free = (pr.sem(f"{tag}_{n}") for n in ("product", "evac", "stored", "stfree"))
    with ExitStack() as cx:
        w = [cx.enter_context(nc.sbuf_tensor(f"{tag}_w{s}", [P, KD, cw], F32)) for s in range(2)]
        st = [cx.enter_context(nc.sbuf_tensor(f"{tag}_st{s}", [P, TOK], F32)) for s in range(2)]
        ps = [cx.enter_context(nc.psum_tensor(f"{tag}_ps{s}", [P, 3 * 512], F32)) for s in range(2)]
        block = cx.enter_context(nc.Block(tag))

        @block.sync
        def _(sp):
            def load(c, s):
                sp.dma_start(w[s][:, :, :], w_v[:, :, bass.ds(c * cw + col0, cw)]).then_inc(w_in[s], 16)

            for s in range(2):
                load(s, s)
            if turns > 1:
                with sp.Fori(1, turns) as i:
                    for s in range(2):
                        sp.wait_ge(product, (i * 2 + s - 1) * ct)
                        load(i * 2 + s, s)

        @block.tensor
        def _(pe):
            with pe.Fori(0, turns) as i:
                for s in range(2):
                    pe.wait_ge(w_in[s], i * 16 + 16)
                    for j in range(ct):
                        n, b = (i * 2 + s) * ct + j, (s * ct + j) % 2
                        pe.wait_ge(evacuated, n + 1)
                        for k in range(KD):
                            for a in range(0, TOK, 512):
                                e = min(a + 512, TOK)
                                mm = nc.tensor.matmul(ps[b][:, a:e], w[s][:, k, j * P:(j + 1) * P], ht[:, k, a:e],
                                                      start=(k == 0), stop=(k == KD - 1))
                        mm.then_inc(product, 1)

        @block.scalar
        def _(act):
            act.sem_inc(evacuated, 2)
            with act.Fori(0, turns) as i:
                for m in range(2 * ct):
                    n = i * 2 * ct + m
                    act.wait_ge(product, n + 1)
                    act.wait_ge(st_free, n + 1)
                    nc.scalar.copy(st[m % 2][:, :], ps[m % 2][:, 0:TOK]).then_inc(evacuated, 1)

        @block.gpsimd
        def _(pool):
            pool.sem_inc(st_free, 2)
            with pool.Fori(0, turns) as i:
                for m in range(2 * ct):
                    n = i * 2 * ct + m
                    pool.wait_ge(evacuated, n + 3)
                    pool.dma_start(dst[bass.ds(n * P + row0, P), :], st[m % 2][:, :]).then_inc(stored, 16)
                    pool.wait_ge(stored, n * 16 + 16)
                    pool.sem_inc(st_free, 1)


def project_tokens(pr, ht, w_v):
    nc, t = pr.nc, pr.t
    cw = 416
    turns = NATC // cw // 2
    assert turns * 2 * cw == NATC
    tiles = PT + 1
    banks = 6
    w_in = [pr.sem(f"pn_win{s}") for s in range(2)]
    product, evacuated, stored, st_free = (pr.sem(f"pn_{n}") for n in ("product", "evac", "stored", "stfree"))
    with ExitStack() as cx:
        w = [cx.enter_context(nc.sbuf_tensor(f"pn_w{s}", [P, KD, cw], F32)) for s in range(2)]
        st = [cx.enter_context(nc.sbuf_tensor(f"pn_st{s}", [P, tiles, cw], F32)) for s in range(2)]
        ps = cx.enter_context(nc.psum_tensor("pn_ps", [P, banks, 512], F32))
        block = cx.enter_context(nc.Block("project_tokens"))

        @block.sync
        def _(sp):
            def load(c, s):
                sp.dma_start(w[s][:, :, :], w_v[:, :, bass.ds(c * cw, cw)]).then_inc(w_in[s], 16)

            for s in range(2):
                load(s, s)
            with sp.Fori(1, turns) as i:
                for s in range(2):
                    sp.wait_ge(product, (i * 2 + s - 1) * tiles)
                    load(i * 2 + s, s)

        @block.tensor
        def _(pe):
            with pe.Fori(0, turns) as i:
                for s in range(2):
                    pe.wait_ge(w_in[s], i * 16 + 16)
                    for m in range(tiles):
                        rows = P if m < PT else NS
                        b = (s * tiles + m) % banks
                        pe.wait_ge(evacuated, (i * 2 + s) * tiles + m + 1)
                        for k in range(KD):
                            mm = nc.tensor.matmul(ps[0:rows, b, 0:cw], ht[:, k, m * P:m * P + rows], w[s][:, k, :],
                                                  start=(k == 0), stop=(k == KD - 1))
                        mm.then_inc(product, 1)

        @block.vector
        def _(dve):
            dve.sem_inc(evacuated, banks)
            with dve.Fori(0, turns) as i:
                for s in range(2):
                    dve.wait_ge(st_free, i * 2 + s + 1)
                    for m in range(tiles):
                        rows = P if m < PT else NS
                        dve.wait_ge(product, (i * 2 + s) * tiles + m + 1)
                        nc.vector.tensor_copy(st[s][0:rows, m, :], ps[0:rows, (s * tiles + m) % banks, 0:cw])\
                            .then_inc(evacuated, 1)

        @block.gpsimd
        def _(pool):
            pool.sem_inc(st_free, 2)
            with pool.Fori(0, turns) as i:
                for s in range(2):
                    c = i * 2 + s
                    pool.wait_ge(evacuated, (c + 1) * tiles + banks)
                    cols = bass.ds(c * cw, cw)
                    pool.dma_start(t["proj_n"][0:SEQ, cols].rearrange("(m p) c -> p m c", p=P),
                                   st[s][:, 0:PT, :]).then_inc(stored, 16)
                    pool.dma_start(t["proj_n"][SEQ:TOK, cols], st[s][0:NS, PT, :]).then_inc(stored, 16)
                    pool.wait_ge(stored, c * 32 + 32)
                    pool.sem_inc(st_free, 1)


def mixer_input(pr):
    nc, t = pr.nc, pr.t
    w_v = t["w_in"][0].rearrange("(k p) n -> p k n", p=P)
    with nc.sbuf_tensor("ht1", [P, KD, TOK], F32) as ht:
        norm_modulate(pr, "n1", t["x_prompt"][0], t["x_sample"].rearrange("b t d -> (b t) d"), t["norm1_g"][0],
                      1, 0, ht)
        project_tokens(pr, ht, w_v)
        project_features(pr, "pt", ht, w_v, C_ZQ, TRC, t["proj_t"], 0, 3 * P)


def retrieval_queries(pr):
    nc, t = pr.nc, pr.t
    with nc.sbuf_tensor("ht2", [P, KD, TOK], F32) as ht:
        norm_modulate(pr, "n2", t["x1"][0:SEQ, :], t["x1"][SEQ:TOK, :], t["norm2_g"][0], 4, 3, ht, keep=t["h2"])
        project_features(pr, "pq", ht, t["peer_wq"][0].rearrange("(k p) n -> p k n", p=P), 0,
                         2 * HEADS * DHALF, t["qry_t"], 0, 2 * P)


def attention_prompt(pr):
    nc, t = pr.nc, pr.t
    BLK, RING = 8, 4
    (tr, qkt, scored, t_done, mstep, m_ready, exp_done, p_turned, pt_ready, pv_done, ml_done, o_done,
     stored, rec_free, zeroed) = (pr.sem(f"ap_{n}") for n in (
         "tr", "qkt", "scored", "tdone", "mstep", "mready", "exp", "pturned", "ptready", "pv", "ml", "o",
         "stored", "recfree", "zeroed"))
    qkv_in = [pr.sem(f"ap_in{s}") for s in range(RING)]
    src = t["proj_n"][0:SEQ, 0:3 * AW].rearrange("s (j g c) -> s j g c", j=3, g=3)

    def rows_of(view, g, i, b):
        if g == 0:
            return [(0, P, view[bass.ds(i * (RING * P) + b * P, P)])]
        if g == 1:
            v = view.rearrange("(n p r) a b -> n r p a b", p=P, r=4)
            return [(0, P, v[b % 2, i * 2 + b // 2])]
        v = view.rearrange("(u r) a b -> r u a b", r=16)
        return [(64 * e, 64 * e + 64, v[i * 8 + 2 * b + e]) for e in range(2)]

    def bank_of(h):
        return h % 2 * 2 + h // 2

    def has_prev(g, b):
        return g == 0 or (g == 1 and b % 2 == 1)

    with ExitStack() as cx:
        sb = lambda name, shape: cx.enter_context(nc.sbuf_tensor(f"ap_{name}", shape, F32))
        ps = lambda name, shape: cx.enter_context(nc.psum_tensor(f"ap_{name}", shape, F32))
        qkv = [sb(f"qkv{s}", [P, 3, GW]) for s in range(RING)]
        qk_t = [sb(f"qkt{s}", [P, 4, P]) for s in range(RING)]
        sc = [sb(f"sc{s}", [P, HPG, 2 * P]) for s in range(2)]
        pr_ = [sb(f"p{s}", [P, HPG, 2 * P]) for s in range(2)]
        p_t = [sb(f"pt{s}", [P, 2 * HPG, P]) for s in range(2)]
        m8 = [sb(f"m8{s}", [P, HPG]) for s in range(2)]
        nb = [sb(f"nb{s}", [P, HPG]) for s in range(2)]
        den = [sb(f"den{s}", [P, HPG]) for s in range(2)]
        rec = [sb(f"rec{s}", [P, HPG, REC]) for s in range(2)]
        ps_tr = ps("ps_tr", [P, 4, P])
        ps_s = ps("ps_s", [P, HPG, 2 * P])
        ps_pt = ps("ps_pt", [P, 2 * HPG, P])
        ps_o = [ps(f"ps_o{s}", [P, HPG, DH]) for s in range(2)]
        block = cx.enter_context(nc.Block("attention_prompt"))

        def turns(eng, body):
            for g in range(3):
                with eng.Fori(0, BLK // RING) as i:
                    body(g, i, i * RING + BLK * g)

        @block.sync
        def _(sp):
            def body(g, i, n0):
                for b in range(RING):
                    sp.wait_ge(pv_done, n0 + b + 1)
                    for a, e, rows in rows_of(src[:, :, g, :], g, i, b):
                        sp.dma_start(qkv[b][a:e, :, :], rows).then_inc(qkv_in[b], 16)

            sp.wait_ge(zeroed, 2)
            turns(sp, body)

        @block.tensor
        def _(pe):
            def front(g, i, n0, b):
                n = n0 + b
                each = 16 if g < 2 else 32
                pe.wait_ge(qkv_in[b], i * each + each + 32 * g)
                pe.wait_ge(qkt, n + 1)
                for j in range(4):
                    mm = nc.tensor.transpose(ps_tr[:, j, :], qkv[b][:, j // 2, (j % 2) * P:(j % 2 + 1) * P],
                                             pr.c("ident"))
                mm.then_inc(tr, 1)
                pe.wait_ge(qkt, n + 2)
                pe.wait_ge(t_done, n + 1)
                for h in range(HPG):
                    a, hp = 64 * (h % 2), h // 2
                    for kb in range(0 if has_prev(g, b) else 1, 2):
                        keys = qk_t[b if kb else (b - 1) % RING]
                        mm = nc.tensor.matmul(ps_s[:, bank_of(h), kb * P:(kb + 1) * P], qk_t[b][a:a + 64, hp, :],
                                              keys[a:a + 64, 2 + hp, :], start=True, stop=True)
                mm.then_inc(scored, 1)

            def back(g, i, n0, b):
                n, s = n0 + b, b % 2
                kbs = range(0 if has_prev(g, b) else 1, 2)
                pe.wait_ge(exp_done, n + 3)
                pe.wait_ge(pt_ready, n + 1)
                for h in range(HPG):
                    for kb in kbs:
                        mm = nc.tensor.transpose(ps_pt[:, 2 * h + kb, :], pr_[s][:, h, kb * P:(kb + 1) * P],
                                                 pr.c("ident"))
                mm.then_inc(p_turned, 1)
                pe.wait_ge(pt_ready, n + 2)
                pe.wait_ge(o_done, n + 1)
                for h in range(HPG):
                    for kb in kbs:
                        values = qkv[b if kb else (b - 1) % RING][:, 2, h * DH:(h + 1) * DH]
                        mm = nc.tensor.matmul(ps_o[s][:, h, :], p_t[s][:, 2 * h + kb, :], values,
                                              start=(kb == kbs[0]), stop=(kb == 1))
                mm.then_inc(pv_done, 1)

            def body(g, i, n0):
                front(g, i, n0, 0)
                for b in range(1, RING):
                    front(g, i, n0, b)
                    back(g, i, n0, b - 1)
                back(g, i, n0, RING - 1)

            pe.sem_inc(scored, 3)
            pe.sem_inc(p_turned, 2)
            pe.sem_inc(pv_done, 3)
            turns(pe, body)

        @block.scalar
        def _(act):
            def turned(g, i, n0, b):
                n = n0 + b
                act.wait_ge(tr, n + 1)
                act.wait_ge(scored, n + 1)
                nc.scalar.copy(qk_t[b][:, :, :], ps_tr[:, :, :]).then_inc(qkt, 1)

            def exps(g, i, n0, b):
                n, s = n0 + b, b % 2
                k0 = 0 if has_prev(g, b) else P
                act.wait_ge(m_ready, n + 1)
                act.wait_ge(p_turned, n + 1)
                act.wait_ge(ml_done, n + 1)
                for h in range(HPG):
                    ex = nc.scalar.activation(pr_[s][:, h, k0:], sc[s][:, h, k0:], ACT.Exp, bias=nb[s][:, h:h + 1],
                                              scale=0.125, accum_out=den[s][:, h:h + 1])
                ex.then_inc(exp_done, 1)

            def outputs(g, i, n0, b):
                n, s = n0 + b, b % 2
                act.wait_ge(pv_done, n + 4)
                act.wait_ge(rec_free, n + 1)
                nc.scalar.copy(rec[s][:, :, 0:DH], ps_o[s][:, :, :]).then_inc(o_done, 1)

            def body(g, i, n0):
                turned(g, i, n0, 0)
                for b in range(1, RING):
                    turned(g, i, n0, b)
                    exps(g, i, n0, b - 1)
                    if b > 1:
                        outputs(g, i, n0, b - 2)
                exps(g, i, n0, RING - 1)
                outputs(g, i, n0, RING - 2)
                outputs(g, i, n0, RING - 1)

            act.sem_inc(qkt, 1)
            act.sem_inc(exp_done, 2)
            act.sem_inc(o_done, 2)
            turns(act, body)

        @block.vector
        def _(dve):
            def maxima(g, i, n0, b):
                n, s = n0 + b, b % 2
                k0 = 0 if has_prev(g, b) else P
                if g == 0 and b == 0:
                    a = AT["pen0"][0]
                    pen = pr.const[:, bass.ds(i * (2 * P) + a, 2 * P)]
                else:
                    pen = pr.c(f"pen{g}")[:, -2 * P:] if g < 2 else pr.c("pen2")
                    pen = pen[:, k0:] if g < 2 else pen
                dve.wait_ge(scored, n + 4)
                dve.wait_ge(exp_done, n + 1)
                for h in range(HPG):
                    st = nc.vector.scalar_tensor_tensor(sc[s][:, h, k0:], pen, 8.0 * SLOPES[4 * g + h],
                                                        ps_s[:, bank_of(h), k0:], ALU.mult, ALU.add)
                st.then_inc(t_done, 1)
                dve.wait_ge(t_done, n + 2)
                nc.vector.tensor_reduce(m8[s][:, :], sc[s][:, :, k0:], AX, ALU.max).then_inc(mstep, 1)
                dve.wait_ge(mstep, n + 1)
                nc.vector.tensor_scalar(nb[s][:, :], m8[s][:, :], -0.125, None, ALU.mult).then_inc(m_ready, 1)

            def probs(g, i, n0, b):
                n, s = n0 + b, b % 2
                dve.wait_ge(p_turned, n + 3)
                dve.wait_ge(pv_done, n + 2)
                if has_prev(g, b):
                    cp = nc.vector.tensor_copy(p_t[s][:, :, :], ps_pt[:, :, :])
                else:
                    half = lambda x: x.rearrange("p (h k) q -> p h k q", k=2)[:, :, 1, :]
                    cp = nc.vector.tensor_copy(half(p_t[s][:, :, :]), half(ps_pt[:, :, :]))
                cp.then_inc(pt_ready, 1)
                dve.wait_ge(rec_free, n + 1)
                nc.vector.tensor_copy(rec[s][:, :, DH], m8[s][:, :])
                nc.vector.tensor_copy(rec[s][:, :, DH + 1], den[s][:, :]).then_inc(ml_done, 1)

            def body(g, i, n0):
                maxima(g, i, n0, 0)
                for b in range(1, RING):
                    maxima(g, i, n0, b)
                    probs(g, i, n0, b - 1)
                probs(g, i, n0, RING - 1)

            nc.vector.memset(qkv[RING - 1][:, :, :], 0.0).then_inc(zeroed, 1)
            nc.vector.memset(qk_t[RING - 1][:, :, :], 0.0).then_inc(zeroed, 1)
            dve.sem_inc(t_done, 1)
            dve.sem_inc(pt_ready, 1)
            dve.sem_inc(ml_done, 2)
            turns(dve, body)

        @block.gpsimd
        def _(pool):
            def body(g, i, n0):
                for b in range(RING):
                    n, s = n0 + b, b % 2
                    pool.wait_ge(o_done, n + 3)
                    pool.wait_ge(ml_done, n + 3)
                    for a, e, rows in rows_of(t["att_rec"][g, 0:SEQ].rearrange("s (h c) -> s h c", h=HPG), g, i, b):
                        pool.dma_start(rows, rec[s][a:e, :, :]).then_inc(stored, 16)
                    pool.wait_ge(stored, stores(g, i, b))
                    pool.sem_inc(rec_free, 1)

            def stores(g, i, b):
                each = 16 if g < 2 else 32
                return i * (RING * each) + (b + 1) * each + BLK * 16 * g

            pool.sem_inc(rec_free, 2)
            turns(pool, body)


def attention_merge(pr):
    nc, t = pr.nc, pr.t
    (top, diff, w_done, den, rden, wn, prod, att, turned, evac, stored, tfree) = (pr.sem(f"am_{n}") for n in (
        "top", "diff", "w", "den", "rden", "wn", "prod", "att", "turned", "evac", "stored", "tfree"))
    wl_done = pr.sem("am_wl")
    rec_in = [pr.sem(f"am_in{s}") for s in range(2)]
    with ExitStack() as cx:
        sb = lambda name, shape: [cx.enter_context(nc.sbuf_tensor(f"am_{name}{s}", shape, F32)) for s in range(2)]
        rec = sb("rec", [P, 3, HPG, REC])
        mx, de, re = sb("mx", [P, HPG]), sb("de", [P, HPG]), sb("re", [P, HPG])
        w, wl = sb("w", [P, 3, HPG]), sb("wl", [P, 3, HPG])
        o3, at, at_t = sb("o3", [P, 3, HPG, DH]), sb("at", [P, GW]), sb("att", [P, 2, P])
        ps = [cx.enter_context(nc.psum_tensor(f"am_ps{s}", [P, 2, P], F32)) for s in range(2)]
        block = cx.enter_context(nc.Block("attention_merge"))
        src = t["att_rec"].rearrange("g t c -> t g c")
        dst = t["att_t"].rearrange("(k p) t -> p k t", p=P)

        def tiles(eng, tile):
            with eng.Fori(0, PT // 2) as i:
                for s in range(2):
                    tile(i * 2 + s, s, i, P)
            tile(PT, 0, PT // 2, NS)

        @block.sync
        def _(sp):
            def load(n, s, i, rows):
                sp.wait_ge(prod, n + 1)
                sp.dma_start(rec[s][0:rows, :, :, :].rearrange("p g h c -> p g (h c)"),
                             src[bass.ds(n * P, rows)]).then_inc(rec_in[s], 16)
            tiles(sp, load)

        @block.vector
        def _(dve):
            def tile(n, s, i, rows):
                r = slice(0, rows)
                m = rec[s][r, :, :, DH]
                over_g = lambda x: x.unsqueeze(1).broadcast_to([rows, 3, HPG])
                dve.wait_ge(rec_in[s], i * 16 + 16)
                nc.vector.tensor_reduce(mx[s][r, :], m.rearrange("p g h -> p h g"), AX, ALU.max).then_inc(top, 1)
                dve.wait_ge(top, n + 1)
                nc.vector.tensor_tensor(w[s][r], m, over_g(mx[s][r, :]), ALU.subtract).then_inc(diff, 1)
                dve.wait_ge(w_done, n + 1)
                nc.vector.tensor_tensor(wl[s][r], w[s][r], rec[s][r, :, :, DH + 1], ALU.mult).then_inc(wl_done, 1)
                dve.wait_ge(wl_done, n + 1)
                nc.vector.tensor_reduce(de[s][r, :], wl[s][r].rearrange("p g h -> p h g"), AX, ALU.add).then_inc(den, 1)
                dve.wait_ge(den, n + 1)
                nc.vector.reciprocal(re[s][r, :], de[s][r, :]).then_inc(rden, 1)
                dve.wait_ge(rden, n + 1)
                nc.vector.tensor_tensor(wl[s][r], w[s][r], over_g(re[s][r, :]), ALU.mult).then_inc(wn, 1)
                dve.wait_ge(wn, n + 1)
                nc.vector.tensor_tensor(o3[s][r], rec[s][r, :, :, 0:DH],
                                        wl[s][r].unsqueeze(3).broadcast_to([rows, 3, HPG, DH]), ALU.mult)\
                    .then_inc(prod, 1)
                dve.wait_ge(prod, n + 3)
                dve.wait_ge(turned, n + 1)
                nc.vector.tensor_reduce(at[s][r, :], o3[s][r].rearrange("p g h c -> p (h c) g"), AX, ALU.add)\
                    .then_inc(att, 1)

            dve.sem_inc(prod, 2)
            tiles(dve, tile)

        @block.scalar
        def _(act):
            def tile(n, s, i, rows):
                act.wait_ge(diff, n + 1)
                nc.scalar.activation(w[s][0:rows], w[s][0:rows], ACT.Exp, scale=0.125).then_inc(w_done, 1)
                act.wait_ge(turned, n + 3)
                act.wait_ge(tfree, n + 1)
                nc.scalar.copy(at_t[s][:, :, 0:rows], ps[s][:, :, 0:rows]).then_inc(evac, 1)

            act.sem_inc(evac, 2)
            tiles(act, tile)

        @block.tensor
        def _(pe):
            def tile(n, s, i, rows):
                pe.wait_ge(att, n + 1)
                pe.wait_ge(evac, n + 1)
                for k in range(2):
                    tr = nc.tensor.transpose(ps[s][:, k, 0:rows], at[s][0:rows, k * P:(k + 1) * P],
                                             pr.c("ident")[0:rows, 0:rows])
                tr.then_inc(turned, 1)

            pe.sem_inc(turned, 2)
            tiles(pe, tile)

        @block.gpsimd
        def _(pool):
            def tile(n, s, i, rows):
                pool.wait_ge(evac, n + 3)
                pool.dma_start(dst[:, :, bass.ds(n * P, rows)], at_t[s][:, :, 0:rows]).then_inc(stored, 16)
                pool.wait_ge(stored, n * 16 + 16)
                pool.sem_inc(tfree, 1)

            pool.sem_inc(tfree, 2)
            tiles(pool, tile)


def attention_sample(pr):
    nc, t = pr.nc, pr.t
    loaded, zeroed, new_tr, new_t, stored = (pr.sem(f"as_{n}") for n in ("loaded", "zeroed", "newtr", "newt", "stored"))
    (qbd_done, ktr, kt_done, scored, t_done, mstep, m_ready, exp_done, p_turned, pt_ready, pv_done, picked,
     rec_done, rec_free) = (pr.sem(f"as_{n}") for n in (
         "qbd", "ktr", "kt", "scored", "tdone", "mstep", "mready", "exp", "pturned", "ptready", "pv", "picked",
         "rec", "recfree"))
    kv_in = [pr.sem(f"as_in{g}") for g in range(3)]
    NKB = (1, 4, 4)
    penw = sum(W_S)
    with ExitStack() as cx:
        sb = lambda name, shape: cx.enter_context(nc.sbuf_tensor(f"as_{name}", shape, F32))
        ps = lambda name, shape: cx.enter_context(nc.psum_tensor(f"as_{name}", shape, F32))
        new = sb("new", [P, 3, 3, GW])
        new_tt = sb("newt", [P, 2, 3, 2, NS])
        kc = [sb(f"k{g}", [P, 4, NKB[g] * GW]) for g in range(3)]
        vc = [sb(f"v{g}", [P, 4, NKB[g] * GW]) for g in range(3)]
        qbd = [sb(f"qbd{g}", [P, 2, 4, HPG, NT]) for g in range(3)]
        k_t = [sb(f"kt{s}", [P, 2, 512]) for s in range(2)]
        sc, prob = sb("sc", [P, 576]), sb("prob", [P, 640])
        p_t = sb("pt", [P, 5, P])
        m8, nb, den = sb("m8", [P, 1]), sb("nb", [P, 1]), sb("den", [P, 1])
        pick, rec = sb("pick", [P, HPG, DH]), sb("rec", [P, REC])
        ps_k = ps("ps_k", [P, 2, 512])
        ps_s, ps_n = ps("ps_s", [P, 512]), ps("ps_n", [P, 512])
        ps_pt, ps_o = ps("ps_pt", [P, 5, P]), ps("ps_o", [P, GW])
        block = cx.enter_context(nc.Block("attention_sample"))

        @block.sync
        def _(sp):
            sp.dma_start(new[0:NS], t["proj_n"][SEQ:TOK, 0:3 * AW].rearrange("s (j g c) -> s j g c", j=3, g=3))\
                .then_inc(loaded, 16)
            with sp.Fori(0, 2) as i:
                for g in range(3):
                    sp.wait_ge(pv_done, i * 3 + g + 1)
                    for buf, name in ((kc, "k"), (vc, "v")):
                        src = t[f"cache_{name}{g}"][0].rearrange("b w h d -> b w (h d)")[bass.ds(i * 4, 4)]
                        if g == 0:
                            sp.dma_start(buf[g][:, :, :], src.rearrange("b p c -> p b c")).then_inc(kv_in[g], 16)
                        elif g == 1:
                            sp.dma_start(buf[g][:, :, :], src.rearrange("b (p k) c -> p b (k c)", p=P)).then_inc(kv_in[g], 16)
                        else:
                            v = src.rearrange("b (u r) c -> u b (r c)", r=16)
                            for e in range(2):
                                sp.dma_start(buf[g][64 * e:64 * e + 64, :, :],
                                             v[:, :, e * 4 * GW:(e + 1) * 4 * GW]).then_inc(kv_in[g], 16)

        @block.tensor
        def _(pe):
            pe.wait_ge(loaded, 16)
            for g in range(3):
                for j in range(4):
                    mm = nc.tensor.transpose(ps_k[:, 0, j * NS:(j + 1) * NS],
                                             new[0:NS, j // 2, g, (j % 2) * P:(j % 2 + 1) * P], pr.c("ident")[0:NS, 0:NS])
                mm.then_inc(new_tr, 1)
                pe.wait_ge(new_t, g + 1)
            pe.sem_inc(pv_done, 3)
            pe.sem_inc(scored, 2)
            with pe.Fori(0, 2) as i:
                for g in range(3):
                    n, nk, w = i * 3 + g, NKB[g], NKB[g] * P
                    pe.wait_ge(kv_in[g], i * (64 if g == 2 else 32) + (64 if g == 2 else 32))
                    pe.wait_ge(qbd_done, n + 1)
                    pe.wait_ge(t_done, n + 1)
                    for b in range(4):
                        q = n * 4 + b
                        pe.wait_ge(kt_done, q + 1)
                        for hp in range(2):
                            for kb in range(nk):
                                a = kb * GW + hp * P
                                mm = nc.tensor.transpose(ps_k[:, hp, kb * P:(kb + 1) * P], kc[g][:, b, a:a + P],
                                                         pr.c("ident"))
                        mm.then_inc(ktr, 1)
                        pe.wait_ge(kt_done, q + 2)
                        rows = slice(32 * b, 32 * b + 32)
                        for hp in range(2):
                            lhs = qbd[g][:, hp, b].rearrange("p h t -> p (h t)")
                            nc.tensor.matmul(ps_s[rows, 0:w], lhs, k_t[b % 2][:, hp, 0:w], start=(hp == 0), stop=(hp == 1))
                        for hp in range(2):
                            lhs = qbd[g][:, hp, b].rearrange("p h t -> p (h t)")
                            mm = nc.tensor.matmul(ps_n[rows, 0:NS], lhs, new_tt[:, 1, g, hp, :], start=(hp == 0), stop=(hp == 1))
                        mm.then_inc(scored, 1)
                    pe.wait_ge(exp_done, n + 1)
                    pe.wait_ge(pt_ready, n + 1)
                    for kb in range(nk + 1):
                        mm = nc.tensor.transpose(ps_pt[:, kb, :], prob[:, kb * P:(kb + 1) * P], pr.c("ident"))
                    mm.then_inc(p_turned, 1)
                    pe.wait_ge(pt_ready, n + 2)
                    pe.wait_ge(picked, n + 1)
                    for b in range(4):
                        rows = slice(32 * b, 32 * b + 32)
                        for kb in range(nk + 1):
                            rhs = vc[g][:, b, kb * GW:(kb + 1) * GW] if kb < nk else new[:, 2, g, :]
                            mm = nc.tensor.matmul(ps_o[rows, :], p_t[:, kb, rows], rhs, start=(kb == 0), stop=(kb == nk))
                    mm.then_inc(pv_done, 1)

        @block.scalar
        def _(act):
            act.sem_inc(kt_done, 1)
            with act.Fori(0, 2) as i:
                for g in range(3):
                    n, w = i * 3 + g, NKB[g] * P
                    for b in range(4):
                        q = n * 4 + b
                        act.wait_ge(ktr, q + 1)
                        act.wait_ge(scored, q + 1)
                        nc.scalar.copy(k_t[b % 2][:, :, 0:w], ps_k[:, :, 0:w]).then_inc(kt_done, 1)
                    act.wait_ge(m_ready, n + 1)
                    nc.scalar.activation(prob[:, 0:w + NS], sc[:, 0:w + NS], ACT.Exp, bias=nb[:, :], scale=0.125,
                                         accum_out=den[:, :]).then_inc(exp_done, 1)

        @block.vector
        def _(dve):
            nc.vector.memset(prob[:, :], 0.0).then_inc(zeroed, 1)
            nc.vector.memset(new[NS:P], 0.0).then_inc(zeroed, 1)
            for g in range(3):
                nc.vector.memset(qbd[g][:, :, :, :, :], 0.0).then_inc(zeroed, 1)
            dve.wait_ge(zeroed, 5)
            for g in range(3):
                dve.wait_ge(new_tr, g + 1)
                nc.vector.tensor_copy(new_tt[:, :, g, :, :],
                                      ps_k[:, 0, 0:4 * NS].rearrange("p (j h t) -> p j h t", j=2, h=2)).then_inc(new_t, 1)
            dve.wait_ge(new_t, 3)
            dve.sem_inc(t_done, 1)
            dve.sem_inc(pt_ready, 1)
            dve.sem_inc(picked, 1)
            with dve.Fori(0, 2) as i:
                for g in range(3):
                    n, nk, w = i * 3 + g, NKB[g], NKB[g] * P
                    dve.wait_ge(scored, n * 4 + 2)
                    for h in range(HPG):
                        e, hp = 64 * (h % 2), h // 2
                        cp = nc.vector.tensor_copy(qbd[g][e:e + 64, hp, :, h, :], new_tt[
                            e:e + 64, 0, g, hp, bass.ds(i * 32, 32)].rearrange("p (b t) -> p b t", b=4))
                    cp.then_inc(qbd_done, 1)
                    dve.wait_ge(scored, n * 4 + 6)
                    slope = pr.c("slope_s")[:, g:g + 1]
                    a = AT[f"pens0{g}"][0]
                    pen = lambda at, width: pr.const[:, bass.ds(i * penw + a + at, width)]
                    dve.wait_ge(pv_done, n + 3)
                    nc.vector.scalar_tensor_tensor(sc[:, 0:w], pen(0, w), slope, ps_s[:, 0:w], ALU.mult, ALU.add)\
                        .then_inc(mstep, 1)
                    nc.vector.scalar_tensor_tensor(sc[:, w:w + NS], pen(w, NS), slope, ps_n[:, 0:NS], ALU.mult, ALU.add)\
                        .then_inc(t_done, 1)
                    dve.wait_ge(mstep, n * 2 + 1)
                    dve.wait_ge(t_done, n + 2)
                    nc.vector.tensor_reduce(m8[:, :], sc[:, 0:w + NS], AX, ALU.max).then_inc(mstep, 1)
                    dve.wait_ge(mstep, n * 2 + 2)
                    nc.vector.tensor_scalar(nb[:, :], m8[:, :], -0.125, None, ALU.mult).then_inc(m_ready, 1)
                    dve.wait_ge(p_turned, n + 1)
                    nc.vector.tensor_copy(p_t[:, 0:nk + 1, :], ps_pt[:, 0:nk + 1, :]).then_inc(pt_ready, 1)
                    dve.wait_ge(pv_done, n + 4)
                    nc.vector.tensor_tensor(pick[:, :, :], ps_o[:, :].rearrange("p (h c) -> p h c", h=HPG),
                                            pr.c("headmask").unsqueeze(2).broadcast_to([P, HPG, DH]), ALU.mult)\
                        .then_inc(picked, 1)
                    dve.wait_ge(picked, n + 2)
                    dve.wait_ge(rec_free, n + 1)
                    nc.vector.tensor_reduce(rec[:, 0:DH], pick[:, :, :].rearrange("p h c -> p c h"), AX, ALU.add)\
                        .then_inc(rec_done, 1)
                    nc.vector.tensor_copy(rec[:, DH:DH + 1], m8[:, :]).then_inc(rec_done, 1)
                    nc.vector.tensor_copy(rec[:, DH + 1:REC], den[:, :]).then_inc(rec_done, 1)
                    dve.wait_ge(rec_done, n * 3 + 3)

        @block.gpsimd
        def _(pool):
            pool.sem_inc(rec_free, 1)
            with pool.Fori(0, 2) as i:
                for g in range(3):
                    n = i * 3 + g
                    pool.wait_ge(rec_done, n * 3 + 3)
                    dst = t["att_rec"][g, SEQ:TOK].rearrange("(b t) (h c) -> b h t c", t=NT, c=REC)
                    for b in range(4):
                        for h in range(HPG):
                            r = 32 * b + 8 * h
                            pool.dma_start(dst[i * 4 + b, h], rec[r:r + 8, :]).then_inc(stored, 16)
                    pool.wait_ge(stored, n * 256 + 256)
                    pool.sem_inc(rec_free, 1)


def recurrence(pr):
    nc, t = pr.nc, pr.t
    (base_in, lb_done, e_f, f_done, lf_done, einv_done, log_done, sums, exps, q_done, k_done, k_tr, k_t, u_done,
     a_done, am_done, sprime, inter, s_done, squared, msum, ms, rln, rexp, o_ready, stored, o_free, seeds, s_out,
     tile_done, act_step, dve_step, km_done) = (pr.sem(f"hg_{n}") for n in (
         "base", "lb", "ef", "f", "lf", "einv", "log", "sums", "exps", "q", "k", "ktr", "kt", "u", "a", "am",
         "sprime", "inter", "sdone", "squared", "msum", "ms", "rln", "rexp", "oready", "stored", "ofree",
         "seeds", "sout", "tile", "actstep", "dvestep", "km"))
    fi_in, tmp_done = pr.sem("hg_fi"), pr.sem("hg_tmp")
    with ExitStack() as cx:
        sb = lambda name, shape: cx.enter_context(nc.sbuf_tensor(f"hg_{name}", shape, F32))
        ps = lambda name, shape: cx.enter_context(nc.psum_tensor(f"hg_{name}", shape, F32))
        lb, oml, gain = sb("lb", [P, HW]), sb("oml", [P, HW]), sb("gain", [P, 1])
        fi, qg = sb("fi", [P, 2 * HW]), sb("qg", [P, 2 * HH, P])
        f, x, lf, kh, en = (sb(n, [P, HW]) for n in ("f", "x", "lf", "kh", "en"))
        eg, eq, kt, am, osq, rs, sg = (sb(n, [P, HH, P]) for n in ("eg", "eq", "kt", "am", "osq", "rs", "sg"))
        em = sb("em", [P, HH, 8])
        state = sb("state", [P, HH, HK])
        sp_ = [sb(f"sp{s}", [P, HH, HK]) for s in range(2)]
        s8 = sb("s8", [P, NB, HH, HK])
        km = sb("km", [NS, NB, HW])
        oh = sb("oh", [P, HH, P])
        ps_ct = ps("ps_ct", [P, HH, 256])
        ps_cn = ps("ps_cn", [P, HW])
        ps_u = [ps(f"ps_u{c}", [P, HH, HK]) for c in range(4)]
        ps_o = ps("ps_o", [P, HH, P])
        block = cx.enter_context(nc.Block("recurrence"))
        state_in = t["state_hgrn"][0].rearrange("b h k v -> k b h v")
        state_out = t["hgrn_s"][0].rearrange("b h k v -> k b h v")

        def tiles(eng, tile):
            with eng.Fori(0, PT) as i:
                tile(i, P, CH, "p")
            tile(PT, NS, NT, "s")

        def x_t(r):
            return kt[:, :, r]

        @block.sync
        def _(sp):
            for r in range(2):
                sp.dma_start((lb, oml)[r][:, :], t["hg_lower_bound"][r].partition_broadcast(P)).then_inc(base_in, 16)
            sp.dma_start(gain[:, :], t["hg_norm_g"].rearrange("a p -> p a")).then_inc(base_in, 16)
            sp.dma_start(s8[:, :, :, :], state_in).then_inc(seeds, 16)

            def tile(n, rows, ch, kind):
                sp.wait_ge(tile_done, n + 1)
                sp.dma_start(fi[0:rows, :], t["proj_n"][bass.ds(n * P, rows), C_ZF:NATC]).then_inc(fi_in, 16)
                sp.dma_start(qg[:, :, 0:rows], t["proj_t"][0:2 * HW, bass.ds(n * P, rows)]
                             .rearrange("(k p) t -> p k t", p=P)).then_inc(fi_in, 16)
                sp.wait_ge(o_ready, n + 1)
                sp.dma_start(t["oh_t"][:, bass.ds(n * P, rows)].rearrange("(k p) t -> p k t", p=P),
                             oh[:, :, 0:rows]).then_inc(stored, 16)
                if kind == "p":
                    sp.wait_ge(stored, n * 16 + 16)
                    sp.sem_inc(o_free, 1)

            with sp.Fori(0, PT) as i:
                tile(i, P, CH, "p")
            tile(PT, NS, NT, "s")
            sp.dma_start(t["hgrn_p"][0, 0].rearrange("h k v -> k h v"), state[:, :, :]).then_inc(s_out, 16)
            sp.wait_ge(s_done, 4 * PT + NB)
            sp.dma_start(state_out, s8[:, :, :, :]).then_inc(s_out, 16)
            sp.wait_ge(s_out, 32)
            sp.wait_ge(stored, (PT + 1) * 16)

        @block.scalar
        def _(act):
            act.wait_ge(lb_done, 1)
            nc.scalar.activation(lb[:, :], lb[:, :], ACT.Exp).then_inc(lb_done, 1)
            act.sem_inc(tile_done, 1)

            def tile(n, rows, ch, kind):
                r, nch = slice(0, rows), rows // ch
                act.wait_ge(fi_in, n * 32 + 32)
                act.wait_ge(f_done, n + 1)
                nc.scalar.activation(x[r, :], fi[r, 0:HW], ACT.Exp, scale=-1.0).then_inc(e_f, 1)
                nc.scalar.activation(eg[:, :, r], qg[:, HH:, r], ACT.Exp, scale=-1.0).then_inc(e_f, 1)
                act.wait_ge(f_done, n + 2)
                nc.scalar.activation(lf[r, :], f[r, :], ACT.Ln).then_inc(lf_done, 1)
                act.wait_ge(lf_done, n + 1)
                nc.scalar.activation(x[r, :], lf[r, :], ACT.Exp, scale=-1.0).then_inc(einv_done, 1)
                act.wait_ge(sums, n + 1)
                nc.scalar.activation(eq[:, :, r], ps_ct[:, :, r], ACT.Exp)
                nc.scalar.activation(en[r, :], ps_cn[r, :], ACT.Exp, scale=-1.0)
                nc.scalar.activation(em[:, :, 0:nch], ps_ct[:, :, rows:rows + nch], ACT.Exp).then_inc(exps, 1)
                act.wait_ge(k_tr, n + 1)
                nc.scalar.copy(kt[:, :, r], ps_cn[:, :].rearrange("p (h t) -> p h t", h=HH)[:, :, r]).then_inc(k_t, 1)
                act.wait_ge(inter, n * 4 + nch + 1)
                nc.scalar.activation(osq[:, :, r], ps_o[:, :, r], ACT.Square).then_inc(squared, 1)
                act.wait_ge(ms, n + 1)
                nc.scalar.activation(rs[:, :, r], x_t(r), ACT.Ln).then_inc(rln, 1)
                act.wait_ge(rln, n + 1)
                nc.scalar.activation(rs[:, :, r], rs[:, :, r], ACT.Exp, scale=-0.5).then_inc(rexp, 1)

            tiles(act, tile)

        @block.vector
        def _(dve):
            step = Ordered(dve, dve_step)
            dve.wait_ge(base_in, 48)
            nc.vector.tensor_tensor(lb[:, :], oml[:, :], lb[:, :], ALU.subtract).then_inc(lb_done, 1)
            dve.wait_ge(lb_done, 2)
            step(nc.vector.tensor_scalar(lb[:, :], lb[:, :], 1.0, None, ALU.add))
            step(nc.vector.reciprocal(lb[:, :], lb[:, :]))
            step(nc.vector.tensor_scalar(oml[:, :], lb[:, :], -1.0, 1.0, ALU.mult, ALU.add))
            step(nc.vector.memset(state[:, :, :], 0.0))
            START, STEPS = 4, 14
            dve.sem_inc(f_done, 1)
            over = lambda y, rows: y.unsqueeze(2).broadcast_to([P, HH, HK])

            def tile(n, rows, ch, kind):
                r, nch = slice(0, rows), rows // ch
                step.turn(n, STEPS, START)
                dve.wait_ge(e_f, n * 2 + 2)
                step(nc.vector.tensor_scalar(f[r, :], x[r, :], 1.0, None, ALU.add))
                step(nc.vector.reciprocal(f[r, :], f[r, :]))
                step(nc.vector.tensor_tensor(f[r, :], f[r, :], oml[r, :], ALU.mult))
                nc.vector.tensor_tensor(f[r, :], f[r, :], lb[r, :], ALU.add).then_inc(f_done, 1)
                dve.wait_ge(f_done, n + 2)
                step(nc.vector.tensor_scalar(kh[r, :], f[r, :], -1.0, 1.0, ALU.mult, ALU.add))
                step(nc.vector.tensor_scalar(sg[:, :, r], eg[:, :, r], 1.0, None, ALU.add))
                step(nc.vector.reciprocal(sg[:, :, r], sg[:, :, r]))
                step(nc.vector.tensor_tensor(sg[:, :, r], sg[:, :, r], qg[:, HH:, r], ALU.mult))
                dve.wait_ge(einv_done, n + 1)
                step(nc.vector.tensor_tensor(x[r, :], f[r, :], x[r, :], ALU.mult))
                nc.vector.scalar_tensor_tensor(lf[r, :], x[r, :], -1.0, lf[r, :], ALU.add, ALU.add).then_inc(log_done, 1)
                dve.wait_ge(exps, n + 1)
                nc.vector.tensor_tensor(kh[r, :], kh[r, :], en[r, :], ALU.mult).then_inc(k_done, 1)
                nc.vector.tensor_tensor(qg[:, 0:HH, r], qg[:, 0:HH, r], eq[:, :, r], ALU.mult).then_inc(q_done, 1)
                if kind == "s":
                    dve.wait_ge(k_done, n + 1)
                    for c in range(nch):
                        nc.vector.tensor_scalar(km[:, c, :], kh[r, :], pr.c("seqmask", NS)[:, c:c + 1], None,
                                                ALU.mult).then_inc(km_done, 1)
                dve.wait_ge(a_done, n + 1)
                causal = pr.c(f"causal_{kind}", rows).unsqueeze(1).broadcast_to([rows, HH, rows])
                nc.vector.tensor_tensor(am[r, :, r], ps_ct[r, 0:2, :].rearrange("p a (b t) -> p (a b) t", b=2)[:, :, r],
                                        causal, ALU.mult).then_inc(am_done, 1)
                for c in range(nch):
                    q = n * 4 + c
                    s_in = state[:, :, :] if kind == "p" else s8[:, c, :, :]
                    dve.wait_ge(inter, q + 1)
                    nc.vector.tensor_tensor(sp_[c % 2][:, :, :], s_in, over(em[:, :, c], rows), ALU.mult).then_inc(sprime, 1)
                    dve.wait_ge(sprime, q + 1)
                    dve.wait_ge(u_done, q + 1)
                    nc.vector.tensor_tensor(s_in, sp_[c % 2][:, :, :], ps_u[c % 4][:, :, :], ALU.add).then_inc(tmp_done, 1)
                    dve.wait_ge(tmp_done, q + 1)
                    nc.vector.tensor_tensor(s_in, s_in, over(eq[:, :, c * ch + ch - 1], rows), ALU.mult).then_inc(s_done, 1)
                    dve.wait_ge(s_done, q + 1)
                dve.wait_ge(msum, n + 1)
                nc.vector.tensor_scalar(x_t(r), ps_cn[:, :].rearrange("p (h t) -> p h t", h=HH)[:, :, r],
                                        1.0 / HK, EPS, ALU.mult, ALU.add).then_inc(ms, 1)
                dve.wait_ge(ms, n + 1)
                dve.wait_ge(rexp, n + 1)
                step(nc.vector.tensor_tensor(eg[:, :, r], rs[:, :, r], rs[:, :, r], ALU.mult))
                step(nc.vector.tensor_tensor(eg[:, :, r], eg[:, :, r], x_t(r), ALU.mult))
                step(nc.vector.tensor_scalar(eg[:, :, r], eg[:, :, r], -0.5, 1.5, ALU.mult, ALU.add))
                step(nc.vector.tensor_tensor(rs[:, :, r], rs[:, :, r], eg[:, :, r], ALU.mult))
                step(nc.vector.tensor_tensor(sg[:, :, r], sg[:, :, r], rs[:, :, r], ALU.mult))
                step(nc.vector.tensor_scalar(sg[:, :, r], sg[:, :, r], gain[:, 0:1], None, ALU.mult))
                dve.wait_ge(o_free, n + 1)
                nc.vector.tensor_tensor(oh[:, :, r], sg[:, :, r], ps_o[:, :, r], ALU.mult).then_inc(o_ready, 1)
                dve.wait_ge(o_ready, n + 1)
                dve.sem_inc(tile_done, 1)
                assert step.n == STEPS, step.n

            dve.sem_inc(inter, 1)
            dve.sem_inc(o_free, 1)
            dve.wait_ge(seeds, 16)
            tiles(dve, tile)

        @block.tensor
        def _(pe):
            def tile(n, rows, ch, kind):
                r, nch = slice(0, rows), rows // ch
                tri = pr.c(f"tri_{kind}", rows)
                pe.wait_ge(log_done, n + 1)
                for h in range(HH):
                    nc.tensor.matmul(ps_ct[:, h, 0:rows + nch], lf[r, h * HK:(h + 1) * HK], tri, start=True, stop=True)
                nc.tensor.matmul(ps_cn[r, :], tri[:, r], lf[r, :], start=True, stop=True).then_inc(sums, 1)
                pe.wait_ge(k_done, n + 1)
                for h in range(HH):
                    mm = nc.tensor.transpose(ps_cn[:, h * P:h * P + rows], kh[r, h * HK:(h + 1) * HK],
                                             pr.c("ident")[r, r])
                mm.then_inc(k_tr, 1)

                def increments(c):
                    if kind == "p":
                        a = slice(c * ch, (c + 1) * ch)
                        lhs, rhs = kh[a], fi[a, HW:]
                    else:
                        pe.wait_ge(km_done, c + 1)
                        lhs, rhs = km[:, c], fi[r, HW:]
                    for h in range(HH):
                        hs = slice(h * HK, (h + 1) * HK)
                        mm = nc.tensor.matmul(ps_u[c % 4][:, h, :], lhs[:, hs], rhs[:, hs], start=True, stop=True)
                    mm.then_inc(u_done, 1)

                for c in range(4):
                    increments(c)
                pe.wait_ge(k_t, n + 1)
                pe.wait_ge(q_done, n + 1)
                for h in range(HH):
                    mm = nc.tensor.matmul(ps_ct[r, h // 2, h % 2 * P:h % 2 * P + rows], kt[:, h, r], qg[:, h, r],
                                          start=True, stop=True)
                mm.then_inc(a_done, 1)
                pe.wait_ge(am_done, n + 1)
                for h in range(HH):
                    nc.tensor.matmul(ps_o[:, h, r], fi[r, HW + h * HK:HW + (h + 1) * HK], am[r, h, r],
                                     start=(h == 0), stop=False, skip_group_check=True)
                for c in range(nch):
                    pe.wait_ge(sprime, n * 4 + c + 1)
                    for h in range(HH):
                        mm = nc.tensor.matmul(ps_o[:, h, c * ch:(c + 1) * ch], sp_[c % 2][:, h, :],
                                              qg[:, h, c * ch:(c + 1) * ch], start=False,
                                              stop=(c == nch - 1 and h == HH - 1), skip_group_check=True)
                    mm.then_inc(inter, 1)
                    if c + 4 < nch:
                        pe.wait_ge(s_done, n * 4 + c + 1)
                        increments(c + 4)
                pe.wait_ge(squared, n + 1)
                nc.tensor.matmul(ps_cn[:, :].rearrange("p (h t) -> p h t", h=HH)[:, :, r], pr.c("ones"), osq[:, :, r],
                                 start=True, stop=True).then_inc(msum, 1)

            tiles(pe, tile)


def mixer_merge(pr):
    nc, t = pr.nc, pr.t
    KA, KH = GW // P, HW // P
    acts_in = pr.sem("mm_acts")
    w_in = [pr.sem(f"mm_win{s}") for s in range(2)]
    z_in = [pr.sem(f"mm_zin{s}") for s in range(2)]
    (prod_a, prod_h, sig, scaled_a, scaled_h, summed, stored, m_free) = (pr.sem(f"mm_{n}") for n in (
        "proda", "prodh", "sig", "scaleda", "scaledh", "summed", "stored", "mfree"))
    with ExitStack() as cx:
        sb = lambda name, shape: cx.enter_context(nc.sbuf_tensor(f"mm_{name}", shape, F32))
        att, oh = sb("att", [P, KA, TOK]), sb("oh", [P, KH, TOK])
        wa, wh = [[sb(f"{n}{s}", [P, k, P]) for s in range(2)] for n, k in (("wa", KA), ("wh", KH))]
        z = [sb(f"z{s}", [P, 2, TOK]) for s in range(2)]
        ma = [sb(f"ma{s}", [P, 2, TOK]) for s in range(2)]
        ps_a = cx.enter_context(nc.psum_tensor("mm_psa", [P, 3 * 512], F32))
        ps_h = cx.enter_context(nc.psum_tensor("mm_psh", [P, 3 * 512], F32))
        block = cx.enter_context(nc.Block("mixer_merge"))
        turns = D // P // 2
        wa_v, wh_v = (t[n][0].rearrange("(k p) n -> p k n", p=P) for n in ("w_att_branch", "w_hg_branch"))
        gates = t["proj_t"][2 * HW:, :].rearrange("(g c p) t -> c p g t", g=2, p=P)

        @block.sync
        def _(sp):
            sp.dma_start(att[:, :, :], t["att_t"].rearrange("(k p) t -> p k t", p=P)).then_inc(acts_in, 16)
            sp.dma_start(oh[:, :, :], t["oh_t"].rearrange("(k p) t -> p k t", p=P)).then_inc(acts_in, 16)

            def load(c, s):
                sp.dma_start(wa[s][:, :, :], wa_v[:, :, bass.ds(c * P, P)]).then_inc(w_in[s], 16)
                sp.dma_start(wh[s][:, :, :], wh_v[:, :, bass.ds(c * P, P)]).then_inc(w_in[s], 16)
                sp.dma_start(z[s][:, :, :], gates[c]).then_inc(z_in[s], 16)

            for s in range(2):
                load(s, s)
            with sp.Fori(1, turns) as i:
                for s in range(2):
                    sp.wait_ge(scaled_h, i * 2 + s)
                    load(i * 2 + s, s)

        @block.tensor
        def _(pe):
            pe.wait_ge(acts_in, 32)
            with pe.Fori(0, turns) as i:
                for s in range(2):
                    pe.wait_ge(w_in[s], i * 32 + 32)
                    for w, x, k_n, ps, done, free in ((wa, att, KA, ps_a, prod_a, scaled_a),
                                                      (wh, oh, KH, ps_h, prod_h, scaled_h)):
                        pe.wait_ge(free, i * 2 + s + 1)
                        for k in range(k_n):
                            for a in range(0, TOK, 512):
                                e = min(a + 512, TOK)
                                mm = nc.tensor.matmul(ps[:, a:e], w[s][:, k, :], x[:, k, a:e],
                                                      start=(k == 0), stop=(k == k_n - 1))
                        mm.then_inc(done, 1)

        @block.scalar
        def _(act):
            with act.Fori(0, turns) as i:
                for s in range(2):
                    act.wait_ge(z_in[s], i * 16 + 16)
                    nc.scalar.activation(z[s][:, :, :], z[s][:, :, :], ACT.Sigmoid).then_inc(sig, 1)

        @block.vector
        def _(dve):
            dve.sem_inc(scaled_a, 1)
            dve.sem_inc(scaled_h, 1)
            with dve.Fori(0, turns) as i:
                for s in range(2):
                    n = i * 2 + s
                    dve.wait_ge(sig, n + 1)
                    dve.wait_ge(m_free, n + 1)
                    for j, (ps, done, scaled) in enumerate(((ps_a, prod_a, scaled_a), (ps_h, prod_h, scaled_h))):
                        dve.wait_ge(done, n + 1)
                        nc.vector.tensor_tensor(ma[s][:, j, :], ps[:, 0:TOK], z[s][:, j, :], ALU.mult).then_inc(scaled, 1)
                    dve.wait_ge(scaled_a, n + 2)
                    dve.wait_ge(scaled_h, n + 2)
                    nc.vector.tensor_tensor(ma[s][:, 0, :], ma[s][:, 0, :], ma[s][:, 1, :], ALU.add).then_inc(summed, 1)

        @block.gpsimd
        def _(pool):
            pool.sem_inc(m_free, 2)
            with pool.Fori(0, turns) as i:
                for s in range(2):
                    n = i * 2 + s
                    pool.wait_ge(summed, n + 1)
                    pool.dma_start(t["mix_t"][bass.ds(n * P, P), :], ma[s][:, 0, :]).then_inc(stored, 16)
                    pool.wait_ge(stored, n * 16 + 16)
                    pool.sem_inc(m_free, 1)


def mixer_output(pr):
    nc, t = pr.nc, pr.t
    w_in, gates_in, product, gated, added, stored, o_free = (pr.sem(f"mo_{n}") for n in (
        "win", "gates", "product", "gated", "added", "stored", "ofree"))
    in_ = [pr.sem(f"mo_in{s}") for s in range(2)]
    with ExitStack() as cx:
        sb = lambda name, shape: cx.enter_context(nc.sbuf_tensor(f"mo_{name}", shape, F32))
        w, g1 = sb("w", [P, KD, D]), [sb(f"g{r}", [P, D]) for r in range(2)]
        mix = [sb(f"mix{s}", [P, KD, P]) for s in range(2)]
        x = [sb(f"x{s}", [P, D]) for s in range(2)]
        o = [sb(f"o{s}", [P, D]) for s in range(2)]
        ps = [cx.enter_context(nc.psum_tensor(f"mo_ps{s}", [P, D], F32)) for s in range(2)]
        block = cx.enter_context(nc.Block("mixer_output"))
        mix_v = t["mix_t"].rearrange("(k p) t -> p k t", p=P)
        x_s = t["x_sample"].rearrange("b t d -> (b t) d")

        def tiles(eng, tile):
            with eng.Fori(0, PT // 2) as i:
                for s in range(2):
                    tile(i * 2 + s, s, i, P)
            tile(PT, 0, PT // 2, NS)

        @block.sync
        def _(sp):
            for r, (a, n) in enumerate(((0, P), (P, NS))):
                sp.dma_start(g1[r][0:n, :], t["modrep"][a:a + n, 2 * D:3 * D]).then_inc(gates_in, 16)
            sp.dma_start(w[:, :, :], t["w_out"][0].rearrange("(k p) n -> p k n", p=P)).then_inc(w_in, 16)

            def tile(n, s, i, rows):
                sp.wait_ge(added, n + 1)
                sp.dma_start(mix[s][:, :, 0:rows], mix_v[:, :, bass.ds(n * P, rows)]).then_inc(in_[s], 16)
                src = t["x_prompt"][0][bass.ds(n * P, P), :] if rows == P else x_s
                sp.dma_start(x[s][0:rows, :], src).then_inc(in_[s], 16)
            tiles(sp, tile)

        @block.tensor
        def _(pe):
            pe.wait_ge(w_in, 16)

            def tile(n, s, i, rows):
                pe.wait_ge(in_[s], i * 32 + 32)
                pe.wait_ge(gated, n + 1)
                for k in range(KD):
                    for a in range(0, D, 512):
                        mm = nc.tensor.matmul(ps[s][0:rows, a:a + 512], mix[s][:, k, 0:rows], w[:, k, a:a + 512],
                                              start=(k == 0), stop=(k == KD - 1))
                mm.then_inc(product, 1)
            tiles(pe, tile)

        @block.vector
        def _(dve):
            dve.sem_inc(gated, 2)
            dve.sem_inc(added, 2)
            dve.wait_ge(gates_in, 32)

            def tile(n, s, i, rows):
                r = slice(0, rows)
                dve.wait_ge(product, n + 1)
                dve.wait_ge(o_free, n + 1)
                nc.vector.tensor_tensor(o[s][r, :], ps[s][r, :], g1[0 if rows == P else 1][r, :], ALU.mult).then_inc(gated, 1)
                dve.wait_ge(gated, n + 3)
                nc.vector.tensor_tensor(o[s][r, :], o[s][r, :], x[s][r, :], ALU.add).then_inc(added, 1)
            tiles(dve, tile)

        @block.gpsimd
        def _(pool):
            pool.sem_inc(o_free, 2)

            def tile(n, s, i, rows):
                pool.wait_ge(added, n + 3)
                pool.dma_start(t["x1"][bass.ds(n * P, rows), :], o[s][0:rows, :]).then_inc(stored, 16)
                pool.wait_ge(stored, n * 16 + 16)
                pool.sem_inc(o_free, 1)
            tiles(pool, tile)


def routing(pr):
    nc, t = pr.nc, pr.t
    HP = 2 * HEADS
    sub_in, sub_tr, sub_t, scored, sc_out, step_s, done, exp_in, exp_done, stored, out_free, passed = (
        pr.sem(f"rt_{n}") for n in ("subin", "subtr", "subt", "scored", "scout", "step", "done", "expin",
                                    "exp", "stored", "outfree", "passed"))
    q_in = [pr.sem(f"rt_qin{s}") for s in range(2)]
    with ExitStack() as cx:
        sb = lambda name, shape, dt=F32: cx.enter_context(nc.sbuf_tensor(f"rt_{name}", shape, dt))
        sub, sub_tt = sb("sub", [P, HP, P]), sb("subt", [P, HP, P])
        q = [sb(f"q{s}", [P, HP, P]) for s in range(2)]
        sc, sc2 = sb("sc", [P, HP, KEYS]), sb("sc2", [P, HP, KEYS])
        top, ix = sb("top", [P, HP, TOPK]), sb("ix", [P, HP, TOPK], U32)
        ixf = sb("ixf", [P, HP, TOPK])
        cand, cand2 = sb("cand", [P, HEADS, TOPK * TOPK]), sb("cand2", [P, HEADS, TOPK * TOPK])
        best, ci = sb("best", [P, HEADS, TOPK]), sb("ci", [P, HEADS, TOPK], U32)
        c1, c2 = sb("c1", [P, HEADS, TOPK], U32), sb("c2", [P, HEADS, TOPK], U32)
        c1f, c2f = sb("c1f", [P, HEADS, TOPK]), sb("c2f", [P, HEADS, TOPK])
        hot = sb("hot", [P, HEADS, TOPK * TOPK])
        e1, e2 = sb("e1", [P, PICKS]), sb("e2", [P, PICKS])
        eid, ex, gate = sb("eid", [P, PICKS], U32), sb("ex", [P, HEADS, TOPK]), sb("gate", [P, HEADS, TOPK])
        dn = sb("dn", [P, HEADS])
        ps = [cx.enter_context(nc.psum_tensor(f"rt_ps{s}", [P, HP, KEYS], F32)) for s in range(2)]
        block = cx.enter_context(nc.Block("routing"))
        qry = t["qry_t"].rearrange("(k p) t -> p k t", p=P)

        def tiles(eng, tile):
            with eng.Fori(0, PT // 2) as i:
                for s in range(2):
                    tile(i * 2 + s, s, i, P)
            tile(PT, 0, PT // 2, NS)

        @block.sync
        def _(sp):
            sp.dma_start(sub[:, :, :], t["peer_subkeys"][0].rearrange("h p k d -> k (h p) d")).then_inc(sub_in, 16)

            def tile(n, s, i, rows):
                sp.wait_ge(scored, n + 1)
                sp.dma_start(q[s][:, :, 0:rows], qry[:, :, bass.ds(n * P, rows)]).then_inc(q_in[s], 16)
            tiles(sp, tile)

        @block.tensor
        def _(pe):
            pe.wait_ge(sub_in, 16)
            for j in range(HP):
                mm = nc.tensor.transpose(ps[0][:, j, :], sub[:, j, :], pr.c("ident"))
            mm.then_inc(sub_tr, 1)
            pe.wait_ge(sub_t, 1)
            pe.sem_inc(scored, 2)

            def tile(n, s, i, rows):
                pe.wait_ge(q_in[s], i * 16 + 16)
                pe.wait_ge(sc_out, n + 1)
                for j in range(HP):
                    mm = nc.tensor.matmul(ps[s][0:rows, j, :], q[s][:, j, 0:rows], sub_tt[:, j, :], start=True, stop=True)
                mm.then_inc(scored, 1)
            tiles(pe, tile)

        @block.scalar
        def _(act):
            act.wait_ge(sub_tr, 1)
            nc.scalar.copy(sub_tt[:, :, :], ps[0][:, :, :]).then_inc(sub_t, 1)
            act.sem_inc(sc_out, 2)

            def tile(n, s, i, rows):
                act.wait_ge(scored, n + 3)
                act.wait_ge(done, n + 1)
                nc.scalar.copy(sc[0:rows, :, :], ps[s][0:rows, :, :]).then_inc(sc_out, 1)
                act.wait_ge(exp_in, n + 1)
                nc.scalar.activation(ex[0:rows], ex[0:rows], ACT.Exp).then_inc(exp_done, 1)
            tiles(act, tile)

        @block.vector
        def _(dve):
            step = Ordered(dve, step_s)
            V = nc.vector
            dve.sem_inc(done, 1)
            STEPS = 4 + 4 + 16

            def tile(n, s, i, rows):
                r = slice(0, rows)
                step.turn(n, STEPS, 0)

                def top16(src, work, values, index, count):
                    dve.sem_inc(passed, 1)
                    for j in range(count):
                        last = V.max(values[r, j, 0:8], src[r, j, :])
                    step(last)
                    dve.sem_inc(passed, 1)
                    for j in range(count):
                        V.max_index(index[r, j, 0:8], values[r, j, 0:8], src[r, j, :])
                        last = V.match_replace(work[r, j, :], values[r, j, 0:8], src[r, j, :], NEG)
                    step(last)
                    dve.sem_inc(passed, 1)
                    for j in range(count):
                        last = V.max(values[r, j, 8:16], work[r, j, :])
                    step(last)
                    dve.sem_inc(passed, 1)
                    for j in range(count):
                        last = V.max_index(index[r, j, 8:16], values[r, j, 8:16], work[r, j, :])
                    step(last)

                dve.wait_ge(sc_out, n + 3)
                top16(sc, sc2, top, ix, HP)
                step(V.tensor_copy(ixf[r], ix[r]))
                halves = top[r].rearrange("p (h e) k -> p h e k", e=2)
                grid = [rows, HEADS, TOPK, TOPK]
                as_grid = lambda x: x.rearrange("p h (a b) -> p h a b", b=TOPK)
                for h in range(HEADS):
                    last = V.tensor_tensor(as_grid(cand[r])[:, h], halves[:, h, 0].unsqueeze(2).broadcast_to([rows, TOPK, TOPK]),
                                           halves[:, h, 1].unsqueeze(1).broadcast_to([rows, TOPK, TOPK]), ALU.add)
                step(last)
                top16(cand, cand2, best, ci, HEADS)
                step(V.tensor_single_scalar(c1[r], ci[r], 4, ALU.logical_shift_right))
                step(V.tensor_single_scalar(c2[r], ci[r], TOPK - 1, ALU.bitwise_and))
                step(V.tensor_copy(c1f[r], c1[r]))
                step(V.tensor_copy(c2f[r], c2[r]))
                keys = ixf[r].rearrange("p (h e) k -> p h e k", e=2)
                for e, (place, out) in enumerate(((c1f, e1), (c2f, e2))):
                    for h in range(HEADS):
                        last = V.tensor_tensor(as_grid(hot[r])[:, h], place[r, h].unsqueeze(2).broadcast_to([rows, TOPK, TOPK]),
                                               pr.c("iota16", rows).unsqueeze(1).broadcast_to([rows, TOPK, TOPK]), ALU.is_equal)
                    step(last)
                    for h in range(HEADS):
                        last = V.tensor_tensor(as_grid(hot[r])[:, h], as_grid(hot[r])[:, h],
                                               keys[:, h, e].unsqueeze(1).broadcast_to([rows, TOPK, TOPK]), ALU.mult)
                    step(last)
                    step(V.tensor_reduce(out[r, :], hot[r].rearrange("p h (a b) -> p (h a) b", b=TOPK), AX, ALU.add))
                dve.wait_ge(out_free, n + 1)
                step(V.scalar_tensor_tensor(eid[r, :], e1[r, :], float(KEYS), e2[r, :], ALU.mult, ALU.add))
                V.tensor_tensor(ex[r], best[r], best[r, :, 0:1].broadcast_to([rows, HEADS, TOPK]), ALU.subtract)\
                    .then_inc(exp_in, 1)
                dve.wait_ge(exp_done, n + 1)
                step(V.tensor_reduce(dn[r, :], ex[r], AX, ALU.add))
                step(V.reciprocal(dn[r, :], dn[r, :]))
                V.tensor_tensor(gate[r], ex[r], dn[r].unsqueeze(2).broadcast_to([rows, HEADS, TOPK]), ALU.mult)\
                    .then_inc(done, 1)
                assert step.n == STEPS - 1, step.n
                step(V.tensor_copy(c1f[r], c2f[r]))
            tiles(dve, tile)

        @block.gpsimd
        def _(pool):
            pool.sem_inc(out_free, 1)

            def tile(n, s, i, rows):
                pool.wait_ge(done, n + 2)
                pool.dma_start(t["eid"][bass.ds(n * P, rows), :], eid[0:rows, :]).then_inc(stored, 16)
                pool.dma_start(t["gate"][bass.ds(n * P, rows), :], gate[0:rows].rearrange("p h k -> p (h k)"))\
                    .then_inc(stored, 16)
                pool.wait_ge(stored, n * 32 + 32)
                pool.sem_inc(out_free, 1)
            tiles(pool, tile)


def retrieval(pr):
    nc, t = pr.nc, pr.t
    RING = 8
    GRP = 2
    INNER = PICKS // RING // GRP
    par = lambda name: [pr.sem(f"rv_{name}{s}") for s in range(2)]
    h_in, eid_in, gate_in, x_in = par("hin"), par("eidin"), par("gatein"), par("xin")
    u_in = [pr.sem(f"rv_u{b}") for b in range(RING)]
    v_in = [pr.sem(f"rv_v{b}") for b in range(RING)]
    (base_in, zeroed, idx_u, idx_v, u_used, v_used, act8_done, acts, gelu_done, w_done, diag, xg, x2, ssq, ms, ln, rstd, newton,
     y_ready, stored, y_free, picked_u, picked_v) = (pr.sem(f"rv_{n}") for n in (
         "base", "zeroed", "idxu", "idxv", "uused", "vused", "act8", "acts", "gelu", "w", "diag", "xg", "x2", "ssq",
         "ms", "ln", "rstd", "newton", "y", "stored", "yfree", "pickedu", "pickedv"))
    passed = [pr.sem(f"rv_passed{e}") for e in range(2)]
    with ExitStack() as cx:
        sb = lambda name, shape, dt=F32: cx.enter_context(nc.sbuf_tensor(f"rv_{name}", shape, dt))
        two = lambda name, shape, dt=F32: [sb(f"{name}{s}", shape, dt) for s in range(2)]
        u = [sb(f"u{b}", [P, D]) for b in range(RING)]
        v = [sb(f"v{b}", [P, D]) for b in range(RING)]
        dg = [sb(f"dg{b}", [P, P]) for b in range(RING)]
        h2, x1, gate, eid = two("h2", [P, D]), two("x1", [P, D]), two("gate", [P, PICKS]), two("eid", [P, PICKS], U32)
        iu, iv = two("iu", [P, RING], U32), two("iv", [P, RING], U32)
        act8 = two("act8", [P, RING])
        act_, w = two("act", [P, PICKS]), two("w", [P, PICKS])
        g2, fg = two("g2", [P, D]), sb("fg", [P, D])
        zero, junk, y, st = sb("zero", [P, 512]), sb("junk", [P, D]), sb("y", [P, D]), sb("st", [P, 8])
        ps = [cx.enter_context(nc.psum_tensor(f"rv_ps{s}", [P, D], F32)) for s in range(2)]
        block = cx.enter_context(nc.Block("retrieval"))
        ROWS = lambda n: NS if isinstance(n, int) and n == PT else P

        def loads_of(n, s):
            return (n // 2 + 1) * 16 if isinstance(n, int) else (n - s) * 8 + 16

        def run(eng, joint):
            joint(0, None, 0)
            with eng.Fori(0, PT // 2 - 1) as i:
                joint(i * 2 + 1, i * 2, 1)
                joint(i * 2 + 2, i * 2 + 1, 0)
            joint(PT - 1, PT - 2, 1)
            joint(PT, PT - 1, 0)
            joint(None, PT, 1)

        @block.sync
        def _(sp):
            for r, (a, n) in enumerate(((0, P), (P, NS))):
                sp.dma_start(g2[r][0:n, :], t["modrep"][a:a + n, 5 * D:6 * D]).then_inc(base_in, 16)
            sp.dma_start(fg[:, :], t["final_norm_g"].partition_broadcast(P)).then_inc(base_in, 16)

            def load(n, s, rows):
                at = bass.ds(n * P, rows)
                sp.wait_ge(acts, n + 1)
                sp.dma_start(h2[s][0:rows, :], t["h2"][at, :]).then_inc(h_in[s], 16)
                sp.wait_ge(w_done, n + 1)
                sp.dma_start(gate[s][0:rows, :], t["gate"][at, :]).then_inc(gate_in[s], 16)
                sp.wait_ge(picked_v, n + 1)
                sp.dma_start(eid[s][0:rows, :], t["eid"][at, :]).then_inc(eid_in[s], 16)
                sp.wait_ge(x2, n + 1)
                sp.dma_start(x1[s][0:rows, :], t["x1"][at, :]).then_inc(x_in[s], 16)

            with sp.Fori(0, PT // 2) as i:
                for s in range(2):
                    load(i * 2 + s, s, P)
            load(PT, 0, NS)

        @block.gpsimd
        def _(pool):
            nc.gpsimd.memset(zero[:, :], 0.0).then_inc(zeroed, 1)
            pool.sem_inc(picked_v, 2)

            def joint(nu, nv, su):
                sv = 1 - su
                if nu is not None:
                    pool.wait_ge(eid_in[su], loads_of(nu, su))
                    pool.sem_inc(passed[0], 1)
                with pool.Fori(0, INNER) as j:
                    for g in range(GRP):
                        for n, s, used, idx, idx_done, ring, in_, table in (
                                (nu, su, u_used, iu, idx_u, u, u_in, "peer_u"), (nv, sv, v_used, iv, idx_v, v, v_in, "peer_v")):
                            if n is None:
                                continue
                            rows = ROWS(n)
                            k = n * (PICKS // RING) + j * GRP + g
                            nc.gpsimd.tensor_copy(idx[g][0:rows, :], eid[s][0:rows, bass.ds(j * (GRP * RING) + g * RING, RING)])\
                                .then_inc(idx_done, 1)
                            pool.wait_ge(idx_done, k + 1)
                            for b in range(RING):
                                pool.wait_ge(used, k * RING + b + 1)
                                pool.sem_inc(passed[0], 1)
                                nc.gpsimd.indirect_dma_start(
                                    out=ring[b][0:rows, :], out_offset=None, in_=t[table][0],
                                    in_offset=bass.IndirectOffsetOnAxis(ap=idx[g][0:rows, b:b + 1], axis=0),
                                ).then_inc(in_[b], 16)
                if nv is not None:
                    pool.sem_inc(picked_v, 1)

            run(pool, joint)

        @block.vector
        def _(dve):
            V = nc.vector
            dve.wait_ge(base_in, 48)
            dve.sem_inc(u_used, RING)
            dve.sem_inc(acts, 2)
            dve.sem_inc(w_done, 2)
            dve.sem_inc(x2, 2)

            def joint(nu, nv, su):
                sv = 1 - su
                if nu is not None:
                    dve.wait_ge(h_in[su], loads_of(nu, su))
                    dve.sem_inc(passed[1], 1)
                with dve.Fori(0, INNER) as j:
                    for g in range(GRP):
                        at = bass.ds(j * (GRP * RING) + g * RING, RING)
                        for b in range(RING):
                            if nu is not None:
                                rows = ROWS(nu)
                                k = nu * (PICKS // RING) + j * GRP + g
                                dve.wait_ge(u_in[b], k * 16 + 16)
                                V.tensor_tensor_reduce(out=u[b][0:rows, :], in0=u[b][0:rows, :], in1=h2[su][0:rows, :],
                                                       scale=1.0, scalar=0.0, op0=ALU.mult, op1=ALU.add,
                                                       accum_out=act8[g][0:rows, b:b + 1]).then_inc(u_used, 1)
                            if nv is not None:
                                rows = ROWS(nv)
                                k = nv * (PICKS // RING) + j * GRP + g
                                dve.wait_ge(v_used, k * RING + b + 1)
                                V.tensor_scalar(dg[b][0:rows, :], pr.c("ident")[0:rows, :],
                                                w[sv][0:rows, bass.ds(j * (GRP * RING) + (g * RING + b), 1)], None,
                                                ALU.mult).then_inc(diag, 1)
                        if nu is not None:
                            rows = ROWS(nu)
                            k = nu * (PICKS // RING) + j * GRP + g
                            dve.wait_ge(u_used, k * RING + 2 * RING)
                            V.tensor_copy(act_[su][0:rows, at], act8[g][0:rows, :]).then_inc(act8_done, 1)
                            dve.wait_ge(act8_done, k + 1)
                if nu is not None:
                    rows = ROWS(nu)
                    dve.sem_inc(acts, 1)
                    dve.wait_ge(gate_in[su], loads_of(nu, su))
                    dve.wait_ge(gelu_done, nu + 1)
                    V.tensor_tensor(w[su][0:rows, :], act_[su][0:rows, :], gate[su][0:rows, :], ALU.mult).then_inc(w_done, 1)
                    dve.wait_ge(w_done, nu + 3)
                if nv is not None:
                    rows = ROWS(nv)
                    r = slice(0, rows)
                    dve.wait_ge(v_used, nv * PICKS + PICKS + RING)
                    dve.wait_ge(x_in[sv], loads_of(nv, sv))
                    V.tensor_tensor(junk[r, :], ps[sv][r, :], g2[0 if rows == P else 1][r, :], ALU.mult).then_inc(xg, 1)
                    dve.wait_ge(xg, nv + 1)
                    V.tensor_tensor(junk[r, :], junk[r, :], x1[sv][r, :], ALU.add).then_inc(x2, 1)
                    dve.wait_ge(y_free, nv + 1)
                    dve.wait_ge(ssq, nv + 1)
                    V.tensor_scalar(st[r, 1:2], st[r, 0:1], 1.0 / D, EPS, ALU.mult, ALU.add).then_inc(ms, 1)
                    dve.wait_ge(ms, nv + 1)
                    dve.wait_ge(rstd, nv + 1)
                    step = Ordered(dve, newton)
                    step.turn(nv, 4, 0)
                    step(V.scalar_tensor_tensor(st[r, 4:5], st[r, 3:4], st[r, 1:2], st[r, 3:4], ALU.mult, ALU.mult))
                    step(V.tensor_scalar(st[r, 4:5], st[r, 4:5], -0.5, 1.5, ALU.mult, ALU.add))
                    step(V.tensor_tensor(st[r, 5:6], st[r, 3:4], st[r, 4:5], ALU.mult))
                    step(V.scalar_tensor_tensor(y[r, :], junk[r, :], st[r, 5:6], fg[r, :], ALU.mult, ALU.mult))
                    dve.sem_inc(y_ready, 1)

            run(dve, joint)

        @block.scalar
        def _(act):
            def joint(nu, nv, su):
                if nu is not None:
                    rows = ROWS(nu)
                    act.wait_ge(acts, nu + 3)
                    nc.scalar.activation(act_[su][0:rows, :], act_[su][0:rows, :], ACT.Gelu_apprx_tanh).then_inc(gelu_done, 1)
                if nv is not None:
                    rows = ROWS(nv)
                    r = slice(0, rows)
                    act.wait_ge(x2, nv + 3)
                    nc.scalar.activation(y[r, :], junk[r, :], ACT.Square, accum_out=st[r, 0:1]).then_inc(ssq, 1)
                    act.wait_ge(ms, nv + 1)
                    nc.scalar.activation(st[r, 2:3], st[r, 1:2], ACT.Ln).then_inc(ln, 1)
                    act.wait_ge(ln, nv + 1)
                    nc.scalar.activation(st[r, 3:4], st[r, 2:3], ACT.Exp, scale=-0.5).then_inc(rstd, 1)
                    act.wait_ge(y_ready, nv + 1)
                    whole = t["y_prompt"][0] if rows == P else t["y_sample"].rearrange("b t d -> (b t) d")
                    dst = whole[bass.ds(nv * P, P), :] if rows == P else whole
                    act.dma_start(dst, y[r, :]).then_inc(stored, 16)
                    act.wait_ge(stored, nv * 16 + 16)
                    act.sem_inc(y_free, 1)

            act.sem_inc(y_free, 1)
            run(act, joint)

        @block.tensor
        def _(pe):
            pe.wait_ge(zeroed, 1)
            pe.sem_inc(v_used, RING)

            def joint(nu, nv, su):
                if nv is None:
                    return
                sv, rows = 1 - su, ROWS(nv)
                pe.wait_ge(x2, nv + 1)
                for a in range(0, D, 512):
                    nc.tensor.matmul(ps[sv][:, a:a + 512], zero[0:rows, 0:P], zero[0:rows, :],
                                     start=True, stop=False, skip_group_check=True)
                with pe.Fori(0, INNER) as j:
                    for g in range(GRP):
                        k = nv * (PICKS // RING) + j * GRP + g
                        for b in range(RING):
                            pe.wait_ge(v_in[b], k * 16 + 16)
                            pe.wait_ge(diag, k * RING + b + 1)
                            for a in range(0, D, 512):
                                mm = nc.tensor.matmul(ps[sv][:, a:a + 512], dg[b][0:rows, :], v[b][0:rows, a:a + 512],
                                                      start=False, stop=False, skip_group_check=True)
                            mm.then_inc(v_used, 1)

            run(pe, joint)


def windows(pr):
    nc, t = pr.nc, pr.t
    done = [pr.sem(f"wd_{n}") for n in ("sp", "act")]
    with nc.Block("windows") as block:
        def copies(eng, sem, which):
            n = 0
            for g, (w, _) in enumerate(GROUPS):
                for name, col in which:
                    cols = slice(col + g * GW, col + (g + 1) * GW)
                    flat = lambda x: x.rearrange("b w h d -> b w (h d)")
                    dst = flat(t[f"{name}{g}_s"][0])
                    for out, src in (
                            (flat(t[f"{name}{g}_p"][0])[0], t["proj_n"][SEQ - w:SEQ, cols]),
                            (dst[:, 0:w - NT], flat(t[f"cache_{name}{g}"][0])[:, NT:]),
                            (dst[:, w - NT:], t["proj_n"][SEQ:TOK, cols].rearrange("(b t) c -> b t c", t=NT))):
                        eng.dma_start(out, src).then_inc(sem, 16)
                        n += 16
            eng.wait_ge(sem, n)

        @block.sync
        def _(sp):
            copies(sp, done[0], (("k", C_K),))

        @block.scalar
        def _(act):
            copies(act, done[1], (("v", C_V),))


STAGES = (conditioning, mixer_input, attention_prompt, attention_sample, attention_merge, recurrence, mixer_merge,
          mixer_output, windows, retrieval_queries, routing, retrieval)


def build(nc, t, scratch_kind="Internal", stages=None):
    with ExitStack() as ctx:
        pr = Program(nc, t, ctx, scratch_kind)
        load_constants(pr)
        for n, stage in enumerate(STAGES):
            if stages is None or n in stages:
                stage(pr)
                pr.clear_semaphores()


_INS = ["x_prompt", "x_sample", "cache_k0", "cache_v0", "cache_k1", "cache_v1", "cache_k2", "cache_v2", "state_hgrn",
        "c_prompt", "c_sample", "ada_w", "ada_b", "norm1_g", "w_in", "w_att_branch", "w_hg_branch", "w_out",
        "hg_lower_bound", "hg_norm_g", "norm2_g", "peer_wq", "peer_subkeys", "peer_u", "peer_v", "final_norm_g"]
_OUTS = [("y_prompt", (1, 1024, 1024)), ("y_sample", (8, 8, 1024)),
         ("k0_p", (1, 1, 128, 4, 64)), ("v0_p", (1, 1, 128, 4, 64)), ("k1_p", (1, 1, 512, 4, 64)),
         ("v1_p", (1, 1, 512, 4, 64)), ("k2_p", (1, 1, 1024, 4, 64)), ("v2_p", (1, 1, 1024, 4, 64)),
         ("hgrn_p", (1, 1, 4, 128, 128)),
         ("k0_s", (1, 8, 128, 4, 64)), ("v0_s", (1, 8, 128, 4, 64)), ("k1_s", (1, 8, 512, 4, 64)),
         ("v1_s", (1, 8, 512, 4, 64)), ("k2_s", (1, 8, 1024, 4, 64)), ("v2_s", (1, 8, 1024, 4, 64)),
         ("hgrn_s", (1, 8, 4, 128, 128))]


def kernel(**inputs):
    import concourse.bacc as _bacc
    from concourse.bass_utils import run_bass_kernel_spmd as _run

    nc = _bacc.Bacc("TRN2", target_bir_lowering=False, num_devices=1)
    arrays, t = {"in_const_dram": CONST}, {}
    for name in _INS:
        arrays[f"in_{name}_dram"] = np.ascontiguousarray(inputs[name])
    for name, a in arrays.items():
        t[name[3:-5]] = nc.dram_tensor(name, a.shape, mybir.dt.from_np(a.dtype), kind="ExternalInput").ap()
    for name, shape in _OUTS:
        t[name] = nc.dram_tensor(f"out_{name}_dram", shape, F32, kind="ExternalOutput").ap()
    build(nc, t)
    r = _run(nc, [arrays], core_ids=[0])
    return tuple(r.results[0][f"out_{name}_dram"] for name, _ in _OUTS)
```

```python
from contextlib import ExitStack

import numpy as np

import concourse.bass as bass
from concourse import mybir

F32 = mybir.dt.float32
U32 = mybir.dt.uint32
ALU = mybir.AluOpType
ACT = mybir.ActivationFunctionType
AX = mybir.AxisListType.X

P = 128
D = 1024
KD = D // P
SEQ = 1024
NB, NT = 8, 8
NS = NB * NT
TOK = SEQ + NS
PT = SEQ // P
EPS = 1e-6
GROUPS = ((128, 1), (512, 4), (1024, 16))
HPG, DH = 4, 64
GW = HPG * DH
AW = len(GROUPS) * GW
HH, HK = 4, 128
HW = HH * HK
CH = 32
NCH = P // CH
HEADS, KEYS, TOPK, DHALF = 8, 128, 16, 128
PICKS = HEADS * TOPK
NEG = -1e30
REC = DH + 2
C_Q, C_K, C_V = 0, AW, 2 * AW
C_ZF, C_ZI = 3 * AW, 3 * AW + HW
C_ZQ = C_ZI + HW
C_ZG = C_ZQ + HW
C_ZA = C_ZG + HW
C_ZH = C_ZA + D
NATC = C_ZQ
TRC = 2 * HW + 2 * D
SLOPES = [float(x) for x in np.exp2(np.float32(-8.0) * np.arange(1, 13, dtype=np.float32) / np.float32(12))]
W_S = (P + NS, 512 + NS, 512 + NS)


def constants():
    i, j = np.arange(P)[:, None], np.arange(P)[None, :]
    out, at = [], {}

    def put(name, a):
        a = np.asarray(a, np.float32)
        full = np.zeros((P, a.shape[1]), np.float32)
        full[: a.shape[0]] = a
        at[name] = (sum(x.shape[1] for x in out), a.shape[1])
        out.append(full)

    put("ident", np.eye(P))
    put("ones", np.ones((P, P)))
    def band(dil):
        delta = i + P - np.arange(2 * P)[None, :]
        return np.where((delta >= 0) & (delta <= P), -delta * dil, NEG)
    first = band(1)
    first[:, :P] = NEG
    put("pen0", np.concatenate([first, band(1)], 1))
    put("pen1", band(4))
    put("pen2", np.where((i // 64 == j // 64) & (i % 64 >= j % 64), -(i % 64 - j % 64) * 16, NEG))
    for half in range(2):
        bb, t = i // 32, i % 8
        new = np.arange(NS)[None, :]
        for g, (w, dil) in enumerate(GROUPS):
            n = np.arange(min(w, 512))[None, :]
            kb, p = n // P, n % P
            idx = (n, p * 4 + kb, p % 64 * 16 + p // 64 * 4 + kb)[g]
            d_old = w + t - idx
            d_new = t - new % 8
            same = new // 8 == 4 * half + bb
            p_old = np.where((d_old % dil == 0) & (d_old <= P * dil), -d_old, NEG)
            p_new = np.where(same & (d_new >= 0) & (d_new % dil == 0), -d_new, NEG)
            put(f"pens{half}{g}", np.concatenate([p_old, p_new], 1))
    sl = np.array([[8.0 * SLOPES[4 * g + r % 32 // 8] for g in range(3)] for r in range(P)])
    put("slope_s", sl)
    put("headmask", (i % 32 // 8 == np.arange(4)[None, :]))
    def sums(n, ch):
        s, t = np.arange(n)[:, None], np.arange(n)[None, :]
        mid = ch // 2 - 1
        c = (s // ch == t // ch) * ((s % ch <= t % ch) * 1.0 - (s % ch <= mid))
        m = (s // ch == np.arange(n // ch)[None, :]) & (s % ch <= mid)
        return np.concatenate([c, m], 1), (s // ch == t // ch) & (s <= t)
    a, m = sums(P, CH)
    put("tri_p", a)
    put("causal_p", m)
    a, m = sums(NS, NT)
    put("tri_s", a)
    put("causal_s", m)
    put("seqmask", (np.arange(NS)[:, None] // 8 == np.arange(8)[None, :]))
    put("sel_p", np.concatenate([np.ones((1, P)), np.zeros((8, P))]))
    put("sel_s", np.arange(9)[:, None] == 1 + np.arange(NS)[None, :] // 8)
    put("iota16", np.broadcast_to(np.arange(16), (P, 16)))
    return np.concatenate(out, 1), at


CONST, AT = constants()

SCRATCH = {
    "modrep": ([P + NS, 6 * D], F32), "proj_n": ([TOK, NATC], F32), "proj_t": ([TRC, TOK], F32),
    "att_rec": ([3, TOK, HPG * REC], F32), "att_t": ([GW, TOK], F32), "oh_t": ([HW, TOK], F32),
    "mix_t": ([D, TOK], F32), "x1": ([TOK, D], F32), "h2": ([TOK, D], F32),
    "qry_t": ([2 * HEADS * DHALF, TOK], F32),
}


class Ordered:

    def __init__(self, eng, sem):
        self.eng, self.sem, self.base, self.n = eng, sem, 0, 0

    def turn(self, i, steps, start):
        self.base, self.n = i * steps + start, 0

    def __call__(self, ins):
        ins.then_inc(self.sem, 1)
        self.n += 1
        self.eng.wait_ge(self.sem, self.base + self.n)


class Program:
    def __init__(self, nc, t, ctx, scratch_kind):
        self.nc, self.t, self.ctx = nc, t, ctx
        self.sems = []
        self.const = ctx.enter_context(nc.sbuf_tensor("const", [P, CONST.shape[1]], F32))
        for name, (shape, dtype) in SCRATCH.items():
            kind = scratch_kind if isinstance(scratch_kind, str) else scratch_kind(name)
            t[name] = nc.dram_tensor(name, shape, dtype, kind=kind).ap()

    def c(self, name, rows=P):
        a, n = AT[name]
        return self.const[0:rows, a:a + n]

    def sem(self, name):
        handle = self.nc.alloc_semaphore(name=name)
        self.sems.append(handle)
        return handle

    def clear_semaphores(self):
        nc = self.nc
        nc.clear_and_free_semaphores(self.sems)
        nc.all_engine_barrier()
        self.sems = []


def load_constants(pr):
    nc = pr.nc
    loaded = pr.sem("const_loaded")
    with nc.Block("load_constants") as block:
        @block.sync
        def _(sp):
            sp.dma_start(pr.const[:, :], pr.t["const"]).then_inc(loaded, 16)
            sp.wait_ge(loaded, 16)


def conditioning(pr):
    nc, t = pr.nc, pr.t
    CW = 512
    turns = 6 * D // CW // 2
    s_in, s_sig, s_act, s_tr, s_ct = (pr.sem(f"ad_{n}") for n in ("in", "sig", "silu", "tr", "ct"))
    w_in = [pr.sem(f"ad_win{s}") for s in range(2)]
    s_mod, s_modsb, s_rep, s_repsb = (pr.sem(f"ad_{n}") for n in ("mod", "modsb", "rep", "repsb"))
    rep_free, s_stored = pr.sem("ad_repfree"), pr.sem("ad_stored")
    w_v = t["ada_w"][0].rearrange("(k p) n -> p k n", p=P)
    with ExitStack() as cx:
        sb = lambda name, shape: cx.enter_context(nc.sbuf_tensor(name, shape, F32))
        ps = lambda name, shape: cx.enter_context(nc.psum_tensor(name, shape, F32))
        c9, sg = sb("c9", [9, D]), sb("sg", [9, D])
        ct = sb("ct", [P, KD, 9])
        w = [sb(f"adw{s}", [P, KD, CW]) for s in range(2)]
        bias = [sb(f"adb{s}", [1, CW]) for s in range(2)]
        modsb = [sb(f"modsb{s}", [9, CW]) for s in range(2)]
        rep = [sb(f"rep{s}", [P, CW]) for s in range(2)]
        reps = [sb(f"reps{s}", [NS, CW]) for s in range(2)]
        p_tr = ps("p_tr", [P, KD, 16])
        p_mod = [ps(f"p_mod{s}", [9, CW]) for s in range(2)]
        p_rep = [ps(f"p_rep{s}", [P, CW]) for s in range(2)]
        p_reps = [ps(f"p_reps{s}", [NS, CW]) for s in range(2)]
        block = cx.enter_context(nc.Block("conditioning"))

        @block.sync
        def _(sp):
            sp.dma_start(c9[0:1, :], t["c_prompt"]).then_inc(s_in, 16)
            sp.dma_start(c9[1:9, :], t["c_sample"]).then_inc(s_in, 16)

            def load(s, col):
                sp.dma_start(w[s][:, :, :], w_v[:, :, bass.ds(col, CW)]).then_inc(w_in[s], 16)
                sp.dma_start(bias[s][:, :], t["ada_b"][:, bass.ds(col, CW)]).then_inc(w_in[s], 16)

            for s in range(2):
                load(s, s * CW)
            with sp.Fori(1, turns) as i:
                for s in range(2):
                    sp.wait_ge(s_mod, i * 2 + s - 1)
                    load(s, (i * 2 + s) * CW)

        @block.tensor
        def _(pe):
            pe.wait_ge(s_act, 1)
            for k in range(KD):
                tr = nc.tensor.transpose(p_tr[:, k, 0:9], c9[:, k * P:(k + 1) * P], pr.c("ident")[0:9, 0:9])
            tr.then_inc(s_tr, 1)
            pe.wait_ge(s_ct, 1)
            with pe.Fori(0, turns) as i:
                for s in range(2):
                    pe.wait_ge(w_in[s], i * 32 + 32)
                    for k in range(KD):
                        nc.tensor.matmul(p_mod[s][:, :], ct[:, k, :], w[s][:, k, :], start=(k == 0), stop=False)
                    nc.tensor.matmul(p_mod[s][:, :], pr.c("ones")[0:1, 0:9], bias[s][:, :],
                                     start=False, stop=True).then_inc(s_mod, 1)
                for s in range(2):
                    pe.wait_ge(s_modsb, i * 2 + s + 1)
                    nc.tensor.matmul(p_rep[s][:, :], pr.c("sel_p", 9), modsb[s][:, :], start=True, stop=True)
                    nc.tensor.matmul(p_reps[s][:, :], pr.c("sel_s", 9), modsb[s][:, :],
                                     start=True, stop=True).then_inc(s_rep, 1)

        @block.scalar
        def _(act):
            act.wait_ge(s_in, 32)
            nc.scalar.activation(sg[:, :], c9[:, :], ACT.Sigmoid).then_inc(s_sig, 1)
            act.sem_inc(rep_free, 2)
            with act.Fori(0, turns) as i:
                for s in range(2):
                    act.wait_ge(s_mod, i * 2 + s + 1)
                    nc.scalar.copy(modsb[s][:, :], p_mod[s][:, :]).then_inc(s_modsb, 1)
                for s in range(2):
                    act.wait_ge(s_rep, i * 2 + s + 1)
                    act.wait_ge(rep_free, i * 2 + s + 1)
                    nc.scalar.copy(rep[s][:, :], p_rep[s][:, :]).then_inc(s_repsb, 1)
                    nc.scalar.copy(reps[s][:, :], p_reps[s][:, :]).then_inc(s_repsb, 1)

        @block.vector
        def _(dve):
            dve.wait_ge(s_sig, 1)
            nc.vector.tensor_tensor(c9[:, :], c9[:, :], sg[:, :], ALU.mult).then_inc(s_act, 1)
            dve.wait_ge(s_tr, 1)
            nc.vector.tensor_copy(ct[:, :, :], p_tr[:, :, 0:9]).then_inc(s_ct, 1)

        @block.gpsimd
        def _(pool):
            with pool.Fori(0, turns) as i:
                for s in range(2):
                    col = (i * 2 + s) * CW
                    pool.wait_ge(s_repsb, (i * 2 + s) * 2 + 2)
                    pool.dma_start(t["modrep"][0:P, bass.ds(col, CW)], rep[s][:, :]).then_inc(s_stored, 16)
                    pool.dma_start(t["modrep"][P:P + NS, bass.ds(col, CW)], reps[s][:, :]).then_inc(s_stored, 16)
                    pool.wait_ge(s_stored, (i * 2 + s) * 32 + 32)
                    pool.sem_inc(rep_free, 1)


def norm_modulate(pr, tag, prompt_src, sample_src, gain, scale_ix, shift_ix, ht, keep=None):
    nc, t = pr.nc, pr.t
    x_in = [pr.sem(f"{tag}_xin{s}") for s in range(2)]
    (mod_in, gmod, sq, ms, ln, rstd, scaled, h_ready, turned, ht_done, kept, h_free) = (
        pr.sem(f"{tag}_{n}") for n in ("modin", "gmod", "sq", "ms", "ln", "rstd", "scaled", "hready",
                                       "turned", "htdone", "kept", "hfree"))
    nstep = pr.sem(f"{tag}_newton")
    with ExitStack() as cx:
        sb = lambda name, shape: cx.enter_context(nc.sbuf_tensor(f"{tag}_{name}", shape, F32))
        x = [sb(f"x{s}", [P, D]) for s in range(2)]
        h = [sb(f"h{s}", [P, D]) for s in range(2)]
        junk = sb("junk", [P, D])
        g_b = sb("g", [P, D])
        scl, shf = [sb(f"scl{r}", [P, D]) for r in range(2)], [sb(f"shf{r}", [P, D]) for r in range(2)]
        st = [sb(f"st{s}", [P, 6]) for s in range(2)]
        p_t = [cx.enter_context(nc.psum_tensor(f"{tag}_pt{s}", [P, KD, P], F32)) for s in range(2)]
        block = cx.enter_context(nc.Block(tag))

        @block.sync
        def _(sp):
            sp.dma_start(g_b[:, :], gain.partition_broadcast(P)).then_inc(mod_in, 16)
            for r, (a, n) in enumerate(((0, P), (P, NS))):
                for buf, ix in ((scl, scale_ix), (shf, shift_ix)):
                    sp.dma_start(buf[r][0:n, :], t["modrep"][a:a + n, ix * D:(ix + 1) * D]).then_inc(mod_in, 16)

            def load(n, s):
                sp.dma_start(x[s][:, :], prompt_src[bass.ds(n * P, P), :]).then_inc(x_in[s], 16)

            for s in range(2):
                load(s, s)
            with sp.Fori(1, PT // 2) as i:
                for s in range(2):
                    sp.wait_ge(scaled, i * 2 + s - 1)
                    load(i * 2 + s, s)
            sp.wait_ge(scaled, PT - 1)
            sp.dma_start(x[0][0:NS, :], sample_src).then_inc(x_in[0], 16)

        @block.scalar
        def _(act):
            def squares(n, s, turn, rows):
                act.wait_ge(x_in[s], turn * 16 + 16)
                nc.scalar.activation(junk[0:rows, :], x[s][0:rows, :], ACT.Square,
                                     accum_out=st[s][0:rows, 0:1]).then_inc(sq, 1)
                act.wait_ge(sq, n + 1)

            def root(n, s, rows):
                act.wait_ge(ms, n + 1)
                nc.scalar.activation(st[s][0:rows, 2:3], st[s][0:rows, 1:2], ACT.Ln).then_inc(ln, 1)
                act.wait_ge(ln, n + 1)
                nc.scalar.activation(st[s][0:rows, 3:4], st[s][0:rows, 2:3], ACT.Exp, scale=-0.5).then_inc(rstd, 1)

            def evacuate(n, s, rows):
                act.wait_ge(turned, n + 3)
                nc.scalar.copy(ht[:, :, bass.ds(n * P, rows)], p_t[s][:, :, 0:rows]).then_inc(ht_done, 1)

            act.sem_inc(ht_done, 2)
            with act.Fori(0, PT // 2) as i:
                for s in range(2):
                    squares(i * 2 + s, s, i, P)
                for s in range(2):
                    root(i * 2 + s, s, P)
                for s in range(2):
                    evacuate(i * 2 + s, s, P)
            squares(PT, 0, PT // 2, NS)
            root(PT, 0, NS)
            evacuate(PT, 0, NS)

        @block.vector
        def _(dve):
            dve.wait_ge(mod_in, 16 * 5)
            for r, n in ((0, P), (1, NS)):
                nc.vector.scalar_tensor_tensor(scl[r][0:n, :], scl[r][0:n, :], 1.0, g_b[0:n, :],
                                               ALU.add, ALU.mult).then_inc(gmod, 1)
            dve.wait_ge(gmod, 2)

            def mean(n, s, rows):
                dve.wait_ge(sq, n + 1)
                nc.vector.tensor_scalar(st[s][0:rows, 1:2], st[s][0:rows, 0:1], 1.0 / D, EPS,
                                        ALU.mult, ALU.add).then_inc(ms, 1)

            def modulate(n, s, rows, r):
                dve.wait_ge(rstd, n + 1)
                newton = Ordered(dve, nstep)
                newton.turn(n, 3, 0)
                y, f = st[s][0:rows, 3:4], st[s][0:rows, 4:5]
                newton(nc.vector.scalar_tensor_tensor(f, y, st[s][0:rows, 1:2], y, ALU.mult, ALU.mult))
                newton(nc.vector.tensor_scalar(f, f, -0.5, 1.5, ALU.mult, ALU.add))
                newton(nc.vector.tensor_tensor(st[s][0:rows, 5:6], y, f, ALU.mult))
                dve.wait_ge(turned, n + 1)
                if keep is not None:
                    dve.wait_ge(h_free, n + 1)
                nc.vector.scalar_tensor_tensor(h[s][0:rows, :], x[s][0:rows, :], st[s][0:rows, 5:6], scl[r][0:rows, :],
                                               ALU.mult, ALU.mult).then_inc(scaled, 1)
                dve.wait_ge(scaled, n + 1)
                nc.vector.tensor_tensor(h[s][0:rows, :], h[s][0:rows, :], shf[r][0:rows, :], ALU.add).then_inc(h_ready, 1)

            with dve.Fori(0, PT // 2) as i:
                for s in range(2):
                    mean(i * 2 + s, s, P)
                for s in range(2):
                    modulate(i * 2 + s, s, P, 0)
            mean(PT, 0, NS)
            modulate(PT, 0, NS, 1)

        @block.tensor
        def _(pe):
            pe.sem_inc(turned, 2)

            def turn(n, s, rows):
                pe.wait_ge(h_ready, n + 1)
                pe.wait_ge(ht_done, n + 1)
                for k in range(KD):
                    tr = nc.tensor.transpose(p_t[s][:, k, 0:rows], h[s][0:rows, k * P:(k + 1) * P],
                                             pr.c("ident")[0:rows, 0:rows])
                tr.then_inc(turned, 1)

            with pe.Fori(0, PT // 2) as i:
                for s in range(2):
                    turn(i * 2 + s, s, P)
            turn(PT, 0, NS)

        if keep is not None:
            @block.gpsimd
            def _(pool):
                pool.sem_inc(h_free, 2)

                def store(n, s, rows):
                    pool.wait_ge(h_ready, n + 1)
                    pool.dma_start(keep[bass.ds(n * P, rows), :], h[s][0:rows, :]).then_inc(kept, 16)
                    pool.wait_ge(kept, n * 16 + 16)
                    pool.sem_inc(h_free, 1)

                with pool.Fori(0, PT // 2) as i:
                    for s in range(2):
                        store(i * 2 + s, s, P)
                store(PT, 0, NS)


def copy_windows(pr, eng, copied):
    t, n = pr.t, 0
    flat = lambda x: x.rearrange("b w h d -> b w (h d)")
    for g, (w, _) in enumerate(GROUPS):
        for name, col in (("k", C_K), ("v", C_V)):
            cols = slice(col + g * GW, col + (g + 1) * GW)
            dst = flat(t[f"{name}{g}_s"][0])
            for out, src in (
                    (flat(t[f"{name}{g}_p"][0])[0], t["proj_n"][SEQ - w:SEQ, cols]),
                    (dst[:, 0:w - NT], flat(t[f"cache_{name}{g}"][0])[:, NT:]),
                    (dst[:, w - NT:], t["proj_n"][SEQ:TOK, cols].rearrange("(b t) c -> b t c", t=NT))):
                eng.dma_start(out, src).then_inc(copied, 16)
                n += 16
    return n


def project_features(pr, tag, ht, w_v, col0, cols, dst, row0, cw, windows=False):
    nc = pr.nc
    ct, turns = cw // P, cols // cw // 2
    assert turns * 2 * cw == cols
    w_in = [pr.sem(f"{tag}_win{s}") for s in range(2)]
    product, evacuated, stored, st_free, copied = (pr.sem(f"{tag}_{n}") for n in (
        "product", "evac", "stored", "stfree", "copied"))
    with ExitStack() as cx:
        w = [cx.enter_context(nc.sbuf_tensor(f"{tag}_w{s}", [P, KD, cw], F32)) for s in range(2)]
        st = [cx.enter_context(nc.sbuf_tensor(f"{tag}_st{s}", [P, TOK], F32)) for s in range(2)]
        ps = [cx.enter_context(nc.psum_tensor(f"{tag}_ps{s}", [P, 3 * 512], F32)) for s in range(2)]
        block = cx.enter_context(nc.Block(tag))

        @block.sync
        def _(sp):
            def load(c, s):
                sp.dma_start(w[s][:, :, :], w_v[:, :, bass.ds(c * cw + col0, cw)]).then_inc(w_in[s], 16)

            for s in range(2):
                load(s, s)
            n = copy_windows(pr, sp, copied) if windows else 0
            with sp.Fori(1, turns) as i:
                for s in range(2):
                    sp.wait_ge(product, (i * 2 + s - 1) * ct)
                    load(i * 2 + s, s)
            if windows:
                sp.wait_ge(copied, n)

        @block.tensor
        def _(pe):
            with pe.Fori(0, turns) as i:
                for s in range(2):
                    pe.wait_ge(w_in[s], i * 16 + 16)
                    for j in range(ct):
                        n, b = (i * 2 + s) * ct + j, (s * ct + j) % 2
                        pe.wait_ge(evacuated, n + 1)
                        for k in range(KD):
                            for a in range(0, TOK, 512):
                                e = min(a + 512, TOK)
                                mm = nc.tensor.matmul(ps[b][:, a:e], w[s][:, k, j * P:(j + 1) * P], ht[:, k, a:e],
                                                      start=(k == 0), stop=(k == KD - 1))
                        mm.then_inc(product, 1)

        @block.scalar
        def _(act):
            act.sem_inc(evacuated, 2)
            with act.Fori(0, turns) as i:
                for m in range(2 * ct):
                    n = i * 2 * ct + m
                    act.wait_ge(product, n + 1)
                    act.wait_ge(st_free, n + 1)
                    nc.scalar.copy(st[m % 2][:, :], ps[m % 2][:, 0:TOK]).then_inc(evacuated, 1)

        @block.gpsimd
        def _(pool):
            pool.sem_inc(st_free, 2)
            with pool.Fori(0, turns) as i:
                for m in range(2 * ct):
                    n = i * 2 * ct + m
                    pool.wait_ge(evacuated, n + 3)
                    pool.dma_start(dst[bass.ds(n * P + row0, P), :], st[m % 2][:, :]).then_inc(stored, 16)
                    pool.wait_ge(stored, n * 16 + 16)
                    pool.sem_inc(st_free, 1)


def project_tokens(pr, ht, w_v):
    nc, t = pr.nc, pr.t
    cw = 416
    turns = NATC // cw // 2
    assert turns * 2 * cw == NATC
    tiles = PT + 1
    banks = 6
    w_in = [pr.sem(f"pn_win{s}") for s in range(2)]
    product, evacuated, stored, st_free = (pr.sem(f"pn_{n}") for n in ("product", "evac", "stored", "stfree"))
    with ExitStack() as cx:
        w = [cx.enter_context(nc.sbuf_tensor(f"pn_w{s}", [P, KD, cw], F32)) for s in range(2)]
        st = [cx.enter_context(nc.sbuf_tensor(f"pn_st{s}", [P, tiles, cw], F32)) for s in range(2)]
        ps = cx.enter_context(nc.psum_tensor("pn_ps", [P, banks, 512], F32))
        block = cx.enter_context(nc.Block("project_tokens"))

        @block.sync
        def _(sp):
            def load(c, s):
                sp.dma_start(w[s][:, :, :], w_v[:, :, bass.ds(c * cw, cw)]).then_inc(w_in[s], 16)

            for s in range(2):
                load(s, s)
            with sp.Fori(1, turns) as i:
                for s in range(2):
                    sp.wait_ge(product, (i * 2 + s - 1) * tiles)
                    load(i * 2 + s, s)

        @block.tensor
        def _(pe):
            with pe.Fori(0, turns) as i:
                for s in range(2):
                    pe.wait_ge(w_in[s], i * 16 + 16)
                    for m in range(tiles):
                        rows = P if m < PT else NS
                        b = (s * tiles + m) % banks
                        pe.wait_ge(evacuated, (i * 2 + s) * tiles + m + 1)
                        for k in range(KD):
                            mm = nc.tensor.matmul(ps[0:rows, b, 0:cw], ht[:, k, m * P:m * P + rows], w[s][:, k, :],
                                                  start=(k == 0), stop=(k == KD - 1))
                        mm.then_inc(product, 1)

        @block.vector
        def _(dve):
            dve.sem_inc(evacuated, banks)
            with dve.Fori(0, turns) as i:
                for s in range(2):
                    dve.wait_ge(st_free, i * 2 + s + 1)
                    for m in range(tiles):
                        rows = P if m < PT else NS
                        dve.wait_ge(product, (i * 2 + s) * tiles + m + 1)
                        nc.vector.tensor_copy(st[s][0:rows, m, :], ps[0:rows, (s * tiles + m) % banks, 0:cw])\
                            .then_inc(evacuated, 1)

        @block.gpsimd
        def _(pool):
            pool.sem_inc(st_free, 2)
            with pool.Fori(0, turns) as i:
                for s in range(2):
                    c = i * 2 + s
                    pool.wait_ge(evacuated, (c + 1) * tiles + banks)
                    cols = bass.ds(c * cw, cw)
                    pool.dma_start(t["proj_n"][0:SEQ, cols].rearrange("(m p) c -> p m c", p=P),
                                   st[s][:, 0:PT, :]).then_inc(stored, 16)
                    pool.dma_start(t["proj_n"][SEQ:TOK, cols], st[s][0:NS, PT, :]).then_inc(stored, 16)
                    pool.wait_ge(stored, c * 32 + 32)
                    pool.sem_inc(st_free, 1)


def mixer_input(pr):
    nc, t = pr.nc, pr.t
    w_v = t["w_in"][0].rearrange("(k p) n -> p k n", p=P)
    with nc.sbuf_tensor("ht1", [P, KD, TOK], F32) as ht:
        norm_modulate(pr, "n1", t["x_prompt"][0], t["x_sample"].rearrange("b t d -> (b t) d"), t["norm1_g"][0],
                      1, 0, ht)
        project_tokens(pr, ht, w_v)
        project_features(pr, "pt", ht, w_v, C_ZQ, TRC, t["proj_t"], 0, 3 * P, windows=True)


def retrieval_queries(pr):
    nc, t = pr.nc, pr.t
    with nc.sbuf_tensor("ht2", [P, KD, TOK], F32) as ht:
        norm_modulate(pr, "n2", t["x1"][0:SEQ, :], t["x1"][SEQ:TOK, :], t["norm2_g"][0], 4, 3, ht, keep=t["h2"])
        project_features(pr, "pq", ht, t["peer_wq"][0].rearrange("(k p) n -> p k n", p=P), 0,
                         2 * HEADS * DHALF, t["qry_t"], 0, 2 * P)


def attention_prompt(pr):
    nc, t = pr.nc, pr.t
    BLK, RING = 8, 4
    (tr, qkt, scored, t_done, mstep, m_ready, exp_done, p_turned, pt_ready, pv_done, ml_done, o_done,
     stored, rec_free, zeroed) = (pr.sem(f"ap_{n}") for n in (
         "tr", "qkt", "scored", "tdone", "mstep", "mready", "exp", "pturned", "ptready", "pv", "ml", "o",
         "stored", "recfree", "zeroed"))
    qkv_in = [pr.sem(f"ap_in{s}") for s in range(RING)]
    src = t["proj_n"][0:SEQ, 0:3 * AW].rearrange("s (j g c) -> s j g c", j=3, g=3)

    def rows_of(view, g, i, b):
        if g == 0:
            return [(0, P, view[bass.ds(i * (RING * P) + b * P, P)])]
        if g == 1:
            v = view.rearrange("(n p r) a b -> n r p a b", p=P, r=4)
            return [(0, P, v[b % 2, i * 2 + b // 2])]
        v = view.rearrange("(u r) a b -> r u a b", r=16)
        return [(64 * e, 64 * e + 64, v[i * 8 + 2 * b + e]) for e in range(2)]

    def bank_of(h):
        return h % 2 * 2 + h // 2

    def has_prev(g, b):
        return g == 0 or (g == 1 and b % 2 == 1)

    with ExitStack() as cx:
        sb = lambda name, shape: cx.enter_context(nc.sbuf_tensor(f"ap_{name}", shape, F32))
        ps = lambda name, shape: cx.enter_context(nc.psum_tensor(f"ap_{name}", shape, F32))
        qkv = [sb(f"qkv{s}", [P, 3, GW]) for s in range(RING)]
        qk_t = [sb(f"qkt{s}", [P, 4, P]) for s in range(RING)]
        sc = [sb(f"sc{s}", [P, HPG, 2 * P]) for s in range(2)]
        pr_ = [sb(f"p{s}", [P, HPG, 2 * P]) for s in range(2)]
        p_t = [sb(f"pt{s}", [P, 2 * HPG, P]) for s in range(2)]
        m8 = [sb(f"m8{s}", [P, HPG]) for s in range(2)]
        nb = [sb(f"nb{s}", [P, HPG]) for s in range(2)]
        den = [sb(f"den{s}", [P, HPG]) for s in range(2)]
        rec = [sb(f"rec{s}", [P, HPG, REC]) for s in range(2)]
        ps_tr = ps("ps_tr", [P, 4, P])
        ps_s = ps("ps_s", [P, HPG, 2 * P])
        ps_pt = ps("ps_pt", [P, 2 * HPG, P])
        ps_o = [ps(f"ps_o{s}", [P, HPG, DH]) for s in range(2)]
        block = cx.enter_context(nc.Block("attention_prompt"))

        def turns(eng, body):
            for g in range(3):
                with eng.Fori(0, BLK // RING) as i:
                    body(g, i, i * RING + BLK * g)

        @block.sync
        def _(sp):
            def body(g, i, n0):
                for b in range(RING):
                    sp.wait_ge(pv_done, n0 + b + 1)
                    for a, e, rows in rows_of(src[:, :, g, :], g, i, b):
                        sp.dma_start(qkv[b][a:e, :, :], rows).then_inc(qkv_in[b], 16)

            sp.wait_ge(zeroed, 2)
            turns(sp, body)

        @block.tensor
        def _(pe):
            def front(g, i, n0, b):
                n = n0 + b
                each = 16 if g < 2 else 32
                pe.wait_ge(qkv_in[b], i * each + each + 32 * g)
                pe.wait_ge(qkt, n + 1)
                for j in range(4):
                    mm = nc.tensor.transpose(ps_tr[:, j, :], qkv[b][:, j // 2, (j % 2) * P:(j % 2 + 1) * P],
                                             pr.c("ident"))
                mm.then_inc(tr, 1)
                pe.wait_ge(qkt, n + 2)
                pe.wait_ge(t_done, n + 1)
                for h in range(HPG):
                    a, hp = 64 * (h % 2), h // 2
                    for kb in range(0 if has_prev(g, b) else 1, 2):
                        keys = qk_t[b if kb else (b - 1) % RING]
                        mm = nc.tensor.matmul(ps_s[:, bank_of(h), kb * P:(kb + 1) * P], qk_t[b][a:a + 64, hp, :],
                                              keys[a:a + 64, 2 + hp, :], start=True, stop=True)
                mm.then_inc(scored, 1)

            def back(g, i, n0, b):
                n, s = n0 + b, b % 2
                kbs = range(0 if has_prev(g, b) else 1, 2)
                pe.wait_ge(exp_done, n + 3)
                pe.wait_ge(pt_ready, n + 1)
                for h in range(HPG):
                    for kb in kbs:
                        mm = nc.tensor.transpose(ps_pt[:, 2 * h + kb, :], pr_[s][:, h, kb * P:(kb + 1) * P],
                                                 pr.c("ident"))
                mm.then_inc(p_turned, 1)
                pe.wait_ge(pt_ready, n + 2)
                pe.wait_ge(o_done, n + 1)
                for h in range(HPG):
                    for kb in kbs:
                        values = qkv[b if kb else (b - 1) % RING][:, 2, h * DH:(h + 1) * DH]
                        mm = nc.tensor.matmul(ps_o[s][:, h, :], p_t[s][:, 2 * h + kb, :], values,
                                              start=(kb == kbs[0]), stop=(kb == 1))
                mm.then_inc(pv_done, 1)

            def body(g, i, n0):
                front(g, i, n0, 0)
                for b in range(1, RING):
                    front(g, i, n0, b)
                    back(g, i, n0, b - 1)
                back(g, i, n0, RING - 1)

            pe.sem_inc(scored, 3)
            pe.sem_inc(p_turned, 2)
            pe.sem_inc(pv_done, 3)
            turns(pe, body)

        @block.scalar
        def _(act):
            def turned(g, i, n0, b):
                n = n0 + b
                act.wait_ge(tr, n + 1)
                act.wait_ge(scored, n + 1)
                nc.scalar.copy(qk_t[b][:, :, :], ps_tr[:, :, :]).then_inc(qkt, 1)

            def exps(g, i, n0, b):
                n, s = n0 + b, b % 2
                k0 = 0 if has_prev(g, b) else P
                act.wait_ge(m_ready, n + 1)
                act.wait_ge(p_turned, n + 1)
                act.wait_ge(ml_done, n + 1)
                for h in range(HPG):
                    ex = nc.scalar.activation(pr_[s][:, h, k0:], sc[s][:, h, k0:], ACT.Exp, bias=nb[s][:, h:h + 1],
                                              scale=0.125, accum_out=den[s][:, h:h + 1])
                ex.then_inc(exp_done, 1)

            def outputs(g, i, n0, b):
                n, s = n0 + b, b % 2
                act.wait_ge(pv_done, n + 4)
                act.wait_ge(rec_free, n + 1)
                nc.scalar.copy(rec[s][:, :, 0:DH], ps_o[s][:, :, :]).then_inc(o_done, 1)

            def body(g, i, n0):
                turned(g, i, n0, 0)
                for b in range(1, RING):
                    turned(g, i, n0, b)
                    exps(g, i, n0, b - 1)
                    if b > 1:
                        outputs(g, i, n0, b - 2)
                exps(g, i, n0, RING - 1)
                outputs(g, i, n0, RING - 2)
                outputs(g, i, n0, RING - 1)

            act.sem_inc(qkt, 1)
            act.sem_inc(exp_done, 2)
            act.sem_inc(o_done, 2)
            turns(act, body)

        @block.vector
        def _(dve):
            def maxima(g, i, n0, b):
                n, s = n0 + b, b % 2
                k0 = 0 if has_prev(g, b) else P
                if g == 0 and b == 0:
                    a = AT["pen0"][0]
                    pen = pr.const[:, bass.ds(i * (2 * P) + a, 2 * P)]
                else:
                    pen = pr.c(f"pen{g}")[:, -2 * P:] if g < 2 else pr.c("pen2")
                    pen = pen[:, k0:] if g < 2 else pen
                dve.wait_ge(scored, n + 4)
                dve.wait_ge(exp_done, n + 1)
                for h in range(HPG):
                    st = nc.vector.scalar_tensor_tensor(sc[s][:, h, k0:], pen, 8.0 * SLOPES[4 * g + h],
                                                        ps_s[:, bank_of(h), k0:], ALU.mult, ALU.add)
                st.then_inc(t_done, 1)
                dve.wait_ge(t_done, n + 2)
                nc.vector.tensor_reduce(m8[s][:, :], sc[s][:, :, k0:], AX, ALU.max).then_inc(mstep, 1)
                dve.wait_ge(mstep, n + 1)
                nc.vector.tensor_scalar(nb[s][:, :], m8[s][:, :], -0.125, None, ALU.mult).then_inc(m_ready, 1)

            def probs(g, i, n0, b):
                n, s = n0 + b, b % 2
                dve.wait_ge(p_turned, n + 3)
                dve.wait_ge(pv_done, n + 2)
                if has_prev(g, b):
                    cp = nc.vector.tensor_copy(p_t[s][:, :, :], ps_pt[:, :, :])
                else:
                    half = lambda x: x.rearrange("p (h k) q -> p h k q", k=2)[:, :, 1, :]
                    cp = nc.vector.tensor_copy(half(p_t[s][:, :, :]), half(ps_pt[:, :, :]))
                cp.then_inc(pt_ready, 1)
                dve.wait_ge(rec_free, n + 1)
                nc.vector.tensor_copy(rec[s][:, :, DH], m8[s][:, :])
                nc.vector.tensor_copy(rec[s][:, :, DH + 1], den[s][:, :]).then_inc(ml_done, 1)

            def body(g, i, n0):
                maxima(g, i, n0, 0)
                for b in range(1, RING):
                    maxima(g, i, n0, b)
                    probs(g, i, n0, b - 1)
                probs(g, i, n0, RING - 1)

            nc.vector.memset(qkv[RING - 1][:, :, :], 0.0).then_inc(zeroed, 1)
            nc.vector.memset(qk_t[RING - 1][:, :, :], 0.0).then_inc(zeroed, 1)
            dve.sem_inc(t_done, 1)
            dve.sem_inc(pt_ready, 1)
            dve.sem_inc(ml_done, 2)
            turns(dve, body)

        @block.gpsimd
        def _(pool):
            def body(g, i, n0):
                for b in range(RING):
                    n, s = n0 + b, b % 2
                    pool.wait_ge(o_done, n + 3)
                    pool.wait_ge(ml_done, n + 3)
                    for a, e, rows in rows_of(t["att_rec"][g, 0:SEQ].rearrange("s (h c) -> s h c", h=HPG), g, i, b):
                        pool.dma_start(rows, rec[s][a:e, :, :]).then_inc(stored, 16)
                    pool.wait_ge(stored, stores(g, i, b))
                    pool.sem_inc(rec_free, 1)

            def stores(g, i, b):
                each = 16 if g < 2 else 32
                return i * (RING * each) + (b + 1) * each + BLK * 16 * g

            pool.sem_inc(rec_free, 2)
            turns(pool, body)


def attention_merge(pr):
    nc, t = pr.nc, pr.t
    (top, diff, w_done, den, rden, wn, prod, att, turned, evac, stored, tfree) = (pr.sem(f"am_{n}") for n in (
        "top", "diff", "w", "den", "rden", "wn", "prod", "att", "turned", "evac", "stored", "tfree"))
    wl_done = pr.sem("am_wl")
    rec_in = [pr.sem(f"am_in{s}") for s in range(2)]
    with ExitStack() as cx:
        sb = lambda name, shape: [cx.enter_context(nc.sbuf_tensor(f"am_{name}{s}", shape, F32)) for s in range(2)]
        rec = sb("rec", [P, 3, HPG, REC])
        mx, de, re = sb("mx", [P, HPG]), sb("de", [P, HPG]), sb("re", [P, HPG])
        w, wl = sb("w", [P, 3, HPG]), sb("wl", [P, 3, HPG])
        o3, at, at_t = sb("o3", [P, 3, HPG, DH]), sb("at", [P, GW]), sb("att", [P, 2, P])
        ps = [cx.enter_context(nc.psum_tensor(f"am_ps{s}", [P, 2, P], F32)) for s in range(2)]
        block = cx.enter_context(nc.Block("attention_merge"))
        src = t["att_rec"].rearrange("g t c -> t g c")
        dst = t["att_t"].rearrange("(k p) t -> p k t", p=P)

        def tiles(eng, tile):
            with eng.Fori(0, PT // 2) as i:
                for s in range(2):
                    tile(i * 2 + s, s, i, P)
            tile(PT, 0, PT // 2, NS)

        @block.sync
        def _(sp):
            def load(n, s, i, rows):
                sp.wait_ge(prod, n + 1)
                sp.dma_start(rec[s][0:rows, :, :, :].rearrange("p g h c -> p g (h c)"),
                             src[bass.ds(n * P, rows)]).then_inc(rec_in[s], 16)
            tiles(sp, load)

        @block.vector
        def _(dve):
            def tile(n, s, i, rows):
                r = slice(0, rows)
                m = rec[s][r, :, :, DH]
                over_g = lambda x: x.unsqueeze(1).broadcast_to([rows, 3, HPG])
                dve.wait_ge(rec_in[s], i * 16 + 16)
                nc.vector.tensor_reduce(mx[s][r, :], m.rearrange("p g h -> p h g"), AX, ALU.max).then_inc(top, 1)
                dve.wait_ge(top, n + 1)
                nc.vector.tensor_tensor(w[s][r], m, over_g(mx[s][r, :]), ALU.subtract).then_inc(diff, 1)
                dve.wait_ge(w_done, n + 1)
                nc.vector.tensor_tensor(wl[s][r], w[s][r], rec[s][r, :, :, DH + 1], ALU.mult).then_inc(wl_done, 1)
                dve.wait_ge(wl_done, n + 1)
                nc.vector.tensor_reduce(de[s][r, :], wl[s][r].rearrange("p g h -> p h g"), AX, ALU.add).then_inc(den, 1)
                dve.wait_ge(den, n + 1)
                nc.vector.reciprocal(re[s][r, :], de[s][r, :]).then_inc(rden, 1)
                dve.wait_ge(rden, n + 1)
                nc.vector.tensor_tensor(wl[s][r], w[s][r], over_g(re[s][r, :]), ALU.mult).then_inc(wn, 1)
                dve.wait_ge(wn, n + 1)
                nc.vector.tensor_tensor(o3[s][r], rec[s][r, :, :, 0:DH],
                                        wl[s][r].unsqueeze(3).broadcast_to([rows, 3, HPG, DH]), ALU.mult)\
                    .then_inc(prod, 1)
                dve.wait_ge(prod, n + 3)
                dve.wait_ge(turned, n + 1)
                nc.vector.tensor_reduce(at[s][r, :], o3[s][r].rearrange("p g h c -> p (h c) g"), AX, ALU.add)\
                    .then_inc(att, 1)

            dve.sem_inc(prod, 2)
            tiles(dve, tile)

        @block.scalar
        def _(act):
            def tile(n, s, i, rows):
                act.wait_ge(diff, n + 1)
                nc.scalar.activation(w[s][0:rows], w[s][0:rows], ACT.Exp, scale=0.125).then_inc(w_done, 1)
                act.wait_ge(turned, n + 3)
                act.wait_ge(tfree, n + 1)
                nc.scalar.copy(at_t[s][:, :, 0:rows], ps[s][:, :, 0:rows]).then_inc(evac, 1)

            act.sem_inc(evac, 2)
            tiles(act, tile)

        @block.tensor
        def _(pe):
            def tile(n, s, i, rows):
                pe.wait_ge(att, n + 1)
                pe.wait_ge(evac, n + 1)
                for k in range(2):
                    tr = nc.tensor.transpose(ps[s][:, k, 0:rows], at[s][0:rows, k * P:(k + 1) * P],
                                             pr.c("ident")[0:rows, 0:rows])
                tr.then_inc(turned, 1)

            pe.sem_inc(turned, 2)
            tiles(pe, tile)

        @block.gpsimd
        def _(pool):
            def tile(n, s, i, rows):
                pool.wait_ge(evac, n + 3)
                pool.dma_start(dst[:, :, bass.ds(n * P, rows)], at_t[s][:, :, 0:rows]).then_inc(stored, 16)
                pool.wait_ge(stored, n * 16 + 16)
                pool.sem_inc(tfree, 1)

            pool.sem_inc(tfree, 2)
            tiles(pool, tile)


def attention_sample(pr):
    nc, t = pr.nc, pr.t
    loaded, zeroed, new_tr, new_t, stored = (pr.sem(f"as_{n}") for n in ("loaded", "zeroed", "newtr", "newt", "stored"))
    (qbd_done, ktr, kt_done, scored, t_done, mstep, m_ready, exp_done, p_turned, pt_ready, pv_done, picked,
     rec_done, rec_free) = (pr.sem(f"as_{n}") for n in (
         "qbd", "ktr", "kt", "scored", "tdone", "mstep", "mready", "exp", "pturned", "ptready", "pv", "picked",
         "rec", "recfree"))
    kv_in = [pr.sem(f"as_in{g}") for g in range(3)]
    NKB = (1, 4, 4)
    penw = sum(W_S)
    with ExitStack() as cx:
        sb = lambda name, shape: cx.enter_context(nc.sbuf_tensor(f"as_{name}", shape, F32))
        ps = lambda name, shape: cx.enter_context(nc.psum_tensor(f"as_{name}", shape, F32))
        new = sb("new", [P, 3, 3, GW])
        new_tt = sb("newt", [P, 2, 3, 2, NS])
        kc = [sb(f"k{g}", [P, 4, NKB[g] * GW]) for g in range(3)]
        vc = [sb(f"v{g}", [P, 4, NKB[g] * GW]) for g in range(3)]
        qbd = [sb(f"qbd{g}", [P, 2, 4, HPG, NT]) for g in range(3)]
        k_t = [sb(f"kt{s}", [P, 2, 512]) for s in range(2)]
        sc, prob = sb("sc", [P, 576]), sb("prob", [P, 640])
        p_t = sb("pt", [P, 5, P])
        m8, nb, den = sb("m8", [P, 1]), sb("nb", [P, 1]), sb("den", [P, 1])
        pick, rec = sb("pick", [P, HPG, DH]), sb("rec", [P, REC])
        ps_k = ps("ps_k", [P, 2, 512])
        ps_s, ps_n = ps("ps_s", [P, 512]), ps("ps_n", [P, 512])
        ps_pt, ps_o = ps("ps_pt", [P, 5, P]), ps("ps_o", [P, GW])
        block = cx.enter_context(nc.Block("attention_sample"))

        @block.sync
        def _(sp):
            sp.dma_start(new[0:NS], t["proj_n"][SEQ:TOK, 0:3 * AW].rearrange("s (j g c) -> s j g c", j=3, g=3))\
                .then_inc(loaded, 16)
            with sp.Fori(0, 2) as i:
                for g in range(3):
                    sp.wait_ge(pv_done, i * 3 + g + 1)
                    for buf, name in ((kc, "k"), (vc, "v")):
                        src = t[f"cache_{name}{g}"][0].rearrange("b w h d -> b w (h d)")[bass.ds(i * 4, 4)]
                        if g == 0:
                            sp.dma_start(buf[g][:, :, :], src.rearrange("b p c -> p b c")).then_inc(kv_in[g], 16)
                        elif g == 1:
                            sp.dma_start(buf[g][:, :, :], src.rearrange("b (p k) c -> p b (k c)", p=P)).then_inc(kv_in[g], 16)
                        else:
                            v = src.rearrange("b (u r) c -> u b (r c)", r=16)
                            for e in range(2):
                                sp.dma_start(buf[g][64 * e:64 * e + 64, :, :],
                                             v[:, :, e * 4 * GW:(e + 1) * 4 * GW]).then_inc(kv_in[g], 16)

        @block.tensor
        def _(pe):
            pe.wait_ge(loaded, 16)
            for g in range(3):
                for j in range(4):
                    mm = nc.tensor.transpose(ps_k[:, 0, j * NS:(j + 1) * NS],
                                             new[0:NS, j // 2, g, (j % 2) * P:(j % 2 + 1) * P], pr.c("ident")[0:NS, 0:NS])
                mm.then_inc(new_tr, 1)
                pe.wait_ge(new_t, g + 1)
            pe.sem_inc(pv_done, 3)
            pe.sem_inc(scored, 2)
            with pe.Fori(0, 2) as i:
                for g in range(3):
                    n, nk, w = i * 3 + g, NKB[g], NKB[g] * P
                    pe.wait_ge(kv_in[g], i * (64 if g == 2 else 32) + (64 if g == 2 else 32))
                    pe.wait_ge(qbd_done, n + 1)
                    pe.wait_ge(t_done, n + 1)
                    for b in range(4):
                        q = n * 4 + b
                        pe.wait_ge(kt_done, q + 1)
                        for hp in range(2):
                            for kb in range(nk):
                                a = kb * GW + hp * P
                                mm = nc.tensor.transpose(ps_k[:, hp, kb * P:(kb + 1) * P], kc[g][:, b, a:a + P],
                                                         pr.c("ident"))
                        mm.then_inc(ktr, 1)
                        pe.wait_ge(kt_done, q + 2)
                        rows = slice(32 * b, 32 * b + 32)
                        for hp in range(2):
                            lhs = qbd[g][:, hp, b].rearrange("p h t -> p (h t)")
                            nc.tensor.matmul(ps_s[rows, 0:w], lhs, k_t[b % 2][:, hp, 0:w], start=(hp == 0), stop=(hp == 1))
                        for hp in range(2):
                            lhs = qbd[g][:, hp, b].rearrange("p h t -> p (h t)")
                            mm = nc.tensor.matmul(ps_n[rows, 0:NS], lhs, new_tt[:, 1, g, hp, :], start=(hp == 0), stop=(hp == 1))
                        mm.then_inc(scored, 1)
                    pe.wait_ge(exp_done, n + 1)
                    pe.wait_ge(pt_ready, n + 1)
                    for kb in range(nk + 1):
                        mm = nc.tensor.transpose(ps_pt[:, kb, :], prob[:, kb * P:(kb + 1) * P], pr.c("ident"))
                    mm.then_inc(p_turned, 1)
                    pe.wait_ge(pt_ready, n + 2)
                    pe.wait_ge(picked, n + 1)
                    for b in range(4):
                        rows = slice(32 * b, 32 * b + 32)
                        for kb in range(nk + 1):
                            rhs = vc[g][:, b, kb * GW:(kb + 1) * GW] if kb < nk else new[:, 2, g, :]
                            mm = nc.tensor.matmul(ps_o[rows, :], p_t[:, kb, rows], rhs, start=(kb == 0), stop=(kb == nk))
                    mm.then_inc(pv_done, 1)

        @block.scalar
        def _(act):
            act.sem_inc(kt_done, 1)
            with act.Fori(0, 2) as i:
                for g in range(3):
                    n, w = i * 3 + g, NKB[g] * P
                    for b in range(4):
                        q = n * 4 + b
                        act.wait_ge(ktr, q + 1)
                        act.wait_ge(scored, q + 1)
                        nc.scalar.copy(k_t[b % 2][:, :, 0:w], ps_k[:, :, 0:w]).then_inc(kt_done, 1)
                    act.wait_ge(m_ready, n + 1)
                    nc.scalar.activation(prob[:, 0:w + NS], sc[:, 0:w + NS], ACT.Exp, bias=nb[:, :], scale=0.125,
                                         accum_out=den[:, :]).then_inc(exp_done, 1)

        @block.vector
        def _(dve):
            nc.vector.memset(prob[:, :], 0.0).then_inc(zeroed, 1)
            nc.vector.memset(new[NS:P], 0.0).then_inc(zeroed, 1)
            for g in range(3):
                nc.vector.memset(qbd[g][:, :, :, :, :], 0.0).then_inc(zeroed, 1)
            dve.wait_ge(zeroed, 5)
            for g in range(3):
                dve.wait_ge(new_tr, g + 1)
                nc.vector.tensor_copy(new_tt[:, :, g, :, :],
                                      ps_k[:, 0, 0:4 * NS].rearrange("p (j h t) -> p j h t", j=2, h=2)).then_inc(new_t, 1)
            dve.wait_ge(new_t, 3)
            dve.sem_inc(t_done, 1)
            dve.sem_inc(pt_ready, 1)
            dve.sem_inc(picked, 1)
            with dve.Fori(0, 2) as i:
                for g in range(3):
                    n, nk, w = i * 3 + g, NKB[g], NKB[g] * P
                    dve.wait_ge(scored, n * 4 + 2)
                    for h in range(HPG):
                        e, hp = 64 * (h % 2), h // 2
                        cp = nc.vector.tensor_copy(qbd[g][e:e + 64, hp, :, h, :], new_tt[
                            e:e + 64, 0, g, hp, bass.ds(i * 32, 32)].rearrange("p (b t) -> p b t", b=4))
                    cp.then_inc(qbd_done, 1)
                    dve.wait_ge(scored, n * 4 + 6)
                    slope = pr.c("slope_s")[:, g:g + 1]
                    a = AT[f"pens0{g}"][0]
                    pen = lambda at, width: pr.const[:, bass.ds(i * penw + a + at, width)]
                    dve.wait_ge(pv_done, n + 3)
                    nc.vector.scalar_tensor_tensor(sc[:, 0:w], pen(0, w), slope, ps_s[:, 0:w], ALU.mult, ALU.add)\
                        .then_inc(mstep, 1)
                    nc.vector.scalar_tensor_tensor(sc[:, w:w + NS], pen(w, NS), slope, ps_n[:, 0:NS], ALU.mult, ALU.add)\
                        .then_inc(t_done, 1)
                    dve.wait_ge(mstep, n * 2 + 1)
                    dve.wait_ge(t_done, n + 2)
                    nc.vector.tensor_reduce(m8[:, :], sc[:, 0:w + NS], AX, ALU.max).then_inc(mstep, 1)
                    dve.wait_ge(mstep, n * 2 + 2)
                    nc.vector.tensor_scalar(nb[:, :], m8[:, :], -0.125, None, ALU.mult).then_inc(m_ready, 1)
                    dve.wait_ge(p_turned, n + 1)
                    nc.vector.tensor_copy(p_t[:, 0:nk + 1, :], ps_pt[:, 0:nk + 1, :]).then_inc(pt_ready, 1)
                    dve.wait_ge(pv_done, n + 4)
                    nc.vector.tensor_tensor(pick[:, :, :], ps_o[:, :].rearrange("p (h c) -> p h c", h=HPG),
                                            pr.c("headmask").unsqueeze(2).broadcast_to([P, HPG, DH]), ALU.mult)\
                        .then_inc(picked, 1)
                    dve.wait_ge(picked, n + 2)
                    dve.wait_ge(rec_free, n + 1)
                    nc.vector.tensor_reduce(rec[:, 0:DH], pick[:, :, :].rearrange("p h c -> p c h"), AX, ALU.add)\
                        .then_inc(rec_done, 1)
                    nc.vector.tensor_copy(rec[:, DH:DH + 1], m8[:, :]).then_inc(rec_done, 1)
                    nc.vector.tensor_copy(rec[:, DH + 1:REC], den[:, :]).then_inc(rec_done, 1)
                    dve.wait_ge(rec_done, n * 3 + 3)

        @block.gpsimd
        def _(pool):
            pool.sem_inc(rec_free, 1)
            with pool.Fori(0, 2) as i:
                for g in range(3):
                    n = i * 3 + g
                    pool.wait_ge(rec_done, n * 3 + 3)
                    dst = t["att_rec"][g, SEQ:TOK].rearrange("(b t) (h c) -> b h t c", t=NT, c=REC)
                    for b in range(4):
                        for h in range(HPG):
                            r = 32 * b + 8 * h
                            pool.dma_start(dst[i * 4 + b, h], rec[r:r + 8, :]).then_inc(stored, 16)
                    pool.wait_ge(stored, n * 256 + 256)
                    pool.sem_inc(rec_free, 1)


def recurrence(pr):
    nc, t = pr.nc, pr.t
    (base_in, lb_done, e_f, f_done, lf_done, einv_done, log_done, sums, exps, q_done, k_done, k_tr, k_t, u_done,
     a_done, am_done, sprime, inter, s_done, squared, msum, ms, rln, rexp, o_ready, stored, o_free, seeds, s_out,
     tile_done, act_step, dve_step, km_done) = (pr.sem(f"hg_{n}") for n in (
         "base", "lb", "ef", "f", "lf", "einv", "log", "sums", "exps", "q", "k", "ktr", "kt", "u", "a", "am",
         "sprime", "inter", "sdone", "squared", "msum", "ms", "rln", "rexp", "oready", "stored", "ofree",
         "seeds", "sout", "tile", "actstep", "dvestep", "km"))
    fi_in, tmp_done = pr.sem("hg_fi"), pr.sem("hg_tmp")
    with ExitStack() as cx:
        sb = lambda name, shape: cx.enter_context(nc.sbuf_tensor(f"hg_{name}", shape, F32))
        ps = lambda name, shape: cx.enter_context(nc.psum_tensor(f"hg_{name}", shape, F32))
        lb, oml, gain = sb("lb", [P, HW]), sb("oml", [P, HW]), sb("gain", [P, 1])
        fi, qg = sb("fi", [P, 2 * HW]), sb("qg", [P, 2 * HH, P])
        f, x, lf, kh, en = (sb(n, [P, HW]) for n in ("f", "x", "lf", "kh", "en"))
        eg, eq, kt, am, osq, rs, sg = (sb(n, [P, HH, P]) for n in ("eg", "eq", "kt", "am", "osq", "rs", "sg"))
        em = sb("em", [P, HH, 8])
        state = sb("state", [P, HH, HK])
        sp_ = [sb(f"sp{s}", [P, HH, HK]) for s in range(2)]
        s8 = sb("s8", [P, NB, HH, HK])
        km = sb("km", [NS, NB, HW])
        oh = sb("oh", [P, HH, P])
        ps_ct = ps("ps_ct", [P, HH, 256])
        ps_cn = ps("ps_cn", [P, HW])
        ps_u = [ps(f"ps_u{c}", [P, HH, HK]) for c in range(4)]
        ps_o = ps("ps_o", [P, HH, P])
        block = cx.enter_context(nc.Block("recurrence"))
        state_in = t["state_hgrn"][0].rearrange("b h k v -> k b h v")
        state_out = t["hgrn_s"][0].rearrange("b h k v -> k b h v")

        def tiles(eng, tile):
            with eng.Fori(0, PT) as i:
                tile(i, P, CH, "p")
            tile(PT, NS, NT, "s")

        def x_t(r):
            return kt[:, :, r]

        @block.sync
        def _(sp):
            for r in range(2):
                sp.dma_start((lb, oml)[r][:, :], t["hg_lower_bound"][r].partition_broadcast(P)).then_inc(base_in, 16)
            sp.dma_start(gain[:, :], t["hg_norm_g"].rearrange("a p -> p a")).then_inc(base_in, 16)
            sp.dma_start(s8[:, :, :, :], state_in).then_inc(seeds, 16)

            def tile(n, rows, ch, kind):
                sp.wait_ge(tile_done, n + 1)
                sp.dma_start(fi[0:rows, :], t["proj_n"][bass.ds(n * P, rows), C_ZF:NATC]).then_inc(fi_in, 16)
                sp.dma_start(qg[:, :, 0:rows], t["proj_t"][0:2 * HW, bass.ds(n * P, rows)]
                             .rearrange("(k p) t -> p k t", p=P)).then_inc(fi_in, 16)
                sp.wait_ge(o_ready, n + 1)
                sp.dma_start(t["oh_t"][:, bass.ds(n * P, rows)].rearrange("(k p) t -> p k t", p=P),
                             oh[:, :, 0:rows]).then_inc(stored, 16)
                if kind == "p":
                    sp.wait_ge(stored, n * 16 + 16)
                    sp.sem_inc(o_free, 1)

            with sp.Fori(0, PT) as i:
                tile(i, P, CH, "p")
            tile(PT, NS, NT, "s")
            sp.dma_start(t["hgrn_p"][0, 0].rearrange("h k v -> k h v"), state[:, :, :]).then_inc(s_out, 16)
            sp.wait_ge(s_done, 4 * PT + NB)
            sp.dma_start(state_out, s8[:, :, :, :]).then_inc(s_out, 16)
            sp.wait_ge(s_out, 32)
            sp.wait_ge(stored, (PT + 1) * 16)

        @block.scalar
        def _(act):
            act.wait_ge(lb_done, 1)
            nc.scalar.activation(lb[:, :], lb[:, :], ACT.Exp).then_inc(lb_done, 1)
            act.sem_inc(tile_done, 1)

            def tile(n, rows, ch, kind):
                r, nch = slice(0, rows), rows // ch
                act.wait_ge(fi_in, n * 32 + 32)
                act.wait_ge(f_done, n + 1)
                nc.scalar.activation(x[r, :], fi[r, 0:HW], ACT.Exp, scale=-1.0).then_inc(e_f, 1)
                nc.scalar.activation(eg[:, :, r], qg[:, HH:, r], ACT.Exp, scale=-1.0).then_inc(e_f, 1)
                act.wait_ge(f_done, n + 2)
                nc.scalar.activation(lf[r, :], f[r, :], ACT.Ln).then_inc(lf_done, 1)
                act.wait_ge(lf_done, n + 1)
                nc.scalar.activation(x[r, :], lf[r, :], ACT.Exp, scale=-1.0).then_inc(einv_done, 1)
                act.wait_ge(sums, n + 1)
                nc.scalar.activation(eq[:, :, r], ps_ct[:, :, r], ACT.Exp)
                nc.scalar.activation(en[r, :], ps_cn[r, :], ACT.Exp, scale=-1.0)
                nc.scalar.activation(em[:, :, 0:nch], ps_ct[:, :, rows:rows + nch], ACT.Exp).then_inc(exps, 1)
                act.wait_ge(k_tr, n + 1)
                nc.scalar.copy(kt[:, :, r], ps_cn[:, :].rearrange("p (h t) -> p h t", h=HH)[:, :, r]).then_inc(k_t, 1)
                act.wait_ge(inter, n * 4 + nch + 1)
                nc.scalar.activation(osq[:, :, r], ps_o[:, :, r], ACT.Square).then_inc(squared, 1)
                act.wait_ge(ms, n + 1)
                nc.scalar.activation(rs[:, :, r], x_t(r), ACT.Ln).then_inc(rln, 1)
                act.wait_ge(rln, n + 1)
                nc.scalar.activation(rs[:, :, r], rs[:, :, r], ACT.Exp, scale=-0.5).then_inc(rexp, 1)

            tiles(act, tile)

        @block.vector
        def _(dve):
            step = Ordered(dve, dve_step)
            dve.wait_ge(base_in, 48)
            nc.vector.tensor_tensor(lb[:, :], oml[:, :], lb[:, :], ALU.subtract).then_inc(lb_done, 1)
            dve.wait_ge(lb_done, 2)
            step(nc.vector.tensor_scalar(lb[:, :], lb[:, :], 1.0, None, ALU.add))
            step(nc.vector.reciprocal(lb[:, :], lb[:, :]))
            step(nc.vector.tensor_scalar(oml[:, :], lb[:, :], -1.0, 1.0, ALU.mult, ALU.add))
            step(nc.vector.memset(state[:, :, :], 0.0))
            START, STEPS = 4, 14
            dve.sem_inc(f_done, 1)
            over = lambda y, rows: y.unsqueeze(2).broadcast_to([P, HH, HK])

            def tile(n, rows, ch, kind):
                r, nch = slice(0, rows), rows // ch
                step.turn(n, STEPS, START)
                dve.wait_ge(e_f, n * 2 + 2)
                step(nc.vector.tensor_scalar(f[r, :], x[r, :], 1.0, None, ALU.add))
                step(nc.vector.reciprocal(f[r, :], f[r, :]))
                step(nc.vector.tensor_tensor(f[r, :], f[r, :], oml[r, :], ALU.mult))
                nc.vector.tensor_tensor(f[r, :], f[r, :], lb[r, :], ALU.add).then_inc(f_done, 1)
                dve.wait_ge(f_done, n + 2)
                step(nc.vector.tensor_scalar(kh[r, :], f[r, :], -1.0, 1.0, ALU.mult, ALU.add))
                step(nc.vector.tensor_scalar(sg[:, :, r], eg[:, :, r], 1.0, None, ALU.add))
                step(nc.vector.reciprocal(sg[:, :, r], sg[:, :, r]))
                step(nc.vector.tensor_tensor(sg[:, :, r], sg[:, :, r], qg[:, HH:, r], ALU.mult))
                dve.wait_ge(einv_done, n + 1)
                step(nc.vector.tensor_tensor(x[r, :], f[r, :], x[r, :], ALU.mult))
                nc.vector.scalar_tensor_tensor(lf[r, :], x[r, :], -1.0, lf[r, :], ALU.add, ALU.add).then_inc(log_done, 1)
                dve.wait_ge(exps, n + 1)
                nc.vector.tensor_tensor(kh[r, :], kh[r, :], en[r, :], ALU.mult).then_inc(k_done, 1)
                nc.vector.tensor_tensor(qg[:, 0:HH, r], qg[:, 0:HH, r], eq[:, :, r], ALU.mult).then_inc(q_done, 1)
                if kind == "s":
                    dve.wait_ge(k_done, n + 1)
                    for c in range(nch):
                        nc.vector.tensor_scalar(km[:, c, :], kh[r, :], pr.c("seqmask", NS)[:, c:c + 1], None,
                                                ALU.mult).then_inc(km_done, 1)
                dve.wait_ge(a_done, n + 1)
                causal = pr.c(f"causal_{kind}", rows).unsqueeze(1).broadcast_to([rows, HH, rows])
                nc.vector.tensor_tensor(am[r, :, r], ps_ct[r, 0:2, :].rearrange("p a (b t) -> p (a b) t", b=2)[:, :, r],
                                        causal, ALU.mult).then_inc(am_done, 1)
                for c in range(nch):
                    q = n * 4 + c
                    s_in = state[:, :, :] if kind == "p" else s8[:, c, :, :]
                    dve.wait_ge(inter, q + 1)
                    nc.vector.tensor_tensor(sp_[c % 2][:, :, :], s_in, over(em[:, :, c], rows), ALU.mult).then_inc(sprime, 1)
                    dve.wait_ge(sprime, q + 1)
                    dve.wait_ge(u_done, q + 1)
                    nc.vector.tensor_tensor(s_in, sp_[c % 2][:, :, :], ps_u[c % 4][:, :, :], ALU.add).then_inc(tmp_done, 1)
                    dve.wait_ge(tmp_done, q + 1)
                    nc.vector.tensor_tensor(s_in, s_in, over(eq[:, :, c * ch + ch - 1], rows), ALU.mult).then_inc(s_done, 1)
                    dve.wait_ge(s_done, q + 1)
                dve.wait_ge(msum, n + 1)
                nc.vector.tensor_scalar(x_t(r), ps_cn[:, :].rearrange("p (h t) -> p h t", h=HH)[:, :, r],
                                        1.0 / HK, EPS, ALU.mult, ALU.add).then_inc(ms, 1)
                dve.wait_ge(ms, n + 1)
                dve.wait_ge(rexp, n + 1)
                step(nc.vector.tensor_tensor(eg[:, :, r], rs[:, :, r], rs[:, :, r], ALU.mult))
                step(nc.vector.tensor_tensor(eg[:, :, r], eg[:, :, r], x_t(r), ALU.mult))
                step(nc.vector.tensor_scalar(eg[:, :, r], eg[:, :, r], -0.5, 1.5, ALU.mult, ALU.add))
                step(nc.vector.tensor_tensor(rs[:, :, r], rs[:, :, r], eg[:, :, r], ALU.mult))
                step(nc.vector.tensor_tensor(sg[:, :, r], sg[:, :, r], rs[:, :, r], ALU.mult))
                step(nc.vector.tensor_scalar(sg[:, :, r], sg[:, :, r], gain[:, 0:1], None, ALU.mult))
                dve.wait_ge(o_free, n + 1)
                nc.vector.tensor_tensor(oh[:, :, r], sg[:, :, r], ps_o[:, :, r], ALU.mult).then_inc(o_ready, 1)
                dve.wait_ge(o_ready, n + 1)
                dve.sem_inc(tile_done, 1)
                assert step.n == STEPS, step.n

            dve.sem_inc(inter, 1)
            dve.sem_inc(o_free, 1)
            dve.wait_ge(seeds, 16)
            tiles(dve, tile)

        @block.tensor
        def _(pe):
            def tile(n, rows, ch, kind):
                r, nch = slice(0, rows), rows // ch
                tri = pr.c(f"tri_{kind}", rows)
                pe.wait_ge(log_done, n + 1)
                for h in range(HH):
                    nc.tensor.matmul(ps_ct[:, h, 0:rows + nch], lf[r, h * HK:(h + 1) * HK], tri, start=True, stop=True)
                nc.tensor.matmul(ps_cn[r, :], tri[:, r], lf[r, :], start=True, stop=True).then_inc(sums, 1)
                pe.wait_ge(k_done, n + 1)
                for h in range(HH):
                    mm = nc.tensor.transpose(ps_cn[:, h * P:h * P + rows], kh[r, h * HK:(h + 1) * HK],
                                             pr.c("ident")[r, r])
                mm.then_inc(k_tr, 1)

                def increments(c):
                    if kind == "p":
                        a = slice(c * ch, (c + 1) * ch)
                        lhs, rhs = kh[a], fi[a, HW:]
                    else:
                        pe.wait_ge(km_done, c + 1)
                        lhs, rhs = km[:, c], fi[r, HW:]
                    for h in range(HH):
                        hs = slice(h * HK, (h + 1) * HK)
                        mm = nc.tensor.matmul(ps_u[c % 4][:, h, :], lhs[:, hs], rhs[:, hs], start=True, stop=True)
                    mm.then_inc(u_done, 1)

                for c in range(4):
                    increments(c)
                pe.wait_ge(k_t, n + 1)
                pe.wait_ge(q_done, n + 1)
                for h in range(HH):
                    mm = nc.tensor.matmul(ps_ct[r, h // 2, h % 2 * P:h % 2 * P + rows], kt[:, h, r], qg[:, h, r],
                                          start=True, stop=True)
                mm.then_inc(a_done, 1)
                pe.wait_ge(am_done, n + 1)
                for h in range(HH):
                    nc.tensor.matmul(ps_o[:, h, r], fi[r, HW + h * HK:HW + (h + 1) * HK], am[r, h, r],
                                     start=(h == 0), stop=False, skip_group_check=True)
                for c in range(nch):
                    pe.wait_ge(sprime, n * 4 + c + 1)
                    for h in range(HH):
                        mm = nc.tensor.matmul(ps_o[:, h, c * ch:(c + 1) * ch], sp_[c % 2][:, h, :],
                                              qg[:, h, c * ch:(c + 1) * ch], start=False,
                                              stop=(c == nch - 1 and h == HH - 1), skip_group_check=True)
                    mm.then_inc(inter, 1)
                    if c + 4 < nch:
                        pe.wait_ge(s_done, n * 4 + c + 1)
                        increments(c + 4)
                pe.wait_ge(squared, n + 1)
                nc.tensor.matmul(ps_cn[:, :].rearrange("p (h t) -> p h t", h=HH)[:, :, r], pr.c("ones"), osq[:, :, r],
                                 start=True, stop=True).then_inc(msum, 1)

            tiles(pe, tile)


def mixer_merge(pr):
    nc, t = pr.nc, pr.t
    KA, KH = GW // P, HW // P
    acts_in = pr.sem("mm_acts")
    w_in = [pr.sem(f"mm_win{s}") for s in range(2)]
    z_in = [pr.sem(f"mm_zin{s}") for s in range(2)]
    (prod_a, prod_h, sig, scaled_a, scaled_h, summed, stored, m_free) = (pr.sem(f"mm_{n}") for n in (
        "proda", "prodh", "sig", "scaleda", "scaledh", "summed", "stored", "mfree"))
    with ExitStack() as cx:
        sb = lambda name, shape: cx.enter_context(nc.sbuf_tensor(f"mm_{name}", shape, F32))
        att, oh = sb("att", [P, KA, TOK]), sb("oh", [P, KH, TOK])
        wa, wh = [[sb(f"{n}{s}", [P, k, P]) for s in range(2)] for n, k in (("wa", KA), ("wh", KH))]
        z = [sb(f"z{s}", [P, 2, TOK]) for s in range(2)]
        ma = [sb(f"ma{s}", [P, 2, TOK]) for s in range(2)]
        ps_a = cx.enter_context(nc.psum_tensor("mm_psa", [P, 3 * 512], F32))
        ps_h = cx.enter_context(nc.psum_tensor("mm_psh", [P, 3 * 512], F32))
        block = cx.enter_context(nc.Block("mixer_merge"))
        turns = D // P // 2
        wa_v, wh_v = (t[n][0].rearrange("(k p) n -> p k n", p=P) for n in ("w_att_branch", "w_hg_branch"))
        gates = t["proj_t"][2 * HW:, :].rearrange("(g c p) t -> c p g t", g=2, p=P)

        @block.sync
        def _(sp):
            sp.dma_start(att[:, :, :], t["att_t"].rearrange("(k p) t -> p k t", p=P)).then_inc(acts_in, 16)
            sp.dma_start(oh[:, :, :], t["oh_t"].rearrange("(k p) t -> p k t", p=P)).then_inc(acts_in, 16)

            def load(c, s):
                sp.dma_start(wa[s][:, :, :], wa_v[:, :, bass.ds(c * P, P)]).then_inc(w_in[s], 16)
                sp.dma_start(wh[s][:, :, :], wh_v[:, :, bass.ds(c * P, P)]).then_inc(w_in[s], 16)
                sp.dma_start(z[s][:, :, :], gates[c]).then_inc(z_in[s], 16)

            for s in range(2):
                load(s, s)
            with sp.Fori(1, turns) as i:
                for s in range(2):
                    sp.wait_ge(scaled_h, i * 2 + s)
                    load(i * 2 + s, s)

        @block.tensor
        def _(pe):
            pe.wait_ge(acts_in, 32)
            with pe.Fori(0, turns) as i:
                for s in range(2):
                    pe.wait_ge(w_in[s], i * 32 + 32)
                    for w, x, k_n, ps, done, free in ((wa, att, KA, ps_a, prod_a, scaled_a),
                                                      (wh, oh, KH, ps_h, prod_h, scaled_h)):
                        pe.wait_ge(free, i * 2 + s + 1)
                        for k in range(k_n):
                            for a in range(0, TOK, 512):
                                e = min(a + 512, TOK)
                                mm = nc.tensor.matmul(ps[:, a:e], w[s][:, k, :], x[:, k, a:e],
                                                      start=(k == 0), stop=(k == k_n - 1))
                        mm.then_inc(done, 1)

        @block.scalar
        def _(act):
            with act.Fori(0, turns) as i:
                for s in range(2):
                    act.wait_ge(z_in[s], i * 16 + 16)
                    nc.scalar.activation(z[s][:, :, :], z[s][:, :, :], ACT.Sigmoid).then_inc(sig, 1)

        @block.vector
        def _(dve):
            dve.sem_inc(scaled_a, 1)
            dve.sem_inc(scaled_h, 1)
            with dve.Fori(0, turns) as i:
                for s in range(2):
                    n = i * 2 + s
                    dve.wait_ge(sig, n + 1)
                    dve.wait_ge(m_free, n + 1)
                    for j, (ps, done, scaled) in enumerate(((ps_a, prod_a, scaled_a), (ps_h, prod_h, scaled_h))):
                        dve.wait_ge(done, n + 1)
                        nc.vector.tensor_tensor(ma[s][:, j, :], ps[:, 0:TOK], z[s][:, j, :], ALU.mult).then_inc(scaled, 1)
                    dve.wait_ge(scaled_a, n + 2)
                    dve.wait_ge(scaled_h, n + 2)
                    nc.vector.tensor_tensor(ma[s][:, 0, :], ma[s][:, 0, :], ma[s][:, 1, :], ALU.add).then_inc(summed, 1)

        @block.gpsimd
        def _(pool):
            pool.sem_inc(m_free, 2)
            with pool.Fori(0, turns) as i:
                for s in range(2):
                    n = i * 2 + s
                    pool.wait_ge(summed, n + 1)
                    pool.dma_start(t["mix_t"][bass.ds(n * P, P), :], ma[s][:, 0, :]).then_inc(stored, 16)
                    pool.wait_ge(stored, n * 16 + 16)
                    pool.sem_inc(m_free, 1)


def mixer_output(pr):
    nc, t = pr.nc, pr.t
    w_in, gates_in, product, gated, added, stored, o_free = (pr.sem(f"mo_{n}") for n in (
        "win", "gates", "product", "gated", "added", "stored", "ofree"))
    in_ = [pr.sem(f"mo_in{s}") for s in range(2)]
    with ExitStack() as cx:
        sb = lambda name, shape: cx.enter_context(nc.sbuf_tensor(f"mo_{name}", shape, F32))
        w, g1 = sb("w", [P, KD, D]), [sb(f"g{r}", [P, D]) for r in range(2)]
        mix = [sb(f"mix{s}", [P, KD, P]) for s in range(2)]
        x = [sb(f"x{s}", [P, D]) for s in range(2)]
        o = [sb(f"o{s}", [P, D]) for s in range(2)]
        ps = [cx.enter_context(nc.psum_tensor(f"mo_ps{s}", [P, D], F32)) for s in range(2)]
        block = cx.enter_context(nc.Block("mixer_output"))
        mix_v = t["mix_t"].rearrange("(k p) t -> p k t", p=P)
        x_s = t["x_sample"].rearrange("b t d -> (b t) d")

        def tiles(eng, tile):
            with eng.Fori(0, PT // 2) as i:
                for s in range(2):
                    tile(i * 2 + s, s, i, P)
            tile(PT, 0, PT // 2, NS)

        @block.sync
        def _(sp):
            for r, (a, n) in enumerate(((0, P), (P, NS))):
                sp.dma_start(g1[r][0:n, :], t["modrep"][a:a + n, 2 * D:3 * D]).then_inc(gates_in, 16)
            sp.dma_start(w[:, :, :], t["w_out"][0].rearrange("(k p) n -> p k n", p=P)).then_inc(w_in, 16)

            def tile(n, s, i, rows):
                sp.wait_ge(added, n + 1)
                sp.dma_start(mix[s][:, :, 0:rows], mix_v[:, :, bass.ds(n * P, rows)]).then_inc(in_[s], 16)
                src = t["x_prompt"][0][bass.ds(n * P, P), :] if rows == P else x_s
                sp.dma_start(x[s][0:rows, :], src).then_inc(in_[s], 16)
            tiles(sp, tile)

        @block.tensor
        def _(pe):
            pe.wait_ge(w_in, 16)

            def tile(n, s, i, rows):
                pe.wait_ge(in_[s], i * 32 + 32)
                pe.wait_ge(gated, n + 1)
                for k in range(KD):
                    for a in range(0, D, 512):
                        mm = nc.tensor.matmul(ps[s][0:rows, a:a + 512], mix[s][:, k, 0:rows], w[:, k, a:a + 512],
                                              start=(k == 0), stop=(k == KD - 1))
                mm.then_inc(product, 1)
            tiles(pe, tile)

        @block.vector
        def _(dve):
            dve.sem_inc(gated, 2)
            dve.sem_inc(added, 2)
            dve.wait_ge(gates_in, 32)

            def tile(n, s, i, rows):
                r = slice(0, rows)
                dve.wait_ge(product, n + 1)
                dve.wait_ge(o_free, n + 1)
                nc.vector.tensor_tensor(o[s][r, :], ps[s][r, :], g1[0 if rows == P else 1][r, :], ALU.mult).then_inc(gated, 1)
                dve.wait_ge(gated, n + 3)
                nc.vector.tensor_tensor(o[s][r, :], o[s][r, :], x[s][r, :], ALU.add).then_inc(added, 1)
            tiles(dve, tile)

        @block.gpsimd
        def _(pool):
            pool.sem_inc(o_free, 2)

            def tile(n, s, i, rows):
                pool.wait_ge(added, n + 3)
                pool.dma_start(t["x1"][bass.ds(n * P, rows), :], o[s][0:rows, :]).then_inc(stored, 16)
                pool.wait_ge(stored, n * 16 + 16)
                pool.sem_inc(o_free, 1)
            tiles(pool, tile)


class Tile:

    def __init__(self, c, i=None):
        self.m = c % 3
        self.q = c // 3 if i is None else i + c // 3
        self.n = c if i is None else i * 3 + c
        self.rows = NS if i is None and c == PT else P


def retrieval(pr):
    nc, t = pr.nc, pr.t
    HP = 2 * HEADS
    RING = 8
    GRP = PICKS // RING // HEADS
    three = lambda name: [pr.sem(f"rv_{name}{s}") for s in range(3)]
    h_in, x_in = three("hin"), three("xin")
    u_in = [pr.sem(f"rv_u{b}") for b in range(RING)]
    v_in = [pr.sem(f"rv_v{b}") for b in range(RING)]
    (sub_in, sub_tr, sub_t, q_in, scored, head_out, lists_free, route, route_end, exp_done) = (pr.sem(f"rt_{n}") for n in (
        "subin", "subtr", "subt", "qin", "scored", "headout", "listsfree", "route", "routeend", "exp"))
    (base_in, zeroed, idx_u, idx_v, u_used, v_used, act8_done, acts, gelu_done, w_done, diag, xg, x2, ssq, ms, ln, rstd,
     newton, y_ready, stored, y_free, routed) = (pr.sem(f"rv_{n}") for n in (
         "base", "zeroed", "idxu", "idxv", "uused", "vused", "act8", "acts", "gelu", "w", "diag", "xg", "x2", "ssq",
         "ms", "ln", "rstd", "newton", "y", "stored", "yfree", "routed"))
    passed = [pr.sem(f"rv_passed{e}") for e in range(2)]
    with ExitStack() as cx:
        sb = lambda name, shape, dt=F32: cx.enter_context(nc.sbuf_tensor(f"rv_{name}", shape, dt))
        trio = lambda name, shape, dt=F32: [sb(f"{name}{s}", shape, dt) for s in range(3)]
        u = [sb(f"u{b}", [P, D]) for b in range(RING)]
        v = [sb(f"v{b}", [P, D]) for b in range(RING)]
        dg = [sb(f"dg{b}", [P, P]) for b in range(RING)]
        h2, x1 = trio("h2", [P, D]), trio("x1", [P, D])
        gate, eid = trio("gate", [P, HEADS, TOPK]), trio("eid", [P, PICKS], U32)
        iu, iv = ([sb(f"{n}{g}", [P, RING], U32) for g in range(GRP)] for n in ("iu", "iv"))
        act8 = [sb(f"act8{g}", [P, RING]) for g in range(GRP)]
        act_, w = trio("act", [P, PICKS]), trio("w", [P, PICKS])
        g2, fg = [sb(f"g2{s}", [P, D]) for s in range(2)], sb("fg", [P, D])
        zero, junk, y, st = sb("zero", [P, 512]), sb("junk", [P, D]), sb("y", [P, D]), sb("st", [P, 8])
        q, sub_tt = sb("q", [P, HP, P]), sb("subt", [P, HP, P])
        lists, rest = sb("lists", [P, 2, KEYS]), sb("rest", [P, 2, KEYS])
        top, ix, ixf = sb("top", [P, 2, TOPK]), sb("ix", [P, 2, TOPK], U32), sb("ixf", [P, 2, TOPK])
        cand, cand2 = sb("cand", [P, 1, TOPK * TOPK]), sb("cand2", [P, 1, TOPK * TOPK])
        best, ci = sb("best", [P, 1, TOPK]), sb("ci", [P, 1, TOPK], U32)
        place, placef = sb("place", [P, 2, TOPK], U32), sb("placef", [P, 2, TOPK])
        hot, num = sb("hot", [P, 2, TOPK, TOPK]), sb("num", [P, 2, TOPK])
        ex, dn = sb("ex", [P, HEADS, TOPK]), sb("dn", [P, HEADS])
        ps_sc = cx.enter_context(nc.psum_tensor("rt_ps", [P, HP, KEYS], F32))
        ps = cx.enter_context(nc.psum_tensor("rv_ps", [P, D], F32))
        block = cx.enter_context(nc.Block("retrieval"))
        sub = v[0:2]

        def run(eng, joint):
            joint(Tile(0), None, None)
            joint(Tile(1), Tile(0), None)
            with eng.Fori(0, (PT - 2) // 3) as i:
                for c in range(3):
                    joint(Tile(c + 2, i), Tile(c + 1, i), Tile(c, i))
            joint(Tile(PT), Tile(PT - 1), Tile(PT - 2))
            joint(None, Tile(PT), Tile(PT - 1))
            joint(None, None, Tile(PT))

        @block.sync
        def _(sp):
            for e in range(2):
                sp.dma_start(sub[e][:, :].rearrange("p (j k) -> p j k", k=P),
                             t["peer_subkeys"][0].rearrange("h p k d -> k (h p) d")[:, e * HEADS:(e + 1) * HEADS, :])\
                    .then_inc(sub_in, 16)
            for r, (a, n) in enumerate(((0, P), (P, NS))):
                sp.dma_start(g2[r][0:n, :], t["modrep"][a:a + n, 5 * D:6 * D]).then_inc(base_in, 16)
            sp.dma_start(fg[:, :], t["final_norm_g"].partition_broadcast(P)).then_inc(base_in, 16)

            def load(tile):
                at, r = bass.ds(tile.n * P, tile.rows), slice(0, tile.rows)
                sp.wait_ge(scored, tile.n + 1)
                sp.dma_start(q[:, :, r], t["qry_t"].rearrange("(k p) t -> p k t", p=P)[:, :, at]).then_inc(q_in, 16)
                sp.wait_ge(acts, tile.n + 1)
                sp.dma_start(h2[tile.m][r, :], t["h2"][at, :]).then_inc(h_in[tile.m], 16)
                sp.wait_ge(x2, tile.n + 1)
                sp.dma_start(x1[tile.m][r, :], t["x1"][at, :]).then_inc(x_in[tile.m], 16)

            with sp.Fori(0, (PT - 2) // 3) as i:
                for c in range(3):
                    load(Tile(c, i))
            for c in range(PT - 2, PT + 1):
                load(Tile(c))

        @block.gpsimd
        def _(pool):
            nc.gpsimd.memset(zero[:, :], 0.0).then_inc(zeroed, 1)
            pool.wait_ge(sub_t, 1)

            def joint(_, tu, tv):
                if tu is None and tv is None:
                    return
                if tu is not None:
                    pool.wait_ge(routed, tu.n + 1)
                    pool.sem_inc(passed[0], 1)
                with pool.Fori(0, HEADS) as j:
                    for g in range(GRP):
                        for tile, used, idx, idx_done, ring, in_, table in (
                                (tu, u_used, iu, idx_u, u, u_in, "peer_u"), (tv, v_used, iv, idx_v, v, v_in, "peer_v")):
                            if tile is None:
                                continue
                            rows = tile.rows
                            k = tile.n * (PICKS // RING) + j * GRP + g
                            nc.gpsimd.tensor_copy(idx[g][0:rows, :],
                                                  eid[tile.m][0:rows, bass.ds(j * (GRP * RING) + g * RING, RING)])\
                                .then_inc(idx_done, 1)
                            pool.wait_ge(idx_done, k + 1)
                            for b in range(RING):
                                pool.wait_ge(used, k * RING + b + 1)
                                pool.sem_inc(passed[0], 1)
                                nc.gpsimd.indirect_dma_start(
                                    out=ring[b][0:rows, :], out_offset=None, in_=t[table][0],
                                    in_offset=bass.IndirectOffsetOnAxis(ap=idx[g][0:rows, b:b + 1], axis=0),
                                ).then_inc(in_[b], 16)

            run(pool, joint)

        @block.vector
        def _(dve):
            V = nc.vector
            step = Ordered(dve, route)
            dve.wait_ge(base_in, 48)
            dve.sem_inc(u_used, RING)
            dve.sem_inc(acts, 3)
            dve.sem_inc(x2, 3)
            dve.sem_inc(lists_free, 1)
            dve.sem_inc(xg, 1)
            STEPS = 15

            def settle(ins):
                step(ins)
                dve.sem_inc(passed[1], 1)

            def top16(src, work, values, index, r, count):
                for e in range(count):
                    last = V.max(values[r, e, 0:8], src[r, e, :])
                settle(last)
                for e in range(count):
                    V.max_index(index[r, e, 0:8], values[r, e, 0:8], src[r, e, :])
                    last = V.match_replace(work[r, e, :], values[r, e, 0:8], src[r, e, :], NEG)
                settle(last)
                for e in range(count):
                    last = V.max(values[r, e, 8:16], work[r, e, :])
                settle(last)
                for e in range(count):
                    last = V.max_index(index[r, e, 8:16], values[r, e, 8:16], work[r, e, :])
                step(last)

            def halves(tile, j):
                r = slice(0, tile.rows)
                step.base, step.n = (tile.n * HEADS + j) * STEPS, 0
                dve.wait_ge(head_out, tile.n * HEADS + j + 1)
                dve.sem_inc(passed[1], 1)
                top16(lists, rest, top, ix, r, 2)
                V.tensor_copy(ixf[r], ix[r]).then_inc(lists_free, 1)

            def sums(tile, j):
                rows, r = tile.rows, slice(0, tile.rows)
                square = [rows, TOPK, TOPK]
                hot_of = lambda x: x.rearrange("p e (a b) -> p e a b", b=TOPK)
                settle(V.tensor_tensor(hot_of(cand[r])[:, 0], top[r, 0].unsqueeze(2).broadcast_to(square),
                                       top[r, 1].unsqueeze(1).broadcast_to(square), ALU.add))
                top16(cand, cand2, best, ci, r, 1)
                V.tensor_tensor(ex[r, bass.ds(j, 1), :], best[r], best[r, :, 0:1].broadcast_to([rows, 1, TOPK]), ALU.subtract)
                V.tensor_single_scalar(place[r, 0], ci[r, 0], 4, ALU.logical_shift_right)
                step(V.tensor_single_scalar(place[r, 1], ci[r, 0], TOPK - 1, ALU.bitwise_and))
                step(V.tensor_copy(placef[r], place[r]))
                for e in range(2):
                    last = V.tensor_tensor(hot[r, e], placef[r, e].unsqueeze(2).broadcast_to(square),
                                           pr.c("iota16", rows).unsqueeze(1).broadcast_to(square), ALU.is_equal)
                step(last)
                for e in range(2):
                    last = V.tensor_tensor(hot[r, e], hot[r, e], ixf[r, e].unsqueeze(1).broadcast_to(square), ALU.mult)
                step(last)
                step(V.tensor_reduce(num[r], hot[r], AX, ALU.add))
                step(V.scalar_tensor_tensor(eid[tile.m][r, bass.ds(j * TOPK, TOPK)], num[r, 0], float(KEYS), num[r, 1],
                                            ALU.mult, ALU.add))
                assert step.n == STEPS, step.n

            def picks(tu, tv, j, g):
                for b in range(RING):
                    if tu is not None:
                        rows = tu.rows
                        k = tu.n * (PICKS // RING) + j * GRP + g
                        dve.wait_ge(u_in[b], k * 16 + 16)
                        V.tensor_tensor_reduce(out=u[b][0:rows, :], in0=u[b][0:rows, :], in1=h2[tu.m][0:rows, :],
                                               scale=1.0, scalar=0.0, op0=ALU.mult, op1=ALU.add,
                                               accum_out=act8[g][0:rows, b:b + 1]).then_inc(u_used, 1)
                    if tv is not None:
                        rows = tv.rows
                        k = tv.n * (PICKS // RING) + j * GRP + g
                        dve.wait_ge(v_used, k * RING + b + 1)
                        V.tensor_scalar(dg[b][0:rows, :], pr.c("ident")[0:rows, :],
                                        w[tv.m][0:rows, bass.ds(j * (GRP * RING) + (g * RING + b), 1)], None,
                                        ALU.mult).then_inc(diag, 1)
                if tu is not None:
                    rows = tu.rows
                    k = tu.n * (PICKS // RING) + j * GRP + g
                    dve.wait_ge(u_used, k * RING + 2 * RING)
                    V.tensor_copy(act_[tu.m][0:rows, bass.ds(j * (GRP * RING) + g * RING, RING)], act8[g][0:rows, :])\
                        .then_inc(act8_done, 1)
                    dve.wait_ge(act8_done, k + 1)

            def joint(tr, tu, tv):
                if tu is not None:
                    dve.wait_ge(h_in[tu.m], tu.q * 16 + 16)
                    dve.sem_inc(passed[1], 1)
                half = HEADS // 2
                for first in (True, False):
                    with dve.Fori(0 if first else half, half if first else HEADS) as j:
                        for g in range(GRP):
                            picks(tu, tv, j, g)
                            if tr is not None and first:
                                halves(tr, j * 2 + g)
                                sums(tr, j * 2 + g)
                    if tr is not None and first:
                        dve.sem_inc(routed, 1)
                        r = slice(0, tr.rows)
                        dve.wait_ge(exp_done, tr.n + 1)
                        ends = Ordered(dve, route_end)
                        ends.turn(tr.n, 3, 0)
                        ends(V.tensor_reduce(dn[r, :], ex[r], AX, ALU.add))
                        ends(V.reciprocal(dn[r, :], dn[r, :]))
                        ends(V.tensor_tensor(gate[tr.m][r], ex[r], dn[r].unsqueeze(2).broadcast_to([tr.rows, HEADS, TOPK]),
                                             ALU.mult))
                        dve.sem_inc(passed[1], 1)
                if tu is not None:
                    rows = tu.rows
                    dve.sem_inc(acts, 1)
                if tv is not None:
                    r = slice(0, tv.rows)
                    dve.wait_ge(v_used, tv.n * PICKS + PICKS + RING)
                    dve.wait_ge(x_in[tv.m], tv.q * 16 + 16)
                    V.tensor_tensor(junk[r, :], ps[r, :], g2[0 if tv.rows == P else 1][r, :], ALU.mult).then_inc(xg, 1)
                    dve.wait_ge(xg, tv.n + 2)
                    V.tensor_tensor(junk[r, :], junk[r, :], x1[tv.m][r, :], ALU.add).then_inc(x2, 1)
                if tu is not None:
                    rows = tu.rows
                    dve.wait_ge(gelu_done, tu.n + 1)
                    V.tensor_tensor(w[tu.m][0:rows, :], act_[tu.m][0:rows, :], gate[tu.m][0:rows].rearrange("p h k -> p (h k)"),
                                    ALU.mult).then_inc(w_done, 1)
                    dve.wait_ge(w_done, tu.n + 1)
                if tv is not None:
                    r = slice(0, tv.rows)
                    dve.wait_ge(y_free, tv.n + 1)
                    dve.wait_ge(ssq, tv.n + 1)
                    V.tensor_scalar(st[r, 1:2], st[r, 0:1], 1.0 / D, EPS, ALU.mult, ALU.add).then_inc(ms, 1)
                    dve.wait_ge(ms, tv.n + 1)
                    dve.wait_ge(rstd, tv.n + 1)
                    last = Ordered(dve, newton)
                    last.turn(tv.n, 4, 0)
                    last(V.scalar_tensor_tensor(st[r, 4:5], st[r, 3:4], st[r, 1:2], st[r, 3:4], ALU.mult, ALU.mult))
                    last(V.tensor_scalar(st[r, 4:5], st[r, 4:5], -0.5, 1.5, ALU.mult, ALU.add))
                    last(V.tensor_tensor(st[r, 5:6], st[r, 3:4], st[r, 4:5], ALU.mult))
                    last(V.scalar_tensor_tensor(y[r, :], junk[r, :], st[r, 5:6], fg[r, :], ALU.mult, ALU.mult))
                    dve.sem_inc(y_ready, 1)

            run(dve, joint)

        @block.scalar
        def _(act):
            act.wait_ge(sub_tr, 1)
            nc.scalar.copy(sub_tt[:, :, :], ps_sc[:, :, :]).then_inc(sub_t, 1)

            def joint(tr, tu, tv):
                if tr is not None:
                    r = slice(0, tr.rows)
                    act.wait_ge(scored, tr.n + 2)
                    act.sem_inc(passed[0], 1)
                    with act.Fori(0, HEADS) as j:
                        act.wait_ge(lists_free, tr.n * HEADS + j + 1)
                        nc.scalar.copy(lists[r], ps_sc[r, bass.ds(j * 2, 2), :]).then_inc(head_out, 1)
                    act.wait_ge(routed, tr.n + 1)
                    nc.scalar.activation(ex[r], ex[r], ACT.Exp).then_inc(exp_done, 1)
                if tu is not None:
                    rows = tu.rows
                    act.wait_ge(acts, tu.n + 4)
                    nc.scalar.activation(act_[tu.m][0:rows, :], act_[tu.m][0:rows, :], ACT.Gelu_apprx_tanh).then_inc(gelu_done, 1)
                if tv is not None:
                    r = slice(0, tv.rows)
                    act.wait_ge(x2, tv.n + 4)
                    nc.scalar.activation(y[r, :], junk[r, :], ACT.Square, accum_out=st[r, 0:1]).then_inc(ssq, 1)
                    act.wait_ge(ms, tv.n + 1)
                    nc.scalar.activation(st[r, 2:3], st[r, 1:2], ACT.Ln).then_inc(ln, 1)
                    act.wait_ge(ln, tv.n + 1)
                    nc.scalar.activation(st[r, 3:4], st[r, 2:3], ACT.Exp, scale=-0.5).then_inc(rstd, 1)
                    act.wait_ge(y_ready, tv.n + 1)
                    whole = t["y_prompt"][0] if tv.rows == P else t["y_sample"].rearrange("b t d -> (b t) d")
                    dst = whole[bass.ds(tv.n * P, P), :] if tv.rows == P else whole
                    act.dma_start(dst, y[r, :]).then_inc(stored, 16)
                    act.wait_ge(stored, tv.n * 16 + 16)
                    act.sem_inc(y_free, 1)

            act.sem_inc(y_free, 1)
            run(act, joint)

        @block.tensor
        def _(pe):
            pe.wait_ge(sub_in, 32)
            for j in range(HP):
                mm = nc.tensor.transpose(ps_sc[:, j, :], sub[j // HEADS][:, j % HEADS * P:(j % HEADS + 1) * P], pr.c("ident"))
            mm.then_inc(sub_tr, 1)
            pe.wait_ge(sub_t, 1)
            pe.wait_ge(zeroed, 1)
            pe.sem_inc(v_used, RING)
            pe.sem_inc(scored, 1)

            def joint(tr, tu, tv):
                if tr is not None:
                    pe.wait_ge(q_in, tr.n * 16 + 16)
                    pe.wait_ge(lists_free, tr.n * HEADS + 1)
                    for j in range(HP):
                        mm = nc.tensor.matmul(ps_sc[0:tr.rows, j, :], q[:, j, 0:tr.rows], sub_tt[:, j, :], start=True, stop=True)
                    mm.then_inc(scored, 1)
                if tv is None:
                    return
                rows = tv.rows
                pe.wait_ge(xg, tv.n + 1)
                for a in range(0, D, 512):
                    nc.tensor.matmul(ps[:, a:a + 512], zero[0:rows, 0:P], zero[0:rows, :],
                                     start=True, stop=False, skip_group_check=True)
                with pe.Fori(0, HEADS) as j:
                    for g in range(GRP):
                        k = tv.n * (PICKS // RING) + j * GRP + g
                        for b in range(RING):
                            pe.wait_ge(v_in[b], k * 16 + 16)
                            pe.wait_ge(diag, k * RING + b + 1)
                            for a in range(0, D, 512):
                                mm = nc.tensor.matmul(ps[:, a:a + 512], dg[b][0:rows, :], v[b][0:rows, a:a + 512],
                                                      start=False, stop=False, skip_group_check=True)
                            mm.then_inc(v_used, 1)

            run(pe, joint)


STAGES = (conditioning, mixer_input, attention_prompt, attention_sample, attention_merge, recurrence, mixer_merge,
          mixer_output, retrieval_queries, retrieval)


def build(nc, t, scratch_kind="Internal", stages=None):
    with ExitStack() as ctx:
        pr = Program(nc, t, ctx, scratch_kind)
        load_constants(pr)
        for n, stage in enumerate(STAGES):
            if stages is None or n in stages:
                stage(pr)
                pr.clear_semaphores()


_INS = ["x_prompt", "x_sample", "cache_k0", "cache_v0", "cache_k1", "cache_v1", "cache_k2", "cache_v2", "state_hgrn",
        "c_prompt", "c_sample", "ada_w", "ada_b", "norm1_g", "w_in", "w_att_branch", "w_hg_branch", "w_out",
        "hg_lower_bound", "hg_norm_g", "norm2_g", "peer_wq", "peer_subkeys", "peer_u", "peer_v", "final_norm_g"]
_OUTS = [("y_prompt", (1, 1024, 1024)), ("y_sample", (8, 8, 1024)),
         ("k0_p", (1, 1, 128, 4, 64)), ("v0_p", (1, 1, 128, 4, 64)), ("k1_p", (1, 1, 512, 4, 64)),
         ("v1_p", (1, 1, 512, 4, 64)), ("k2_p", (1, 1, 1024, 4, 64)), ("v2_p", (1, 1, 1024, 4, 64)),
         ("hgrn_p", (1, 1, 4, 128, 128)),
         ("k0_s", (1, 8, 128, 4, 64)), ("v0_s", (1, 8, 128, 4, 64)), ("k1_s", (1, 8, 512, 4, 64)),
         ("v1_s", (1, 8, 512, 4, 64)), ("k2_s", (1, 8, 1024, 4, 64)), ("v2_s", (1, 8, 1024, 4, 64)),
         ("hgrn_s", (1, 8, 4, 128, 128))]


def kernel(**inputs):
    import concourse.bacc as _bacc
    from concourse.bass_utils import run_bass_kernel_spmd as _run

    nc = _bacc.Bacc("TRN2", target_bir_lowering=False, num_devices=1)
    arrays, t = {"in_const_dram": CONST}, {}
    for name in _INS:
        arrays[f"in_{name}_dram"] = np.ascontiguousarray(inputs[name])
    for name, a in arrays.items():
        t[name[3:-5]] = nc.dram_tensor(name, a.shape, mybir.dt.from_np(a.dtype), kind="ExternalInput").ap()
    for name, shape in _OUTS:
        t[name] = nc.dram_tensor(f"out_{name}_dram", shape, F32, kind="ExternalOutput").ap()
    build(nc, t)
    r = _run(nc, [arrays], core_ids=[0])
    return tuple(r.results[0][f"out_{name}_dram"] for name, _ in _OUTS)
```

```python
from contextlib import ExitStack

import numpy as np

import concourse.bass as bass
from concourse import mybir

F32 = mybir.dt.float32
F16 = mybir.dt.float16
U32 = mybir.dt.uint32
ALU = mybir.AluOpType
ACT = mybir.ActivationFunctionType
AX = mybir.AxisListType.X

P = 128
D = 1024
KD = D // P
SEQ = 1024
NB, NT = 8, 8
NS = NB * NT
TOK = SEQ + NS
PT = SEQ // P
EPS = 1e-6
GROUPS = ((128, 1), (512, 4), (1024, 16))
HPG, DH = 4, 64
GW = HPG * DH
AW = len(GROUPS) * GW
HH, HK = 4, 128
HW = HH * HK
CH = 32
NCH = P // CH
HEADS, KEYS, TOPK, DHALF = 8, 128, 16, 128
PICKS = HEADS * TOPK
HALF = 64
NEG = -1e30
REC = DH + 2
C_Q, C_K, C_V = 0, AW, 2 * AW
C_ZF, C_ZI = 3 * AW, 3 * AW + HW
C_ZQ = C_ZI + HW
C_ZG = C_ZQ + HW
C_ZA = C_ZG + HW
C_ZH = C_ZA + D
NATC = C_ZQ
TRC = 2 * HW + 2 * D
SLOPES = [float(x) for x in np.exp2(np.float32(-8.0) * np.arange(1, 13, dtype=np.float32) / np.float32(12))]
W_S = (P + NS, 512 + NS, 512 + NS)


def constants():
    i, j = np.arange(P)[:, None], np.arange(P)[None, :]
    out, at = [], {}

    def put(name, a):
        a = np.asarray(a, np.float32)
        full = np.zeros((P, a.shape[1]), np.float32)
        full[: a.shape[0]] = a
        at[name] = (sum(x.shape[1] for x in out), a.shape[1])
        out.append(full)

    put("ident", np.eye(P))
    put("ones", np.ones((P, P)))
    def band(dil):
        delta = i + P - np.arange(2 * P)[None, :]
        return np.where((delta >= 0) & (delta <= P), -delta * dil, NEG)
    first = band(1)
    first[:, :P] = NEG
    put("pen0", np.concatenate([first, band(1)], 1))
    put("pen1", band(4))
    put("pen2", np.where((i // 64 == j // 64) & (i % 64 >= j % 64), -(i % 64 - j % 64) * 16, NEG))
    for half in range(2):
        bb, t = i // 32, i % 8
        new = np.arange(NS)[None, :]
        for g, (w, dil) in enumerate(GROUPS):
            n = np.arange(min(w, 512))[None, :]
            kb, p = n // P, n % P
            idx = (n, p * 4 + kb, p % 64 * 16 + p // 64 * 4 + kb)[g]
            d_old = w + t - idx
            d_new = t - new % 8
            same = new // 8 == 4 * half + bb
            p_old = np.where((d_old % dil == 0) & (d_old <= P * dil), -d_old, NEG)
            p_new = np.where(same & (d_new >= 0) & (d_new % dil == 0), -d_new, NEG)
            put(f"pens{half}{g}", np.concatenate([p_old, p_new], 1))
    sl = np.array([[8.0 * SLOPES[4 * g + r % 32 // 8] for g in range(3)] for r in range(P)])
    put("slope_s", sl)
    put("headmask", (i % 32 // 8 == np.arange(4)[None, :]))
    def sums(n, ch):
        s, t = np.arange(n)[:, None], np.arange(n)[None, :]
        mid = ch // 2 - 1
        c = (s // ch == t // ch) * ((s % ch <= t % ch) * 1.0 - (s % ch <= mid))
        m = (s // ch == np.arange(n // ch)[None, :]) & (s % ch <= mid)
        return np.concatenate([c, m], 1), (s // ch == t // ch) & (s <= t)
    a, m = sums(P, CH)
    put("tri_p", a)
    put("causal_p", m)
    a, m = sums(NS, NT)
    put("tri_s", a)
    put("causal_s", m)
    put("seqmask", (np.arange(NS)[:, None] // 8 == np.arange(8)[None, :]))
    put("sel_p", np.concatenate([np.ones((1, P)), np.zeros((8, P))]))
    put("sel_s", np.arange(9)[:, None] == 1 + np.arange(NS)[None, :] // 8)
    put("iota128", np.broadcast_to(np.arange(P), (P, P)))
    put("iota16", np.broadcast_to(np.arange(16), (P, 16)))
    return np.concatenate(out, 1), at


CONST, AT = constants()

SCRATCH = {
    "modrep": ([P + NS, 6 * D], F32), "proj_n": ([TOK, NATC], F32), "proj_t": ([TRC, TOK], F32),
    "att_rec": ([3, SEQ, HPG * REC], F32), "sample_rec": ([3, NS * HPG, REC], F32), "att_t": ([GW, TOK], F32), "oh_t": ([HW, TOK], F32),
    "mix_t": ([D, TOK], F32), "x1": ([TOK, D], F32),
    "e1": ([TOK, PICKS], F32), "e2": ([TOK, PICKS], F32),
    "gate": ([TOK, PICKS], F32), "gate_all": ([KEYS, TOK // HALF, KEYS, HALF], F32),
}


class Ordered:

    def __init__(self, eng, sem):
        self.eng, self.sem, self.base, self.n = eng, sem, 0, 0

    def turn(self, i, steps, start):
        self.base, self.n = i * steps + start, 0

    def __call__(self, ins):
        ins.then_inc(self.sem, 1)
        self.n += 1
        self.eng.wait_ge(self.sem, self.base + self.n)


class Program:
    def __init__(self, nc, t, ctx, scratch_kind):
        self.nc, self.t, self.ctx = nc, t, ctx
        self.sems = []
        self.const = ctx.enter_context(nc.sbuf_tensor("const", [P, CONST.shape[1]], F32))
        for name, (shape, dtype) in SCRATCH.items():
            kind = scratch_kind if isinstance(scratch_kind, str) else scratch_kind(name)
            t[name] = nc.dram_tensor(name, shape, dtype, kind=kind).ap()

    def c(self, name, rows=P):
        a, n = AT[name]
        return self.const[0:rows, a:a + n]

    def sem(self, name):
        handle = self.nc.alloc_semaphore(name=name)
        self.sems.append(handle)
        return handle

    def clear_semaphores(self):
        nc = self.nc
        nc.clear_and_free_semaphores(self.sems)
        nc.all_engine_barrier()
        self.sems = []


def load_constants(pr):
    nc = pr.nc
    loaded = pr.sem("const_loaded")
    with nc.Block("load_constants") as block:
        @block.sync
        def _(sp):
            sp.dma_start(pr.const[:, :], pr.t["const"]).then_inc(loaded, 16)
            sp.wait_ge(loaded, 16)


SPLIT = 64.0


def conditioning(pr):
    nc, t = pr.nc, pr.t
    CW = 512
    chunks = 6 * D // CW
    RING = 4
    s_in, s_sig, s_act, s_tr, s_ct = (pr.sem(f"ad_{n}") for n in ("in", "sig", "silu", "tr", "ct"))
    w_in = [pr.sem(f"ad_win{s}") for s in range(RING)]
    s_hi, s_lo, s_mod, s_modsb, s_rep, s_repsb = (pr.sem(f"ad_{n}") for n in ("hi", "lo", "mod", "modsb", "rep", "repsb"))
    rep_free, s_stored = pr.sem("ad_repfree"), pr.sem("ad_stored")
    w_v = t["ada_w"][0].rearrange("(k p) n -> p k n", p=P)
    with ExitStack() as cx:
        sb = lambda name, shape, dt=F32: cx.enter_context(nc.sbuf_tensor(name, shape, dt))
        ps = lambda name, shape: cx.enter_context(nc.psum_tensor(name, shape, F32))
        c9, sg = sb("c9", [9, D]), sb("sg", [9, D])
        ct_hi, ct_lo = sb("ct_hi", [P, KD, 9], F16), sb("ct_lo", [P, KD, 9], F16)
        w = [sb(f"adw{s}", [P, KD, CW]) for s in range(RING)]
        w_hi, w_lo = ([sb(f"ad{n}{s}", [P, KD, CW], F16) for s in range(RING)] for n in ("whi", "wlo"))
        bias = [sb(f"adb{s}", [9, CW]) for s in range(RING)]
        modsb = [sb(f"modsb{s}", [9, CW]) for s in range(2)]
        rep = [sb(f"rep{s}", [P, CW]) for s in range(2)]
        reps = [sb(f"reps{s}", [NS, CW]) for s in range(2)]
        p_tr = ps("p_tr", [P, KD, 16])
        p_mod = [ps(f"p_mod{s}", [9, CW]) for s in range(2)]
        p_rep = [ps(f"p_rep{s}", [P, CW]) for s in range(2)]
        p_reps = [ps(f"p_reps{s}", [NS, CW]) for s in range(2)]
        block = cx.enter_context(nc.Block("conditioning"))

        def run(eng, step):
            with eng.Fori(0, chunks // RING - 1) as i:
                for s in range(RING):
                    step(i * RING + s, s)
            for s in range(RING):
                step(chunks - RING + s, s)

        def follows(n, ahead):
            return not isinstance(n, int) or n + ahead < chunks

        @block.sync
        def _(sp):
            sp.dma_start(c9[0:1, :], t["c_prompt"]).then_inc(s_in, 16)
            sp.dma_start(c9[1:9, :], t["c_sample"]).then_inc(s_in, 16)

            def load(n, s):
                cols = bass.ds(n * CW, CW)
                sp.dma_start(w[s][:, :, :], w_v[:, :, cols]).then_inc(w_in[s], 16)
                sp.dma_start(bias[s][:, :], t["ada_b"][0, cols].partition_broadcast(9)).then_inc(w_in[s], 16)

            def step(n, s):
                if follows(n, RING):
                    sp.wait_ge(s_modsb, n + 3)
                    load(n + RING, s)

            for s in range(RING):
                load(s, s)
            run(sp, step)

        @block.tensor
        def _(pe):
            pe.wait_ge(s_act, 1)
            for k in range(KD):
                tr = nc.tensor.transpose(p_tr[:, k, 0:9], c9[:, k * P:(k + 1) * P], pr.c("ident")[0:9, 0:9])
            tr.then_inc(s_tr, 1)
            pe.wait_ge(s_ct, 2)

            def multiply(n, s):
                pe.wait_ge(s_lo, n + 1)
                pe.wait_ge(s_modsb, n + 1)
                mms = [(c, x, k) for k in range(KD) for c, x in ((ct_hi, w_hi), (ct_hi, w_lo), (ct_lo, w_hi))]
                for j, (c, x, k) in enumerate(mms):
                    mm = nc.tensor.matmul(p_mod[s % 2][:, :], c[:, k, :], x[s][:, k, :], start=(j == 0), stop=(j == len(mms) - 1))
                mm.then_inc(s_mod, 1)

            def step(n, s):
                if follows(n, 1):
                    multiply(n + 1, (s + 1) % RING)
                pe.wait_ge(s_modsb, n + 3)
                pe.wait_ge(s_repsb, n * 2 + 2)
                nc.tensor.matmul(p_rep[s % 2][:, :], pr.c("sel_p", 9), modsb[s % 2][:, :], start=True, stop=True)
                nc.tensor.matmul(p_reps[s % 2][:, :], pr.c("sel_s", 9), modsb[s % 2][:, :], start=True, stop=True).then_inc(s_rep, 1)

            pe.sem_inc(s_repsb, 4)
            multiply(0, 0)
            run(pe, step)

        @block.scalar
        def _(act):
            act.wait_ge(s_in, 32)
            nc.scalar.activation(sg[:, :], c9[:, :], ACT.Sigmoid).then_inc(s_sig, 1)
            act.sem_inc(rep_free, 2)
            act.sem_inc(s_mod, RING)
            act.wait_ge(s_tr, 1)
            nc.scalar.copy(ct_hi[:, :, :], p_tr[:, :, 0:9]).then_inc(s_ct, 1)

            def high(n, s):
                act.wait_ge(w_in[s], (n - s) * 8 + 32)
                act.wait_ge(s_mod, n + 1)
                nc.scalar.activation(w_hi[s][:, :, :], w[s][:, :, :], ACT.Copy, scale=SPLIT).then_inc(s_hi, 1)

            def step(n, s):
                if follows(n, 3):
                    high(n + 3, (s + 3) % RING)
                act.wait_ge(s_rep, n + 3)
                act.wait_ge(rep_free, n + 1)
                nc.scalar.copy(rep[s % 2][:, :], p_rep[s % 2][:, :]).then_inc(s_repsb, 1)
                nc.scalar.copy(reps[s % 2][:, :], p_reps[s % 2][:, :]).then_inc(s_repsb, 1)

            for s in range(3):
                high(s, s)
            run(act, step)

        @block.vector
        def _(dve):
            dve.wait_ge(s_sig, 1)
            nc.vector.tensor_tensor(c9[:, :], c9[:, :], sg[:, :], ALU.mult).then_inc(s_act, 1)
            dve.wait_ge(s_ct, 1)
            nc.vector.tensor_tensor(ct_lo[:, :, :], p_tr[:, :, 0:9], ct_hi[:, :, :], ALU.subtract).then_inc(s_ct, 1)

            def low(n, s):
                dve.wait_ge(s_hi, n + 1)
                nc.vector.scalar_tensor_tensor(w_lo[s][:, :, :], w[s][:, :, :], SPLIT, w_hi[s][:, :, :],
                                               ALU.mult, ALU.subtract).then_inc(s_lo, 1)

            def step(n, s):
                dve.wait_ge(s_mod, n + RING + 1)
                dve.wait_ge(s_rep, n + 1)
                nc.vector.scalar_tensor_tensor(modsb[s % 2][:, :], p_mod[s % 2][:, :], 1.0 / SPLIT, bias[s][:, :],
                                               ALU.mult, ALU.add).then_inc(s_modsb, 1)
                if follows(n, 3):
                    low(n + 3, (s + 3) % RING)

            dve.sem_inc(s_modsb, 2)
            dve.sem_inc(s_rep, 2)
            for s in range(3):
                low(s, s)
            run(dve, step)

        @block.gpsimd
        def _(pool):
            with pool.Fori(0, chunks // 2) as i:
                for s in range(2):
                    col = (i * 2 + s) * CW
                    pool.wait_ge(s_repsb, (i * 2 + s) * 2 + 6)
                    pool.dma_start(t["modrep"][0:P, bass.ds(col, CW)], rep[s][:, :]).then_inc(s_stored, 16)
                    pool.dma_start(t["modrep"][P:P + NS, bass.ds(col, CW)], reps[s][:, :]).then_inc(s_stored, 16)
                    pool.wait_ge(s_stored, (i * 2 + s) * 32 + 32)
                    pool.sem_inc(rep_free, 1)


def norm_modulate(pr, tag, prompt_src, sample_src, gain, scale_ix, shift_ix, h_hi, h_lo, ht=None):
    nc, t = pr.nc, pr.t
    TILES = PT + 1
    x_in = [pr.sem(f"{tag}_xin{j}") for j in range(PT // 2 + 1)]
    (mod_in, gmod, sq, ms, ln, rexp, newton, scaled, h_ready, turned, hi_done, lo_done, passed) = (
        pr.sem(f"{tag}_{n}") for n in ("modin", "gmod", "sq", "ms", "ln", "rexp", "newton", "scaled", "hready",
                                       "turned", "hidone", "lodone", "passed"))
    with ExitStack() as cx:
        sb = lambda name, shape: cx.enter_context(nc.sbuf_tensor(f"{tag}_{name}", shape, F32))
        x = sb("x", [P, TILES, D])
        h = [sb(f"h{s}", [P, D]) for s in range(2)]
        junk = sb("junk", [P, D])
        g_b = sb("g", [P, D])
        scl, shf = [sb(f"scl{r}", [P, D]) for r in range(2)], [sb(f"shf{r}", [P, D]) for r in range(2)]
        ssq, mean, log, root, factor, rstd = (sb(n, [P, TILES]) for n in ("ssq", "mean", "log", "root", "factor", "rstd"))
        p_t = [cx.enter_context(nc.psum_tensor(f"{tag}_pt{s}", [P, KD, P], F32)) for s in range(2)]
        block = cx.enter_context(nc.Block(tag))

        def tiles(eng, tile):
            with eng.Fori(0, PT // 2) as i:
                for s in range(2):
                    tile(i * 2 + s, s, P)
            tile(PT, 0, NS)

        @block.sync
        def _(sp):
            for j in range(PT // 2):
                sp.dma_start(x[:, 2 * j:2 * j + 2, :], prompt_src[2 * j * P:(2 * j + 2) * P].rearrange("(m p) d -> p m d", p=P))\
                    .then_inc(x_in[j], 16)
            sp.dma_start(x[0:NS, PT, :], sample_src).then_inc(x_in[PT // 2], 16)
            sp.dma_start(g_b[:, :], gain.partition_broadcast(P)).then_inc(mod_in, 16)
            for r, (a, n) in enumerate(((0, P), (P, NS))):
                for buf, ix in ((scl, scale_ix), (shf, shift_ix)):
                    sp.dma_start(buf[r][0:n, :], t["modrep"][a:a + n, ix * D:(ix + 1) * D]).then_inc(mod_in, 16)

        @block.scalar
        def _(act):
            act.wait_ge(sq, 1)
            for n in range(TILES):
                rows = P if n < PT else NS
                act.wait_ge(x_in[n // 2], 16)
                nc.scalar.activation(junk[0:rows, :], x[0:rows, n, :], ACT.Square, accum_out=ssq[0:rows, n:n + 1]).then_inc(sq, 1)
                act.wait_ge(sq, n + 2)
            act.wait_ge(ms, 1)
            nc.scalar.activation(log[:, :], mean[:, :], ACT.Ln).then_inc(ln, 1)
            act.wait_ge(ln, 1)
            nc.scalar.activation(root[:, :], log[:, :], ACT.Exp, scale=-0.5).then_inc(rexp, 1)

            def evacuate(n, s, rows):
                act.wait_ge(turned, n + 3)
                if ht is not None:
                    nc.scalar.copy(ht[:, :, bass.ds(n * P, rows)], p_t[s][:, :, 0:rows])
                nc.scalar.copy(h_hi[:, :, bass.ds(n * P, rows)], p_t[s][:, :, 0:rows]).then_inc(hi_done, 1)

            tiles(act, evacuate)

        @block.vector
        def _(dve):
            nc.vector.memset(ssq[:, :], 1.0).then_inc(sq, 1)
            dve.wait_ge(sq, TILES + 1)
            nc.vector.tensor_scalar(mean[:, :], ssq[:, :], 1.0 / D, EPS, ALU.mult, ALU.add).then_inc(ms, 1)
            dve.wait_ge(mod_in, 16 * 5)
            for r, n in ((0, P), (1, NS)):
                nc.vector.scalar_tensor_tensor(scl[r][0:n, :], scl[r][0:n, :], 1.0, g_b[0:n, :],
                                               ALU.add, ALU.mult).then_inc(gmod, 1)
            dve.wait_ge(gmod, 2)
            dve.wait_ge(ms, 1)
            dve.wait_ge(rexp, 1)
            step = Ordered(dve, newton)
            step(nc.vector.tensor_tensor(factor[:, :], root[:, :], root[:, :], ALU.mult))
            step(nc.vector.tensor_tensor(factor[:, :], factor[:, :], mean[:, :], ALU.mult))
            step(nc.vector.tensor_scalar(factor[:, :], factor[:, :], -0.5, 1.5, ALU.mult, ALU.add))
            step(nc.vector.tensor_tensor(rstd[:, :], root[:, :], factor[:, :], ALU.mult))

            def modulate(n, s, rows, r):
                dve.wait_ge(turned, n + 1)
                nc.vector.scalar_tensor_tensor(h[s][0:rows, :], x[0:rows, bass.ds(n, 1), :].rearrange("p a d -> p (a d)"),
                                               rstd[0:rows, bass.ds(n, 1)], scl[r][0:rows, :], ALU.mult, ALU.mult)\
                    .then_inc(scaled, 1)

            def low_part(n, s, rows):
                dve.wait_ge(hi_done, n + 1)
                cols = bass.ds(n * P, rows)
                nc.vector.tensor_tensor(h_lo[:, :, cols], p_t[s][:, :, 0:rows], h_hi[:, :, cols], ALU.subtract).then_inc(lo_done, 1)

            dve.sem_inc(lo_done, 2)
            for s in range(2):
                modulate(s, s, P, 0)
            with dve.Fori(0, PT // 2 - 1) as i:
                for s in range(2):
                    modulate(i * 2 + (s + 2), s, P, 0)
                    low_part(i * 2 + s, s, P)
            modulate(PT, 0, NS, 1)
            for n in range(PT - 2, TILES):
                low_part(n, n % 2, P if n < PT else NS)

        @block.gpsimd
        def _(pool):
            pool.wait_ge(mod_in, 16 * 5)

            def shift(n, s, rows):
                pool.wait_ge(scaled, n + 1)
                pool.sem_inc(passed, 1)
                nc.gpsimd.tensor_tensor(h[s][0:rows, :], h[s][0:rows, :], shf[0 if rows == P else 1][0:rows, :], ALU.add)\
                    .then_inc(h_ready, 1)

            tiles(pool, shift)

        @block.tensor
        def _(pe):
            pe.sem_inc(turned, 2)

            def turn(n, s, rows):
                pe.wait_ge(h_ready, n + 1)
                pe.wait_ge(lo_done, n + 1)
                for k in range(KD):
                    tr = nc.tensor.transpose(p_t[s][:, k, 0:rows], h[s][0:rows, k * P:(k + 1) * P],
                                             pr.c("ident")[0:rows, 0:rows])
                tr.then_inc(turned, 1)

            tiles(pe, turn)


def window_copies(pr):
    t, copies = pr.t, []
    flat = lambda x: x.rearrange("b w h d -> b w (h d)")
    for g, (w, _) in enumerate(GROUPS):
        for name, col in (("k", C_K), ("v", C_V)):
            cols = slice(col + g * GW, col + (g + 1) * GW)
            dst, old = flat(t[f"{name}{g}_s"][0]), flat(t[f"cache_{name}{g}"][0])
            each = 2 if w > 128 else NB
            copies += [(flat(t[f"{name}{g}_p"][0])[0], t["proj_n"][SEQ - w:SEQ, cols]),
                       (dst[:, w - NT:], t["proj_n"][SEQ:TOK, cols].rearrange("(b t) c -> b t c", t=NT))]
            copies += [(dst[b:b + each, 0:w - NT], old[b:b + each, NT:]) for b in range(0, NB, each)]
    return copies


def chunks_ahead(eng, chunks, step):
    with eng.Fori(0, chunks // 2 - 1) as i:
        for s in range(2):
            step(i * 2 + s, s, True)
    step(chunks - 2, 0, True)
    step(chunks - 1, 1, False)


def project_features(pr, tag, h_hi, h_lo, w_v, col0, cols, dst, row0, cw, windows=False):
    nc = pr.nc
    ct, chunks = cw // P, cols // cw
    assert chunks % 2 == 0 and chunks * cw == cols
    w_in = [pr.sem(f"{tag}_win{s}") for s in range(2)]
    hi_done, lo_done, product, evacuated, stored, st_free, copied = (pr.sem(f"{tag}_{n}") for n in (
        "hi", "lo", "product", "evac", "stored", "stfree", "copied"))
    with ExitStack() as cx:
        w = [cx.enter_context(nc.sbuf_tensor(f"{tag}_w{s}", [P, KD, cw], F32)) for s in range(2)]
        w_hi, w_lo = ([cx.enter_context(nc.sbuf_tensor(f"{tag}_{n}{s}", [P, KD, cw], F16)) for s in range(2)]
                      for n in ("whi", "wlo"))
        st = [cx.enter_context(nc.sbuf_tensor(f"{tag}_st{s}", [P, TOK], F32)) for s in range(2)]
        ps = [cx.enter_context(nc.psum_tensor(f"{tag}_ps{s}", [P, 3 * 512], F32)) for s in range(2)]
        block = cx.enter_context(nc.Block(tag))

        @block.sync
        def _(sp):
            def load(c, s):
                sp.dma_start(w[s][:, :, :], w_v[:, :, bass.ds(c * cw + col0, cw)]).then_inc(w_in[s], 16)

            for s in range(2):
                load(s, s)
            copies = window_copies(pr) if windows else []
            each = -(-len(copies) // (chunks - 1))
            for c in range(2, chunks + 1):
                sp.wait_ge(lo_done, c - 1)
                if c < chunks:
                    load(c, c % 2)
                for out, src in copies[(c - 2) * each:(c - 1) * each]:
                    sp.dma_start(out, src).then_inc(copied, 16)
            if windows:
                sp.wait_ge(copied, 16 * len(copies))

        @block.tensor
        def _(pe):
            with pe.Fori(0, chunks // 2) as i:
                for s in range(2):
                    pe.wait_ge(hi_done, i * 2 + s + 1)
                    pe.wait_ge(lo_done, i * 2 + s + 1)
                    for j in range(ct):
                        n, b = (i * 2 + s) * ct + j, (s * ct + j) % 2
                        pe.wait_ge(evacuated, n + 1)
                        mms = [(x, h, k) for k in range(KD) for x, h in ((w_hi, h_hi), (w_hi, h_lo), (w_lo, h_hi))]
                        for q, (x, h, k) in enumerate(mms):
                            for a in range(0, TOK, 512):
                                e = min(a + 512, TOK)
                                mm = nc.tensor.matmul(ps[b][:, a:e], x[s][:, k, j * P:(j + 1) * P], h[:, k, a:e],
                                                      start=(q == 0), stop=(q == len(mms) - 1))
                        mm.then_inc(product, 1)

        @block.scalar
        def _(act):
            act.sem_inc(evacuated, 2)
            act.sem_inc(product, 2 * ct)

            def high(c, s):
                act.wait_ge(w_in[s], (c - s) * 8 + 16)
                act.wait_ge(product, (c + 1) * ct)
                nc.scalar.activation(w_hi[s][:, :, :], w[s][:, :, :], ACT.Copy, scale=SPLIT).then_inc(hi_done, 1)

            def step(c, s, more):
                if more:
                    high(c + 1, 1 - s)
                for j in range(ct):
                    n, m = c * ct + j, (s * ct + j) % 2
                    act.wait_ge(product, n + 2 * ct + 1)
                    act.wait_ge(st_free, n + 1)
                    nc.scalar.activation(st[m][:, :], ps[m][:, 0:TOK], ACT.Copy, scale=1.0 / SPLIT).then_inc(evacuated, 1)

            high(0, 0)
            chunks_ahead(act, chunks, step)

        @block.vector
        def _(dve):
            def low(c, s):
                dve.wait_ge(hi_done, c + 1)
                nc.vector.scalar_tensor_tensor(w_lo[s][:, :, :], w[s][:, :, :], SPLIT, w_hi[s][:, :, :],
                                               ALU.mult, ALU.subtract).then_inc(lo_done, 1)

            with dve.Fori(0, chunks // 2) as i:
                for s in range(2):
                    low(i * 2 + s, s)

        @block.gpsimd
        def _(pool):
            pool.sem_inc(st_free, 2)
            with pool.Fori(0, chunks // 2) as i:
                for m in range(2 * ct):
                    n = i * 2 * ct + m
                    pool.wait_ge(evacuated, n + 3)
                    pool.dma_start(dst[bass.ds(n * P + row0, P), :], st[m % 2][:, :]).then_inc(stored, 16)
                    pool.wait_ge(stored, n * 16 + 16)
                    pool.sem_inc(st_free, 1)


def project_tokens(pr, h_hi, h_lo, w_v):
    nc, t = pr.nc, pr.t
    cw = 416
    chunks = NATC // cw
    assert chunks % 2 == 0 and chunks * cw == NATC
    tiles = PT + 1
    banks = 6
    w_in = [pr.sem(f"pn_win{s}") for s in range(2)]
    hi_done, lo_done, product, evacuated, stored, st_free = (pr.sem(f"pn_{n}") for n in (
        "hi", "lo", "product", "evac", "stored", "stfree"))
    with ExitStack() as cx:
        w = [cx.enter_context(nc.sbuf_tensor(f"pn_w{s}", [P, KD, cw], F32)) for s in range(2)]
        w_hi, w_lo = ([cx.enter_context(nc.sbuf_tensor(f"pn_{n}{s}", [P, KD, cw], F16)) for s in range(2)] for n in ("whi", "wlo"))
        st = [cx.enter_context(nc.sbuf_tensor(f"pn_st{s}", [P, tiles, cw], F32)) for s in range(2)]
        ps = cx.enter_context(nc.psum_tensor("pn_ps", [P, banks, 512], F32))
        block = cx.enter_context(nc.Block("project_tokens"))

        @block.sync
        def _(sp):
            def load(c, s):
                sp.dma_start(w[s][:, :, :], w_v[:, :, bass.ds(c * cw, cw)]).then_inc(w_in[s], 16)

            for s in range(2):
                load(s, s)
            with sp.Fori(1, chunks // 2) as i:
                for s in range(2):
                    sp.wait_ge(lo_done, i * 2 + s - 1)
                    load(i * 2 + s, s)

        @block.scalar
        def _(act):
            act.sem_inc(product, 2 * tiles)
            with act.Fori(0, chunks // 2) as i:
                for s in range(2):
                    act.wait_ge(w_in[s], i * 16 + 16)
                    act.wait_ge(product, (i * 2 + s + 1) * tiles)
                    nc.scalar.activation(w_hi[s][:, :, :], w[s][:, :, :], ACT.Copy, scale=SPLIT).then_inc(hi_done, 1)

        @block.tensor
        def _(pe):
            with pe.Fori(0, chunks // 2) as i:
                for s in range(2):
                    pe.wait_ge(hi_done, i * 2 + s + 1)
                    pe.wait_ge(lo_done, i * 2 + s + 1)
                    for m in range(tiles):
                        rows = P if m < PT else NS
                        b = (s * tiles + m) % banks
                        pe.wait_ge(evacuated, (i * 2 + s) * tiles + m + 1)
                        mms = [(h, x, k) for k in range(KD) for h, x in ((h_hi, w_hi), (h_hi, w_lo), (h_lo, w_hi))]
                        for q, (h, x, k) in enumerate(mms):
                            mm = nc.tensor.matmul(ps[0:rows, b, 0:cw], h[:, k, m * P:m * P + rows], x[s][:, k, :],
                                                  start=(q == 0), stop=(q == len(mms) - 1))
                        mm.then_inc(product, 1)

        @block.vector
        def _(dve):
            dve.sem_inc(evacuated, banks)

            def low(c, s):
                dve.wait_ge(hi_done, c + 1)
                nc.vector.scalar_tensor_tensor(w_lo[s][:, :, :], w[s][:, :, :], SPLIT, w_hi[s][:, :, :],
                                               ALU.mult, ALU.subtract).then_inc(lo_done, 1)

            def step(c, s, more):
                if more:
                    low(c + 1, 1 - s)
                dve.wait_ge(st_free, c + 1)
                for m in range(tiles):
                    rows = P if m < PT else NS
                    dve.wait_ge(product, (c + 2) * tiles + m + 1)
                    nc.vector.tensor_scalar(st[s][0:rows, m, :], ps[0:rows, (s * tiles + m) % banks, 0:cw], 1.0 / SPLIT,
                                            None, ALU.mult).then_inc(evacuated, 1)

            low(0, 0)
            chunks_ahead(dve, chunks, step)

        @block.gpsimd
        def _(pool):
            pool.sem_inc(st_free, 2)
            with pool.Fori(0, chunks // 2) as i:
                for s in range(2):
                    c = i * 2 + s
                    pool.wait_ge(evacuated, (c + 1) * tiles + banks)
                    cols = bass.ds(c * cw, cw)
                    pool.dma_start(t["proj_n"][0:SEQ, cols].rearrange("(m p) c -> p m c", p=P),
                                   st[s][:, 0:PT, :]).then_inc(stored, 16)
                    pool.dma_start(t["proj_n"][SEQ:TOK, cols], st[s][0:NS, PT, :]).then_inc(stored, 16)
                    pool.wait_ge(stored, c * 32 + 32)
                    pool.sem_inc(st_free, 1)


def mixer_input(pr):
    nc, t = pr.nc, pr.t
    w_v = t["w_in"][0].rearrange("(k p) n -> p k n", p=P)
    with nc.sbuf_tensor("h_hi1", [P, KD, TOK], F16) as h_hi, nc.sbuf_tensor("h_lo1", [P, KD, TOK], F16) as h_lo:
        norm_modulate(pr, "n1", t["x_prompt"][0], t["x_sample"].rearrange("b t d -> (b t) d"), t["norm1_g"][0],
                      1, 0, h_hi, h_lo)
        project_tokens(pr, h_hi, h_lo, w_v)
        project_features(pr, "pt", h_hi, h_lo, w_v, C_ZQ, TRC, t["proj_t"], 0, 3 * P, windows=True)


def attention_prompt(pr):
    nc, t = pr.nc, pr.t
    BLK, RING = 8, 4
    (tr, qkt, scored, t_done, mstep, m_ready, exp_done, p_turned, pt_ready, pv_done, ml_done, o_done,
     stored, rec_free, zeroed) = (pr.sem(f"ap_{n}") for n in (
         "tr", "qkt", "scored", "tdone", "mstep", "mready", "exp", "pturned", "ptready", "pv", "ml", "o",
         "stored", "recfree", "zeroed"))
    qkv_in = [pr.sem(f"ap_in{s}") for s in range(RING)]
    src = t["proj_n"][0:SEQ, 0:3 * AW].rearrange("s (j g c) -> s j g c", j=3, g=3)

    def rows_of(view, g, i, b):
        if g == 0:
            return [(0, P, view[bass.ds(i * (RING * P) + b * P, P)])]
        if g == 1:
            v = view.rearrange("(n p r) a b -> n r p a b", p=P, r=4)
            return [(0, P, v[b % 2, i * 2 + b // 2])]
        v = view.rearrange("(u r) a b -> r u a b", r=16)
        return [(64 * e, 64 * e + 64, v[i * 8 + 2 * b + e]) for e in range(2)]

    def bank_of(h):
        return h % 2 * 2 + h // 2

    def has_prev(g, b):
        return g == 0 or (g == 1 and b % 2 == 1)

    with ExitStack() as cx:
        sb = lambda name, shape: cx.enter_context(nc.sbuf_tensor(f"ap_{name}", shape, F32))
        ps = lambda name, shape: cx.enter_context(nc.psum_tensor(f"ap_{name}", shape, F32))
        qkv = [sb(f"qkv{s}", [P, 3, GW]) for s in range(RING)]
        qk_t = [sb(f"qkt{s}", [P, 4, P]) for s in range(RING)]
        sc = [sb(f"sc{s}", [P, HPG, 2 * P]) for s in range(2)]
        pr_ = [sb(f"p{s}", [P, HPG, 2 * P]) for s in range(2)]
        p_t = [sb(f"pt{s}", [P, 2 * HPG, P]) for s in range(2)]
        m8 = [sb(f"m8{s}", [P, HPG]) for s in range(2)]
        nb = [sb(f"nb{s}", [P, HPG]) for s in range(2)]
        den = [sb(f"den{s}", [P, HPG]) for s in range(2)]
        rec = [sb(f"rec{s}", [P, HPG, REC]) for s in range(2)]
        ps_tr = ps("ps_tr", [P, 4, P])
        ps_s = ps("ps_s", [P, HPG, 2 * P])
        ps_pt = ps("ps_pt", [P, 2 * HPG, P])
        ps_o = [ps(f"ps_o{s}", [P, HPG, DH]) for s in range(2)]
        block = cx.enter_context(nc.Block("attention_prompt"))

        def turns(eng, body):
            for g in range(3):
                with eng.Fori(0, BLK // RING) as i:
                    body(g, i, i * RING + BLK * g)

        @block.sync
        def _(sp):
            def body(g, i, n0):
                for b in range(RING):
                    sp.wait_ge(pv_done, n0 + b + 1)
                    for a, e, rows in rows_of(src[:, :, g, :], g, i, b):
                        sp.dma_start(qkv[b][a:e, :, :], rows).then_inc(qkv_in[b], 16)

            sp.wait_ge(zeroed, 2)
            turns(sp, body)

        @block.tensor
        def _(pe):
            def turn(g, i, n0, b):
                n = n0 + b
                each = 16 if g < 2 else 32
                pe.wait_ge(qkv_in[b], i * each + each + 32 * g)
                pe.wait_ge(qkt, n + 1)
                for j in range(4):
                    mm = nc.tensor.transpose(ps_tr[:, j, :], qkv[b][:, j // 2, (j % 2) * P:(j % 2 + 1) * P],
                                             pr.c("ident"))
                mm.then_inc(tr, 1)

            def score(g, i, n0, b):
                n = n0 + b
                pe.wait_ge(qkt, n + 2)
                pe.wait_ge(t_done, n + 1)
                for h in range(HPG):
                    a, hp = 64 * (h % 2), h // 2
                    for kb in range(0 if has_prev(g, b) else 1, 2):
                        keys = qk_t[b if kb else (b - 1) % RING]
                        mm = nc.tensor.matmul(ps_s[:, bank_of(h), kb * P:(kb + 1) * P], qk_t[b][a:a + 64, hp, :],
                                              keys[a:a + 64, 2 + hp, :], start=True, stop=True)
                mm.then_inc(scored, 1)

            def keys_of(g, b):
                return range(0 if has_prev(g, b) else 1, 2)

            def turn_probs(g, i, n0, b):
                n, s, kbs = n0 + b, b % 2, keys_of(g, b)
                pe.wait_ge(exp_done, n + 3)
                pe.wait_ge(pt_ready, n + 1)
                for h in range(HPG):
                    for kb in kbs:
                        mm = nc.tensor.transpose(ps_pt[:, 2 * h + kb, :], pr_[s][:, h, kb * P:(kb + 1) * P],
                                                 pr.c("ident"))
                mm.then_inc(p_turned, 1)

            def values(g, i, n0, b):
                n, s, kbs = n0 + b, b % 2, keys_of(g, b)
                pe.wait_ge(pt_ready, n + 2)
                pe.wait_ge(o_done, n + 1)
                for h in range(HPG):
                    for kb in kbs:
                        v = qkv[b if kb else (b - 1) % RING][:, 2, h * DH:(h + 1) * DH]
                        mm = nc.tensor.matmul(ps_o[s][:, h, :], p_t[s][:, 2 * h + kb, :], v,
                                              start=(kb == kbs[0]), stop=(kb == 1))
                mm.then_inc(pv_done, 1)

            def body(g, i, n0):
                for b in range(2):
                    turn(g, i, n0, b)
                    score(g, i, n0, b)
                for b in range(RING):
                    turn_probs(g, i, n0, b)
                    if b + 2 < RING:
                        turn(g, i, n0, b + 2)
                    values(g, i, n0, b)
                    if b + 2 < RING:
                        score(g, i, n0, b + 2)

            pe.sem_inc(scored, 3)
            pe.sem_inc(p_turned, 2)
            pe.sem_inc(pv_done, 3)
            turns(pe, body)

        @block.scalar
        def _(act):
            def turned(g, i, n0, b):
                n = n0 + b
                act.wait_ge(tr, n + 1)
                act.wait_ge(scored, n + 1)
                nc.scalar.copy(qk_t[b][:, :, :], ps_tr[:, :, :]).then_inc(qkt, 1)

            def exps(g, i, n0, b):
                n, s = n0 + b, b % 2
                k0 = 0 if has_prev(g, b) else P
                act.wait_ge(m_ready, n + 1)
                act.wait_ge(p_turned, n + 1)
                act.wait_ge(ml_done, n + 1)
                for h in range(HPG):
                    ex = nc.scalar.activation(pr_[s][:, h, k0:], sc[s][:, h, k0:], ACT.Exp, bias=nb[s][:, h:h + 1],
                                              scale=0.125, accum_out=den[s][:, h:h + 1])
                ex.then_inc(exp_done, 1)

            def outputs(g, i, n0, b):
                n, s = n0 + b, b % 2
                act.wait_ge(pv_done, n + 4)
                act.wait_ge(rec_free, n + 1)
                nc.scalar.copy(rec[s][:, :, 0:DH], ps_o[s][:, :, :]).then_inc(o_done, 1)

            def body(g, i, n0):
                for b in range(2):
                    turned(g, i, n0, b)
                for b in range(RING):
                    exps(g, i, n0, b)
                    if b + 2 < RING:
                        turned(g, i, n0, b + 2)
                    if b > 0:
                        outputs(g, i, n0, b - 1)
                outputs(g, i, n0, RING - 1)

            act.sem_inc(qkt, 1)
            act.sem_inc(exp_done, 2)
            act.sem_inc(o_done, 2)
            turns(act, body)

        @block.vector
        def _(dve):
            def maxima(g, i, n0, b):
                n, s = n0 + b, b % 2
                k0 = 0 if has_prev(g, b) else P
                if g == 0 and b == 0:
                    a = AT["pen0"][0]
                    pen = pr.const[:, bass.ds(i * (2 * P) + a, 2 * P)]
                else:
                    pen = pr.c(f"pen{g}")[:, -2 * P:] if g < 2 else pr.c("pen2")
                    pen = pen[:, k0:] if g < 2 else pen
                dve.wait_ge(scored, n + 4)
                dve.wait_ge(exp_done, n + 1)
                for h in range(HPG):
                    st = nc.vector.scalar_tensor_tensor(sc[s][:, h, k0:], pen, 8.0 * SLOPES[4 * g + h],
                                                        ps_s[:, bank_of(h), k0:], ALU.mult, ALU.add)
                st.then_inc(t_done, 1)
                dve.wait_ge(t_done, n + 2)
                nc.vector.tensor_reduce(m8[s][:, :], sc[s][:, :, k0:], AX, ALU.max).then_inc(mstep, 1)
                dve.wait_ge(mstep, n + 1)
                nc.vector.tensor_scalar(nb[s][:, :], m8[s][:, :], -0.125, None, ALU.mult).then_inc(m_ready, 1)

            def probs(g, i, n0, b):
                n, s = n0 + b, b % 2
                dve.wait_ge(p_turned, n + 3)
                dve.wait_ge(pv_done, n + 2)
                if has_prev(g, b):
                    cp = nc.vector.tensor_copy(p_t[s][:, :, :], ps_pt[:, :, :])
                else:
                    half = lambda x: x.rearrange("p (h k) q -> p h k q", k=2)[:, :, 1, :]
                    cp = nc.vector.tensor_copy(half(p_t[s][:, :, :]), half(ps_pt[:, :, :]))
                cp.then_inc(pt_ready, 1)
                dve.wait_ge(rec_free, n + 1)
                nc.vector.tensor_copy(rec[s][:, :, DH], m8[s][:, :])
                nc.vector.tensor_copy(rec[s][:, :, DH + 1], den[s][:, :]).then_inc(ml_done, 1)

            def body(g, i, n0):
                for b in range(2):
                    maxima(g, i, n0, b)
                for b in range(RING):
                    probs(g, i, n0, b)
                    if b + 2 < RING:
                        maxima(g, i, n0, b + 2)

            nc.vector.memset(qkv[RING - 1][:, :, :], 0.0).then_inc(zeroed, 1)
            nc.vector.memset(qk_t[RING - 1][:, :, :], 0.0).then_inc(zeroed, 1)
            dve.sem_inc(t_done, 1)
            dve.sem_inc(pt_ready, 1)
            dve.sem_inc(ml_done, 2)
            turns(dve, body)

        @block.gpsimd
        def _(pool):
            def body(g, i, n0):
                for b in range(RING):
                    n, s = n0 + b, b % 2
                    pool.wait_ge(o_done, n + 3)
                    pool.wait_ge(ml_done, n + 3)
                    for a, e, rows in rows_of(t["att_rec"][g, 0:SEQ].rearrange("s (h c) -> s h c", h=HPG), g, i, b):
                        pool.dma_start(rows, rec[s][a:e, :, :]).then_inc(stored, 16)
                    pool.wait_ge(stored, stores(g, i, b))
                    pool.sem_inc(rec_free, 1)

            def stores(g, i, b):
                each = 16 if g < 2 else 32
                return i * (RING * each) + (b + 1) * each + BLK * 16 * g

            pool.sem_inc(rec_free, 2)
            turns(pool, body)


def attention_merge(pr):
    nc, t = pr.nc, pr.t
    (top, diff, w_done, den, rden, wn, prod, att, turned, evac, stored, tfree) = (pr.sem(f"am_{n}") for n in (
        "top", "diff", "w", "den", "rden", "wn", "prod", "att", "turned", "evac", "stored", "tfree"))
    wl_done = pr.sem("am_wl")
    rec_in = [pr.sem(f"am_in{s}") for s in range(2)]
    with ExitStack() as cx:
        sb = lambda name, shape: [cx.enter_context(nc.sbuf_tensor(f"am_{name}{s}", shape, F32)) for s in range(2)]
        rec = sb("rec", [P, 3, HPG, REC])
        mx, de, re = sb("mx", [P, HPG]), sb("de", [P, HPG]), sb("re", [P, HPG])
        w, wl = sb("w", [P, 3, HPG]), sb("wl", [P, 3, HPG])
        o3, at, at_t = sb("o3", [P, 3, HPG, DH]), sb("at", [P, GW]), sb("att", [P, 2, P])
        ps = [cx.enter_context(nc.psum_tensor(f"am_ps{s}", [P, 2, P], F32)) for s in range(2)]
        block = cx.enter_context(nc.Block("attention_merge"))
        src = t["att_rec"].rearrange("g t c -> t g c")
        sample = t["sample_rec"].rearrange("g (b h t) c -> g b h t c", h=HPG, t=NT)
        dst = t["att_t"].rearrange("(k p) t -> p k t", p=P)

        def tiles(eng, tile):
            with eng.Fori(0, PT // 2) as i:
                for s in range(2):
                    tile(i * 2 + s, s, i, P)
            tile(PT, 0, PT // 2, NS)

        @block.sync
        def _(sp):
            def load(n, s, i, rows):
                sp.wait_ge(prod, n + 1)
                if rows == P:
                    sp.dma_start(rec[s][:, :, :, :].rearrange("p g h c -> p g (h c)"), src[bass.ds(n * P, P)])\
                        .then_inc(rec_in[s], 16)
                    return
                for g in range(3):
                    for h in range(HPG):
                        sp.dma_start(rec[s][0:NS, g, h, :], sample[g, :, h]).then_inc(rec_in[s], 16)
            tiles(sp, load)

        @block.vector
        def _(dve):
            def tile(n, s, i, rows):
                r = slice(0, rows)
                m = rec[s][r, :, :, DH]
                over_g = lambda x: x.unsqueeze(1).broadcast_to([rows, 3, HPG])
                dve.wait_ge(rec_in[s], i * 16 + (16 if rows == P else 16 * 3 * HPG))
                nc.vector.tensor_reduce(mx[s][r, :], m.rearrange("p g h -> p h g"), AX, ALU.max).then_inc(top, 1)
                dve.wait_ge(top, n + 1)
                nc.vector.tensor_tensor(w[s][r], m, over_g(mx[s][r, :]), ALU.subtract).then_inc(diff, 1)
                dve.wait_ge(w_done, n + 1)
                nc.vector.tensor_tensor(wl[s][r], w[s][r], rec[s][r, :, :, DH + 1], ALU.mult).then_inc(wl_done, 1)
                dve.wait_ge(wl_done, n + 1)
                nc.vector.tensor_reduce(de[s][r, :], wl[s][r].rearrange("p g h -> p h g"), AX, ALU.add).then_inc(den, 1)
                dve.wait_ge(den, n + 1)
                nc.vector.reciprocal(re[s][r, :], de[s][r, :]).then_inc(rden, 1)
                dve.wait_ge(rden, n + 1)
                nc.vector.tensor_tensor(wl[s][r], w[s][r], over_g(re[s][r, :]), ALU.mult).then_inc(wn, 1)
                dve.wait_ge(wn, n + 1)
                nc.vector.tensor_tensor(o3[s][r], rec[s][r, :, :, 0:DH],
                                        wl[s][r].unsqueeze(3).broadcast_to([rows, 3, HPG, DH]), ALU.mult)\
                    .then_inc(prod, 1)
                dve.wait_ge(prod, n + 3)
                dve.wait_ge(turned, n + 1)
                nc.vector.tensor_reduce(at[s][r, :], o3[s][r].rearrange("p g h c -> p (h c) g"), AX, ALU.add)\
                    .then_inc(att, 1)

            dve.sem_inc(prod, 2)
            tiles(dve, tile)

        @block.scalar
        def _(act):
            def tile(n, s, i, rows):
                act.wait_ge(diff, n + 1)
                nc.scalar.activation(w[s][0:rows], w[s][0:rows], ACT.Exp, scale=0.125).then_inc(w_done, 1)
                act.wait_ge(turned, n + 3)
                act.wait_ge(tfree, n + 1)
                nc.scalar.copy(at_t[s][:, :, 0:rows], ps[s][:, :, 0:rows]).then_inc(evac, 1)

            act.sem_inc(evac, 2)
            tiles(act, tile)

        @block.tensor
        def _(pe):
            def tile(n, s, i, rows):
                pe.wait_ge(att, n + 1)
                pe.wait_ge(evac, n + 1)
                for k in range(2):
                    tr = nc.tensor.transpose(ps[s][:, k, 0:rows], at[s][0:rows, k * P:(k + 1) * P],
                                             pr.c("ident")[0:rows, 0:rows])
                tr.then_inc(turned, 1)

            pe.sem_inc(turned, 2)
            tiles(pe, tile)

        @block.gpsimd
        def _(pool):
            def tile(n, s, i, rows):
                pool.wait_ge(evac, n + 3)
                pool.dma_start(dst[:, :, bass.ds(n * P, rows)], at_t[s][:, :, 0:rows]).then_inc(stored, 16)
                pool.wait_ge(stored, n * 16 + 16)
                pool.sem_inc(tfree, 1)

            pool.sem_inc(tfree, 2)
            tiles(pool, tile)


def attention_sample(pr):
    nc, t = pr.nc, pr.t
    loaded, zeroed, new_tr, new_t, stored = (pr.sem(f"as_{n}") for n in ("loaded", "zeroed", "newtr", "newt", "stored"))
    (qbd_done, ktr, kt_done, scored, t_done, mstep, m_ready, exp_done, p_turned, pt_ready, pv_done, picked,
     rec_done, rec_free) = (pr.sem(f"as_{n}") for n in (
         "qbd", "ktr", "kt", "scored", "tdone", "mstep", "mready", "exp", "pturned", "ptready", "pv", "picked",
         "rec", "recfree"))
    kv_in = [pr.sem(f"as_in{g}") for g in range(3)]
    NKB = (1, 4, 4)
    penw = sum(W_S)
    with ExitStack() as cx:
        sb = lambda name, shape: cx.enter_context(nc.sbuf_tensor(f"as_{name}", shape, F32))
        ps = lambda name, shape: cx.enter_context(nc.psum_tensor(f"as_{name}", shape, F32))
        new = sb("new", [P, 3, 3, GW])
        new_tt = sb("newt", [P, 2, 3, 2, NS])
        kc = [sb(f"k{g}", [P, 4, NKB[g] * GW]) for g in range(3)]
        vc = [sb(f"v{g}", [P, 4, NKB[g] * GW]) for g in range(3)]
        qbd = [sb(f"qbd{g}", [P, 2, 4, HPG, NT]) for g in range(3)]
        k_t = [sb(f"kt{s}", [P, 2, 512]) for s in range(2)]
        sc, prob = sb("sc", [P, 576]), sb("prob", [P, 640])
        p_t = sb("pt", [P, 5, P])
        m8, nb, den = sb("m8", [P, 1]), sb("nb", [P, 1]), sb("den", [P, 1])
        pick, rec = sb("pick", [P, HPG, DH]), sb("rec", [P, REC])
        ps_k = ps("ps_k", [P, 2, 512])
        ps_s, ps_n = ps("ps_s", [P, 512]), ps("ps_n", [P, 512])
        ps_pt, ps_o = ps("ps_pt", [P, 5, P]), ps("ps_o", [P, GW])
        block = cx.enter_context(nc.Block("attention_sample"))

        @block.sync
        def _(sp):
            sp.dma_start(new[0:NS], t["proj_n"][SEQ:TOK, 0:3 * AW].rearrange("s (j g c) -> s j g c", j=3, g=3))\
                .then_inc(loaded, 16)
            with sp.Fori(0, 2) as i:
                for g in range(3):
                    sp.wait_ge(pv_done, i * 3 + g + 1)
                    for buf, name in ((kc, "k"), (vc, "v")):
                        src = t[f"cache_{name}{g}"][0].rearrange("b w h d -> b w (h d)")[bass.ds(i * 4, 4)]
                        if g == 0:
                            sp.dma_start(buf[g][:, :, :], src.rearrange("b p c -> p b c")).then_inc(kv_in[g], 16)
                        elif g == 1:
                            sp.dma_start(buf[g][:, :, :], src.rearrange("b (p k) c -> p b (k c)", p=P)).then_inc(kv_in[g], 16)
                        else:
                            v = src.rearrange("b (u r) c -> u b (r c)", r=16)
                            for e in range(2):
                                sp.dma_start(buf[g][64 * e:64 * e + 64, :, :],
                                             v[:, :, e * 4 * GW:(e + 1) * 4 * GW]).then_inc(kv_in[g], 16)

        @block.tensor
        def _(pe):
            pe.wait_ge(loaded, 16)
            for g in range(3):
                for j in range(4):
                    mm = nc.tensor.transpose(ps_k[:, 0, j * NS:(j + 1) * NS],
                                             new[0:NS, j // 2, g, (j % 2) * P:(j % 2 + 1) * P], pr.c("ident")[0:NS, 0:NS])
                mm.then_inc(new_tr, 1)
                pe.wait_ge(new_t, g + 1)
            pe.sem_inc(pv_done, 3)
            pe.sem_inc(scored, 2)
            with pe.Fori(0, 2) as i:
                for g in range(3):
                    n, nk, w = i * 3 + g, NKB[g], NKB[g] * P
                    pe.wait_ge(kv_in[g], i * (64 if g == 2 else 32) + (64 if g == 2 else 32))
                    pe.wait_ge(qbd_done, n + 1)
                    pe.wait_ge(t_done, n + 1)
                    for b in range(4):
                        q = n * 4 + b
                        pe.wait_ge(kt_done, q + 1)
                        for hp in range(2):
                            for kb in range(nk):
                                a = kb * GW + hp * P
                                mm = nc.tensor.transpose(ps_k[:, hp, kb * P:(kb + 1) * P], kc[g][:, b, a:a + P],
                                                         pr.c("ident"))
                        mm.then_inc(ktr, 1)
                        pe.wait_ge(kt_done, q + 2)
                        rows = slice(32 * b, 32 * b + 32)
                        for hp in range(2):
                            lhs = qbd[g][:, hp, b].rearrange("p h t -> p (h t)")
                            nc.tensor.matmul(ps_s[rows, 0:w], lhs, k_t[b % 2][:, hp, 0:w], start=(hp == 0), stop=(hp == 1))
                        for hp in range(2):
                            lhs = qbd[g][:, hp, b].rearrange("p h t -> p (h t)")
                            mm = nc.tensor.matmul(ps_n[rows, 0:NS], lhs, new_tt[:, 1, g, hp, :], start=(hp == 0), stop=(hp == 1))
                        mm.then_inc(scored, 1)
                    pe.wait_ge(exp_done, n + 1)
                    pe.wait_ge(pt_ready, n + 1)
                    for kb in range(nk + 1):
                        mm = nc.tensor.transpose(ps_pt[:, kb, :], prob[:, kb * P:(kb + 1) * P], pr.c("ident"))
                    mm.then_inc(p_turned, 1)
                    pe.wait_ge(pt_ready, n + 2)
                    pe.wait_ge(picked, n + 1)
                    for b in range(4):
                        rows = slice(32 * b, 32 * b + 32)
                        for kb in range(nk + 1):
                            rhs = vc[g][:, b, kb * GW:(kb + 1) * GW] if kb < nk else new[:, 2, g, :]
                            mm = nc.tensor.matmul(ps_o[rows, :], p_t[:, kb, rows], rhs, start=(kb == 0), stop=(kb == nk))
                    mm.then_inc(pv_done, 1)

        @block.scalar
        def _(act):
            act.sem_inc(kt_done, 1)
            with act.Fori(0, 2) as i:
                for g in range(3):
                    n, w = i * 3 + g, NKB[g] * P
                    for b in range(4):
                        q = n * 4 + b
                        act.wait_ge(ktr, q + 1)
                        act.wait_ge(scored, q + 1)
                        nc.scalar.copy(k_t[b % 2][:, :, 0:w], ps_k[:, :, 0:w]).then_inc(kt_done, 1)
                    act.wait_ge(m_ready, n + 1)
                    nc.scalar.activation(prob[:, 0:w + NS], sc[:, 0:w + NS], ACT.Exp, bias=nb[:, :], scale=0.125,
                                         accum_out=den[:, :]).then_inc(exp_done, 1)

        @block.vector
        def _(dve):
            nc.vector.memset(prob[:, :], 0.0).then_inc(zeroed, 1)
            nc.vector.memset(new[NS:P], 0.0).then_inc(zeroed, 1)
            for g in range(3):
                nc.vector.memset(qbd[g][:, :, :, :, :], 0.0).then_inc(zeroed, 1)
            dve.wait_ge(zeroed, 5)
            for g in range(3):
                dve.wait_ge(new_tr, g + 1)
                nc.vector.tensor_copy(new_tt[:, :, g, :, :],
                                      ps_k[:, 0, 0:4 * NS].rearrange("p (j h t) -> p j h t", j=2, h=2)).then_inc(new_t, 1)
            dve.wait_ge(new_t, 3)
            dve.sem_inc(t_done, 1)
            dve.sem_inc(pt_ready, 1)
            dve.sem_inc(picked, 1)
            with dve.Fori(0, 2) as i:
                for g in range(3):
                    n, nk, w = i * 3 + g, NKB[g], NKB[g] * P
                    dve.wait_ge(scored, n * 4 + 2)
                    for h in range(HPG):
                        e, hp = 64 * (h % 2), h // 2
                        cp = nc.vector.tensor_copy(qbd[g][e:e + 64, hp, :, h, :], new_tt[
                            e:e + 64, 0, g, hp, bass.ds(i * 32, 32)].rearrange("p (b t) -> p b t", b=4))
                    cp.then_inc(qbd_done, 1)
                    dve.wait_ge(scored, n * 4 + 6)
                    slope = pr.c("slope_s")[:, g:g + 1]
                    a = AT[f"pens0{g}"][0]
                    pen = lambda at, width: pr.const[:, bass.ds(i * penw + a + at, width)]
                    dve.wait_ge(pv_done, n + 3)
                    nc.vector.scalar_tensor_tensor(sc[:, 0:w], pen(0, w), slope, ps_s[:, 0:w], ALU.mult, ALU.add)\
                        .then_inc(mstep, 1)
                    nc.vector.scalar_tensor_tensor(sc[:, w:w + NS], pen(w, NS), slope, ps_n[:, 0:NS], ALU.mult, ALU.add)\
                        .then_inc(t_done, 1)
                    dve.wait_ge(mstep, n * 2 + 1)
                    dve.wait_ge(t_done, n + 2)
                    nc.vector.tensor_reduce(m8[:, :], sc[:, 0:w + NS], AX, ALU.max).then_inc(mstep, 1)
                    dve.wait_ge(mstep, n * 2 + 2)
                    nc.vector.tensor_scalar(nb[:, :], m8[:, :], -0.125, None, ALU.mult).then_inc(m_ready, 1)
                    dve.wait_ge(p_turned, n + 1)
                    nc.vector.tensor_copy(p_t[:, 0:nk + 1, :], ps_pt[:, 0:nk + 1, :]).then_inc(pt_ready, 1)
                    dve.wait_ge(pv_done, n + 4)
                    nc.vector.tensor_tensor(pick[:, :, :], ps_o[:, :].rearrange("p (h c) -> p h c", h=HPG),
                                            pr.c("headmask").unsqueeze(2).broadcast_to([P, HPG, DH]), ALU.mult)\
                        .then_inc(picked, 1)
                    dve.wait_ge(picked, n + 2)
                    dve.wait_ge(rec_free, n + 1)
                    nc.vector.tensor_reduce(rec[:, 0:DH], pick[:, :, :].rearrange("p h c -> p c h"), AX, ALU.add)\
                        .then_inc(rec_done, 1)
                    nc.vector.tensor_copy(rec[:, DH:DH + 1], m8[:, :]).then_inc(rec_done, 1)
                    nc.vector.tensor_copy(rec[:, DH + 1:REC], den[:, :]).then_inc(rec_done, 1)
                    dve.wait_ge(rec_done, n * 3 + 3)

        @block.gpsimd
        def _(pool):
            pool.sem_inc(rec_free, 1)
            with pool.Fori(0, 2) as i:
                for g in range(3):
                    n = i * 3 + g
                    pool.wait_ge(rec_done, n * 3 + 3)
                    pool.dma_start(t["sample_rec"][g, bass.ds(i * P, P)], rec[:, :]).then_inc(stored, 16)
                    pool.wait_ge(stored, n * 16 + 16)
                    pool.sem_inc(rec_free, 1)


def recurrence(pr):
    nc, t = pr.nc, pr.t
    plus1, inverted, kh_done, sg_done, xf_done, pool_step, passed = (pr.sem(f"hg_{n}") for n in (
        "plus1", "inverted", "kh", "sg", "xf", "poolstep", "passed"))
    (base_in, lb_done, e_f, f_done, lf_done, einv_done, log_done, sums, exps, q_done, k_done, k_tr, k_t, u_done,
     a_done, am_done, sprime, inter, s_done, squared, msum, ms, rln, rexp, o_ready, stored, o_free, seeds, s_out,
     tile_done, dve_step, km_done) = (pr.sem(f"hg_{n}") for n in (
         "base", "lb", "ef", "f", "lf", "einv", "log", "sums", "exps", "q", "k", "ktr", "kt", "u", "a", "am",
         "sprime", "inter", "sdone", "squared", "msum", "ms", "rln", "rexp", "oready", "stored", "ofree",
         "seeds", "sout", "tile", "dvestep", "km"))
    fi_in, tmp_done = [pr.sem(f"hg_fi{s}") for s in range(2)], pr.sem("hg_tmp")
    with ExitStack() as cx:
        sb = lambda name, shape: cx.enter_context(nc.sbuf_tensor(f"hg_{name}", shape, F32))
        ps = lambda name, shape: cx.enter_context(nc.psum_tensor(f"hg_{name}", shape, F32))
        lb, oml, gain = sb("lb", [P, HW]), sb("oml", [P, HW]), sb("gain", [P, 1])
        fi, qg = [sb(f"fi{s}", [P, 2 * HW]) for s in range(2)], [sb(f"qg{s}", [P, 2 * HH, P]) for s in range(2)]
        f, x, lf, en = (sb(n, [P, HW]) for n in ("f", "x", "lf", "en"))
        kh, sg = [sb(f"kh{s}", [P, HW]) for s in range(2)], [sb(f"sg{s}", [P, HH, P]) for s in range(2)]
        eg, eq, kt, am, osq, rs, nw = (sb(n, [P, HH, P]) for n in ("eg", "eq", "kt", "am", "osq", "rs", "nw"))
        em = sb("em", [P, HH, 8])
        state = sb("state", [P, HH, HK])
        sp_ = [sb(f"sp{s}", [P, HH, HK]) for s in range(2)]
        s8 = sb("s8", [P, NB, HH, HK])
        km = sb("km", [NS, NB, HW])
        oh = sb("oh", [P, HH, P])
        ps_ct = ps("ps_ct", [P, HH, 256])
        ps_cn = ps("ps_cn", [P, HW])
        ps_u = [ps(f"ps_u{c}", [P, HH, HK]) for c in range(4)]
        ps_o = ps("ps_o", [P, HH, P])
        block = cx.enter_context(nc.Block("recurrence"))
        state_in = t["state_hgrn"][0].rearrange("b h k v -> k b h v")
        state_out = t["hgrn_s"][0].rearrange("b h k v -> k b h v")

        def tiles(eng, tile, first):
            with eng.Fori(0, PT // 2 - 1) as i:
                for d in range(first, first + 2):
                    tile(i * 2 + d, d % 2, P, CH, "p")
            for n in range(PT - 2 + first, PT + 1):
                tile(n, n % 2, *((P, CH, "p") if n < PT else (NS, NT, "s")))

        def x_t(r):
            return kt[:, :, r]

        @block.sync
        def _(sp):
            for r in range(2):
                sp.dma_start((lb, oml)[r][:, :], t["hg_lower_bound"][r].partition_broadcast(P)).then_inc(base_in, 16)
            sp.dma_start(gain[:, :], t["hg_norm_g"].rearrange("a p -> p a")).then_inc(base_in, 16)

            def load(n, s, rows):
                sp.dma_start(fi[s][0:rows, :], t["proj_n"][bass.ds(n * P, rows), C_ZF:NATC]).then_inc(fi_in[s], 16)
                sp.dma_start(qg[s][:, :, 0:rows], t["proj_t"][0:2 * HW, bass.ds(n * P, rows)]
                             .rearrange("(k p) t -> p k t", p=P)).then_inc(fi_in[s], 16)

            def tile(n, s, rows, ch, kind):
                if not (isinstance(n, int) and n > PT - 2):
                    sp.wait_ge(squared, n + 1)
                    load(n + 2, s, NS if isinstance(n, int) else P)
                sp.wait_ge(o_ready, n + 1)
                sp.dma_start(t["oh_t"][:, bass.ds(n * P, rows)].rearrange("(k p) t -> p k t", p=P),
                             oh[:, :, 0:rows]).then_inc(stored, 16)
                if kind == "p":
                    sp.wait_ge(stored, n * 16 + 16)
                    sp.sem_inc(o_free, 1)

            load(0, 0, P)
            load(1, 1, P)
            sp.dma_start(s8[:, :, :, :], state_in).then_inc(seeds, 16)
            tiles(sp, tile, 0)
            sp.dma_start(t["hgrn_p"][0, 0].rearrange("h k v -> k h v"), state[:, :, :]).then_inc(s_out, 16)
            sp.wait_ge(s_done, 4 * PT + NB)
            sp.dma_start(state_out, s8[:, :, :, :]).then_inc(s_out, 16)
            sp.wait_ge(s_out, 32)
            sp.wait_ge(stored, (PT + 1) * 16)

        @block.scalar
        def _(act):
            act.wait_ge(lb_done, 1)
            nc.scalar.activation(lb[:, :], lb[:, :], ACT.Exp).then_inc(lb_done, 1)
            act.sem_inc(tile_done, 2)

            def exponentials(n, s, rows):
                r = slice(0, rows)
                act.wait_ge(fi_in[s], (n - s) * 16 + 32)
                nc.scalar.activation(x[r, :], fi[s][r, 0:HW], ACT.Exp, scale=-1.0).then_inc(e_f, 1)
                nc.scalar.activation(eg[:, :, r], qg[s][:, HH:, r], ACT.Exp, scale=-1.0).then_inc(e_f, 1)

            def logs(n, rows):
                r = slice(0, rows)
                act.wait_ge(f_done, n + 1)
                nc.scalar.activation(lf[r, :], f[r, :], ACT.Ln).then_inc(lf_done, 1)
                act.wait_ge(lf_done, n + 1)
                nc.scalar.activation(x[r, :], lf[r, :], ACT.Exp, scale=-1.0).then_inc(einv_done, 1)

            def tile(n, s, rows, ch, kind):
                r, nch = slice(0, rows), rows // ch
                act.wait_ge(sums, n + 1)
                nc.scalar.activation(eq[:, :, r], ps_ct[:, :, r], ACT.Exp)
                nc.scalar.activation(en[r, :], ps_cn[r, :], ACT.Exp, scale=-1.0)
                nc.scalar.activation(em[:, :, 0:nch], ps_ct[:, :, rows:rows + nch], ACT.Exp).then_inc(exps, 1)
                after = NS if isinstance(n, int) and n == PT - 1 else P
                if kind == "p":
                    exponentials(n + 1, 1 - s, after)
                act.wait_ge(k_tr, n + 1)
                nc.scalar.copy(kt[:, :, r], ps_cn[:, :].rearrange("p (h t) -> p h t", h=HH)[:, :, r]).then_inc(k_t, 1)
                if kind == "p":
                    logs(n + 1, after)
                act.wait_ge(inter, n * 4 + nch + 1)
                act.wait_ge(sg_done, n + 1)
                nc.scalar.activation(osq[:, :, r], ps_o[:, :, r], ACT.Square).then_inc(squared, 1)
                act.wait_ge(ms, n + 1)
                nc.scalar.activation(rs[:, :, r], x_t(r), ACT.Ln).then_inc(rln, 1)
                act.wait_ge(rln, n + 1)
                nc.scalar.activation(rs[:, :, r], rs[:, :, r], ACT.Exp, scale=-0.5).then_inc(rexp, 1)

            exponentials(0, 0, P)
            logs(0, P)
            tiles(act, tile, 0)

        @block.gpsimd
        def _(pool):
            step = Ordered(pool, pool_step)
            G = nc.gpsimd

            def wait(sem, value):
                pool.wait_ge(sem, value)
                pool.sem_inc(passed, 1)

            def prepare(n, s, rows, ch, kind):
                r = slice(0, rows)
                step.turn(n, 1, 0)
                pool.wait_ge(tile_done, n + 1)
                wait(e_f, n * 2 + 1)
                G.tensor_scalar(f[r, :], x[r, :], 1.0, None, ALU.add).then_inc(plus1, 1)
                wait(e_f, n * 2 + 2)
                G.tensor_scalar(sg[s][:, :, r], eg[:, :, r], 1.0, None, ALU.add).then_inc(plus1, 1)
                wait(inverted, n * 2 + 1)
                step(G.tensor_tensor(f[r, :], f[r, :], oml[r, :], ALU.mult))
                pool.sem_inc(passed, 1)
                G.tensor_tensor(f[r, :], f[r, :], lb[r, :], ALU.add).then_inc(f_done, 1)
                wait(f_done, n + 1)
                G.tensor_scalar(kh[s][r, :], f[r, :], -1.0, 1.0, ALU.mult, ALU.add).then_inc(kh_done, 1)
                wait(einv_done, n + 1)
                G.tensor_tensor(x[r, :], f[r, :], x[r, :], ALU.mult).then_inc(xf_done, 1)
                wait(inverted, n * 2 + 2)
                G.tensor_tensor(sg[s][:, :, r], sg[s][:, :, r], qg[s][:, HH:, r], ALU.mult).then_inc(sg_done, 1)

            prepare(0, 0, P, CH, "p")
            tiles(pool, prepare, 1)

        @block.vector
        def _(dve):
            step = Ordered(dve, dve_step)
            dve.wait_ge(base_in, 48)
            nc.vector.tensor_tensor(lb[:, :], oml[:, :], lb[:, :], ALU.subtract).then_inc(lb_done, 1)
            dve.wait_ge(lb_done, 2)
            step(nc.vector.tensor_scalar(lb[:, :], lb[:, :], 1.0, None, ALU.add))
            step(nc.vector.reciprocal(lb[:, :], lb[:, :]))
            step(nc.vector.tensor_scalar(oml[:, :], lb[:, :], -1.0, 1.0, ALU.mult, ALU.add))
            step(nc.vector.memset(state[:, :, :], 0.0))
            START, STEPS = 4, 6
            over = lambda y, rows: y.unsqueeze(2).broadcast_to([P, HH, HK])

            def invert_forget(n, rows):
                dve.wait_ge(plus1, n * 2 + 1)
                nc.vector.reciprocal(f[0:rows, :], f[0:rows, :]).then_inc(inverted, 1)

            def invert_gate(n, s, rows):
                dve.wait_ge(plus1, n * 2 + 2)
                nc.vector.reciprocal(sg[s][:, :, 0:rows], sg[s][:, :, 0:rows]).then_inc(inverted, 1)

            def correct_log(n, rows):
                dve.wait_ge(xf_done, n + 1)
                nc.vector.scalar_tensor_tensor(lf[0:rows, :], x[0:rows, :], -1.0, lf[0:rows, :], ALU.add, ALU.add)\
                    .then_inc(log_done, 1)

            def tile(n, s, rows, ch, kind):
                r, nch = slice(0, rows), rows // ch
                after = NS if isinstance(n, int) and n == PT - 1 else P
                step.turn(n, STEPS, START)
                dve.wait_ge(exps, n + 1)
                dve.wait_ge(kh_done, n + 1)
                nc.vector.tensor_tensor(kh[s][r, :], kh[s][r, :], en[r, :], ALU.mult).then_inc(k_done, 1)
                nc.vector.tensor_tensor(qg[s][:, 0:HH, r], qg[s][:, 0:HH, r], eq[:, :, r], ALU.mult).then_inc(q_done, 1)
                if kind == "p":
                    invert_forget(n + 1, after)
                if kind == "s":
                    dve.wait_ge(k_done, n + 1)
                    for c in range(nch):
                        nc.vector.tensor_scalar(km[:, c, :], kh[s][r, :], pr.c("seqmask", NS)[:, c:c + 1], None,
                                                ALU.mult).then_inc(km_done, 1)
                dve.wait_ge(a_done, n + 1)
                causal = pr.c(f"causal_{kind}", rows).unsqueeze(1).broadcast_to([rows, HH, rows])
                nc.vector.tensor_tensor(am[r, :, r], ps_ct[r, 0:2, :].rearrange("p a (b t) -> p (a b) t", b=2)[:, :, r],
                                        causal, ALU.mult).then_inc(am_done, 1)
                if kind == "s":
                    dve.wait_ge(seeds, 16)
                for c in range(nch):
                    q = n * 4 + c
                    s_in = state[:, :, :] if kind == "p" else s8[:, c, :, :]
                    dve.wait_ge(inter, q + 1)
                    nc.vector.tensor_tensor(sp_[c % 2][:, :, :], s_in, over(em[:, :, c], rows), ALU.mult).then_inc(sprime, 1)
                    dve.wait_ge(sprime, q + 1)
                    dve.wait_ge(u_done, q + 1)
                    nc.vector.tensor_tensor(s_in, sp_[c % 2][:, :, :], ps_u[c % 4][:, :, :], ALU.add).then_inc(tmp_done, 1)
                    dve.wait_ge(tmp_done, q + 1)
                    nc.vector.tensor_tensor(s_in, s_in, over(eq[:, :, c * ch + ch - 1], rows), ALU.mult).then_inc(s_done, 1)
                    dve.wait_ge(s_done, q + 1)
                if kind == "p":
                    invert_gate(n + 1, 1 - s, after)
                dve.wait_ge(msum, n + 1)
                nc.vector.tensor_scalar(x_t(r), ps_cn[:, :].rearrange("p (h t) -> p h t", h=HH)[:, :, r],
                                        1.0 / HK, EPS, ALU.mult, ALU.add).then_inc(ms, 1)
                dve.wait_ge(ms, n + 1)
                if kind == "p":
                    correct_log(n + 1, after)
                dve.wait_ge(rexp, n + 1)
                step(nc.vector.tensor_tensor(nw[:, :, r], rs[:, :, r], rs[:, :, r], ALU.mult))
                step(nc.vector.tensor_tensor(nw[:, :, r], nw[:, :, r], x_t(r), ALU.mult))
                step(nc.vector.tensor_scalar(nw[:, :, r], nw[:, :, r], -0.5, 1.5, ALU.mult, ALU.add))
                step(nc.vector.tensor_tensor(rs[:, :, r], rs[:, :, r], nw[:, :, r], ALU.mult))
                dve.wait_ge(sg_done, n + 1)
                step(nc.vector.tensor_tensor(sg[s][:, :, r], sg[s][:, :, r], rs[:, :, r], ALU.mult))
                step(nc.vector.tensor_scalar(sg[s][:, :, r], sg[s][:, :, r], gain[:, 0:1], None, ALU.mult))
                dve.wait_ge(o_free, n + 1)
                nc.vector.tensor_tensor(oh[:, :, r], sg[s][:, :, r], ps_o[:, :, r], ALU.mult).then_inc(o_ready, 1)
                dve.wait_ge(o_ready, n + 1)
                dve.sem_inc(tile_done, 1)
                assert step.n == STEPS, step.n

            dve.sem_inc(inter, 1)
            dve.sem_inc(o_free, 1)
            invert_forget(0, P)
            invert_gate(0, 0, P)
            correct_log(0, P)
            tiles(dve, tile, 0)

        @block.tensor
        def _(pe):
            def tile(n, s, rows, ch, kind):
                r, nch = slice(0, rows), rows // ch
                tri = pr.c(f"tri_{kind}", rows)
                pe.wait_ge(log_done, n + 1)
                for h in range(HH):
                    nc.tensor.matmul(ps_ct[:, h, 0:rows + nch], lf[r, h * HK:(h + 1) * HK], tri, start=True, stop=True)
                nc.tensor.matmul(ps_cn[r, :], tri[:, r], lf[r, :], start=True, stop=True).then_inc(sums, 1)
                pe.wait_ge(k_done, n + 1)
                for h in range(HH):
                    mm = nc.tensor.transpose(ps_cn[:, h * P:h * P + rows], kh[s][r, h * HK:(h + 1) * HK],
                                             pr.c("ident")[r, r])
                mm.then_inc(k_tr, 1)

                def increments(c):
                    if kind == "p":
                        a = slice(c * ch, (c + 1) * ch)
                        lhs, rhs = kh[s][a], fi[s][a, HW:]
                    else:
                        pe.wait_ge(km_done, c + 1)
                        lhs, rhs = km[:, c], fi[s][r, HW:]
                    for h in range(HH):
                        hs = slice(h * HK, (h + 1) * HK)
                        mm = nc.tensor.matmul(ps_u[c % 4][:, h, :], lhs[:, hs], rhs[:, hs], start=True, stop=True)
                    mm.then_inc(u_done, 1)

                increments(0)
                pe.wait_ge(k_t, n + 1)
                pe.wait_ge(q_done, n + 1)
                for h in range(HH):
                    mm = nc.tensor.matmul(ps_ct[r, h // 2, h % 2 * P:h % 2 * P + rows], kt[:, h, r], qg[s][:, h, r],
                                          start=True, stop=True)
                mm.then_inc(a_done, 1)
                for c in range(1, 4):
                    increments(c)
                pe.wait_ge(am_done, n + 1)
                for h in range(HH):
                    nc.tensor.matmul(ps_o[:, h, r], fi[s][r, HW + h * HK:HW + (h + 1) * HK], am[r, h, r],
                                     start=(h == 0), stop=False, skip_group_check=True)
                for c in range(nch):
                    pe.wait_ge(sprime, n * 4 + c + 1)
                    for h in range(HH):
                        mm = nc.tensor.matmul(ps_o[:, h, c * ch:(c + 1) * ch], sp_[c % 2][:, h, :],
                                              qg[s][:, h, c * ch:(c + 1) * ch], start=False,
                                              stop=(c == nch - 1 and h == HH - 1), skip_group_check=True)
                    mm.then_inc(inter, 1)
                    if c + 4 < nch:
                        pe.wait_ge(s_done, n * 4 + c + 1)
                        increments(c + 4)
                pe.wait_ge(squared, n + 1)
                nc.tensor.matmul(ps_cn[:, :].rearrange("p (h t) -> p h t", h=HH)[:, :, r], pr.c("ones"), osq[:, :, r],
                                 start=True, stop=True).then_inc(msum, 1)

            tiles(pe, tile, 0)


def mixer_merge(pr):
    nc, t = pr.nc, pr.t
    KA, KH = GW // P, HW // P
    acts_in = [pr.sem(f"mm_acts{k}") for k in range(KA + KH)]
    x_hi_done, x_lo_done, w_hi_done, w_lo_done = (pr.sem(f"mm_{n}") for n in ("xhi", "xlo", "whi", "wlo"))
    w_in = [pr.sem(f"mm_win{s}") for s in range(2)]
    z_in = [pr.sem(f"mm_zin{s}") for s in range(2)]
    (prod_a, prod_h, sig, scaled_a, scaled_h, summed, stored, m_free) = (pr.sem(f"mm_{n}") for n in (
        "proda", "prodh", "sig", "scaleda", "scaledh", "summed", "stored", "mfree"))
    with ExitStack() as cx:
        sb = lambda name, shape: cx.enter_context(nc.sbuf_tensor(f"mm_{name}", shape, F32))
        half = lambda name, shape: cx.enter_context(nc.sbuf_tensor(f"mm_{name}", shape, F16))
        x = sb("x", [P, KA + KH, TOK])
        x_hi, x_lo = half("xhi", [P, KA + KH, TOK]), half("xlo", [P, KA + KH, TOK])
        w = [sb(f"w{s}", [P, KA + KH, P]) for s in range(2)]
        w_hi, w_lo = ([half(f"{n}{s}", [P, KA + KH, P]) for s in range(2)] for n in ("whi", "wlo"))
        z = [sb(f"z{s}", [P, 2, TOK]) for s in range(2)]
        ma = [sb(f"ma{s}", [P, 2, TOK]) for s in range(2)]
        ps_a = cx.enter_context(nc.psum_tensor("mm_psa", [P, 3 * 512], F32))
        ps_h = cx.enter_context(nc.psum_tensor("mm_psh", [P, 3 * 512], F32))
        block = cx.enter_context(nc.Block("mixer_merge"))
        turns = D // P // 2
        wa_v, wh_v = (t[n][0].rearrange("(k p) n -> p k n", p=P) for n in ("w_att_branch", "w_hg_branch"))
        gates = t["proj_t"][2 * HW:, :].rearrange("(g c p) t -> c p g t", g=2, p=P)

        @block.sync
        def _(sp):
            for k in range(KA + KH):
                src = t["att_t"][k * P:(k + 1) * P] if k < KA else t["oh_t"][(k - KA) * P:(k - KA + 1) * P]
                sp.dma_start(x[:, k, :], src).then_inc(acts_in[k], 16)

            def load(c, s):
                sp.dma_start(w[s][:, 0:KA, :], wa_v[:, :, bass.ds(c * P, P)]).then_inc(w_in[s], 16)
                sp.dma_start(w[s][:, KA:, :], wh_v[:, :, bass.ds(c * P, P)]).then_inc(w_in[s], 16)
                sp.dma_start(z[s][:, :, :], gates[c]).then_inc(z_in[s], 16)

            for s in range(2):
                load(s, s)
            with sp.Fori(1, turns) as i:
                for s in range(2):
                    sp.wait_ge(scaled_h, i * 2 + s)
                    load(i * 2 + s, s)

        @block.tensor
        def _(pe):
            pe.wait_ge(x_lo_done, KA + KH)
            with pe.Fori(0, turns) as i:
                for s in range(2):
                    pe.wait_ge(w_lo_done, i * 2 + s + 1)
                    for ks, ps, done, free in ((range(KA), ps_a, prod_a, scaled_a), (range(KA, KA + KH), ps_h, prod_h, scaled_h)):
                        pe.wait_ge(free, i * 2 + s + 1)
                        mms = [(y, z_, k) for k in ks for y, z_ in ((w_hi, x_hi), (w_hi, x_lo), (w_lo, x_hi))]
                        for j, (y, z_, k) in enumerate(mms):
                            for a in range(0, TOK, 512):
                                e = min(a + 512, TOK)
                                mm = nc.tensor.matmul(ps[:, a:e], y[s][:, k, :], z_[:, k, a:e],
                                                      start=(j == 0), stop=(j == len(mms) - 1))
                        mm.then_inc(done, 1)

        @block.scalar
        def _(act):
            for k in range(KA + KH):
                act.wait_ge(acts_in[k], 16)
                nc.scalar.copy(x_hi[:, k, :], x[:, k, :]).then_inc(x_hi_done, 1)
            act.sem_inc(prod_h, 2)
            with act.Fori(0, turns) as i:
                for s in range(2):
                    act.wait_ge(w_in[s], i * 32 + 32)
                    act.wait_ge(prod_h, i * 2 + s + 1)
                    nc.scalar.activation(w_hi[s][:, :, :], w[s][:, :, :], ACT.Copy, scale=SPLIT).then_inc(w_hi_done, 1)
                    act.wait_ge(z_in[s], i * 16 + 16)
                    nc.scalar.activation(z[s][:, :, :], z[s][:, :, :], ACT.Sigmoid).then_inc(sig, 1)

        @block.vector
        def _(dve):
            for k in range(KA + KH):
                dve.wait_ge(x_hi_done, k + 1)
                nc.vector.tensor_tensor(x_lo[:, k, :], x[:, k, :], x_hi[:, k, :], ALU.subtract).then_inc(x_lo_done, 1)
            dve.sem_inc(scaled_a, 1)
            dve.sem_inc(scaled_h, 1)

            def low(n, s):
                dve.wait_ge(w_hi_done, n + 1)
                nc.vector.scalar_tensor_tensor(w_lo[s][:, :, :], w[s][:, :, :], SPLIT, w_hi[s][:, :, :],
                                               ALU.mult, ALU.subtract).then_inc(w_lo_done, 1)

            def merge(n, s, another):
                if another:
                    low(n + 1, 1 - s)
                dve.wait_ge(sig, n + 1)
                dve.wait_ge(m_free, n + 1)
                for j, (ps, done, scaled) in enumerate(((ps_a, prod_a, scaled_a), (ps_h, prod_h, scaled_h))):
                    dve.wait_ge(done, n + (3 if j else 1))
                    nc.vector.scalar_tensor_tensor(ma[s][:, j, :], ps[:, 0:TOK], 1.0 / SPLIT, z[s][:, j, :],
                                                   ALU.mult, ALU.mult).then_inc(scaled, 1)
                dve.wait_ge(scaled_a, n + 2)
                dve.wait_ge(scaled_h, n + 2)
                nc.vector.tensor_tensor(ma[s][:, 0, :], ma[s][:, 0, :], ma[s][:, 1, :], ALU.add).then_inc(summed, 1)

            low(0, 0)
            chunks_ahead(dve, 2 * turns, merge)

        @block.gpsimd
        def _(pool):
            pool.sem_inc(m_free, 2)
            with pool.Fori(0, turns) as i:
                for s in range(2):
                    n = i * 2 + s
                    pool.wait_ge(summed, n + 1)
                    pool.dma_start(t["mix_t"][bass.ds(n * P, P), :], ma[s][:, 0, :]).then_inc(stored, 16)
                    pool.wait_ge(stored, n * 16 + 16)
                    pool.sem_inc(m_free, 1)


def mixer_output(pr):
    nc, t = pr.nc, pr.t
    w_hi_done, w_lo_done, m_hi_done, m_lo_done = (pr.sem(f"mo_{n}") for n in ("whi", "wlo", "mhi", "mlo"))
    gates_in, product, gated, added, stored, o_free = (pr.sem(f"mo_{n}") for n in (
        "gates", "product", "gated", "added", "stored", "ofree"))
    w_in = [pr.sem(f"mo_win{k}") for k in range(KD)]
    in_ = [pr.sem(f"mo_in{s}") for s in range(2)]
    with ExitStack() as cx:
        sb = lambda name, shape: cx.enter_context(nc.sbuf_tensor(f"mo_{name}", shape, F32))
        w, g1 = sb("w", [P, KD, D]), [sb(f"g{r}", [P, D]) for r in range(2)]
        half = lambda name, shape: cx.enter_context(nc.sbuf_tensor(f"mo_{name}", shape, F16))
        w_hi, w_lo = half("whi", [P, KD, D]), half("wlo", [P, KD, D])
        mix = [sb(f"mix{s}", [P, KD, P]) for s in range(2)]
        m_hi, m_lo = ([half(f"{n}{s}", [P, KD, P]) for s in range(2)] for n in ("mhi", "mlo"))
        x = [sb(f"x{s}", [P, D]) for s in range(2)]
        o = [sb(f"o{s}", [P, D]) for s in range(2)]
        ps = [cx.enter_context(nc.psum_tensor(f"mo_ps{s}", [P, D], F32)) for s in range(2)]
        block = cx.enter_context(nc.Block("mixer_output"))
        mix_v = t["mix_t"].rearrange("(k p) t -> p k t", p=P)
        x_s = t["x_sample"].rearrange("b t d -> (b t) d")

        def tiles(eng, tile, before_second=lambda: None):
            tile(0, 0, 0, P)
            before_second()
            tile(1, 1, 0, P)
            with eng.Fori(1, PT // 2) as i:
                for s in range(2):
                    tile(i * 2 + s, s, i, P)
            tile(PT, 0, PT // 2, NS)

        @block.sync
        def _(sp):
            def constant_loads():
                for k in range(KD):
                    sp.dma_start(w[:, k, :], t["w_out"][0, k * P:(k + 1) * P, :]).then_inc(w_in[k], 16)
                for r, (a, n) in enumerate(((0, P), (P, NS))):
                    sp.dma_start(g1[r][0:n, :], t["modrep"][a:a + n, 2 * D:3 * D]).then_inc(gates_in, 16)

            def tile(n, s, i, rows):
                sp.wait_ge(added, n + 1)
                sp.dma_start(mix[s][:, :, 0:rows], mix_v[:, :, bass.ds(n * P, rows)]).then_inc(in_[s], 16)
                src = t["x_prompt"][0][bass.ds(n * P, P), :] if rows == P else x_s
                sp.dma_start(x[s][0:rows, :], src).then_inc(in_[s], 16)
            tiles(sp, tile, constant_loads)

        @block.tensor
        def _(pe):
            def tile(n, s, i, rows):
                pe.wait_ge(m_lo_done, n + 1)
                pe.wait_ge(gated, n + 1)
                mms = [(m, x, k) for k in range(KD) for m, x in ((m_hi, w_hi), (m_hi, w_lo), (m_lo, w_hi))]
                for j, (m, x, k) in enumerate(mms):
                    if j % 3 == 0 and isinstance(n, int) and n == 0:
                        pe.wait_ge(w_lo_done, k + 1)
                    for a in range(0, D, 512):
                        mm = nc.tensor.matmul(ps[s][0:rows, a:a + 512], m[s][:, k, 0:rows], x[:, k, a:a + 512],
                                              start=(j == 0), stop=(j == len(mms) - 1))
                mm.then_inc(product, 1)
            tiles(pe, tile)

        @block.scalar
        def _(act):
            def high_weights():
                for k in range(KD):
                    act.wait_ge(w_in[k], 16)
                    nc.scalar.activation(w_hi[:, k, :], w[:, k, :], ACT.Copy, scale=SPLIT).then_inc(w_hi_done, 1)

            act.sem_inc(product, 2)

            def tile(n, s, i, rows):
                act.wait_ge(in_[s], i * 32 + 32)
                act.wait_ge(product, n + 1)
                nc.scalar.copy(m_hi[s][:, :, 0:rows], mix[s][:, :, 0:rows]).then_inc(m_hi_done, 1)
            tiles(act, tile, high_weights)

        @block.vector
        def _(dve):
            dve.sem_inc(gated, 2)
            dve.sem_inc(added, 2)

            def low(n, s, rows):
                dve.wait_ge(m_hi_done, n + 1)
                nc.vector.tensor_tensor(m_lo[s][:, :, 0:rows], mix[s][:, :, 0:rows], m_hi[s][:, :, 0:rows], ALU.subtract)\
                    .then_inc(m_lo_done, 1)

            def tile(n, s, i, rows):
                r = slice(0, rows)
                if rows == P:
                    low(n + 1, 1 - s, NS if isinstance(n, int) and n == PT - 1 else P)
                dve.wait_ge(product, n + 3)
                dve.wait_ge(o_free, n + 1)
                nc.vector.scalar_tensor_tensor(o[s][r, :], ps[s][r, :], 1.0 / SPLIT, g1[0 if rows == P else 1][r, :],
                                               ALU.mult, ALU.mult).then_inc(gated, 1)
                dve.wait_ge(gated, n + 3)
                nc.vector.tensor_tensor(o[s][r, :], o[s][r, :], x[s][r, :], ALU.add).then_inc(added, 1)

            low(0, 0, P)
            for k in range(KD):
                dve.wait_ge(w_hi_done, k + 1)
                nc.vector.scalar_tensor_tensor(w_lo[:, k, :], w[:, k, :], SPLIT, w_hi[:, k, :], ALU.mult, ALU.subtract)\
                    .then_inc(w_lo_done, 1)
            dve.wait_ge(gates_in, 32)
            with dve.Fori(0, PT // 2 - 1) as i:
                for s in range(2):
                    tile(i * 2 + s, s, i, P)
            for n in range(PT - 2, PT + 1):
                tile(n, n % 2, None, P if n < PT else NS)

        @block.gpsimd
        def _(pool):
            pool.sem_inc(o_free, 2)

            def tile(n, s, i, rows):
                pool.wait_ge(added, n + 3)
                pool.dma_start(t["x1"][bass.ds(n * P, rows), :], o[s][0:rows, :]).then_inc(stored, 16)
                pool.wait_ge(stored, n * 16 + 16)
                pool.sem_inc(o_free, 1)
            tiles(pool, tile)


WSCALE = 16.0


def score_weights(pr, wsc):
    nc, t = pr.nc, pr.t
    HP = 2 * HEADS
    NQ = HP // 4
    sub_in, sub_tr, sub_t, turned, wt_done, product, out = (pr.sem(f"sw_{n}") for n in (
        "subin", "subtr", "subt", "turned", "wt", "product", "out"))
    w_in = [pr.sem(f"sw_in{s}") for s in range(2)]
    with ExitStack() as cx:
        sb = lambda name, shape: cx.enter_context(nc.sbuf_tensor(f"sw_{name}", shape, F32))
        sub, sub_tt = sb("sub", [P, HP, P]), sb("subt", [P, HP, P])
        raw = [sb(f"raw{s}", [P, HP, P]) for s in range(2)]
        wt = [sb(f"wt{s}", [P, 4, P]) for s in range(2)]
        ps_s = cx.enter_context(nc.psum_tensor("sw_pss", [P, 4, P], F32))
        ps_t = [cx.enter_context(nc.psum_tensor(f"sw_pst{s}", [P, 4, P], F32)) for s in range(2)]
        ps_o = [cx.enter_context(nc.psum_tensor(f"sw_pso{s}", [P, 4 * P], F32)) for s in range(2)]
        block = cx.enter_context(nc.Block("score_weights"))
        wq = t["peer_wq"][0].rearrange("(k p) n -> k p n", p=P)

        @block.sync
        def _(sp):
            sp.dma_start(sub[:, :, :], t["peer_subkeys"][0].rearrange("h p k d -> k (h p) d")).then_inc(sub_in, 16)
            load = lambda k, s: sp.dma_start(raw[s][:, :, :].rearrange("p j f -> p (j f)"), wq[k]).then_inc(w_in[s], 16)
            for s in range(2):
                load(s, s)
            for k in range(2, KD):
                sp.wait_ge(turned, (k - 1) * NQ)
                load(k, k % 2)

        @block.tensor
        def _(pe):
            pe.wait_ge(sub_in, 16)
            for q in range(NQ):
                if q:
                    pe.wait_ge(sub_t, q)
                for j in range(4):
                    mm = nc.tensor.transpose(ps_s[:, j, :], sub[:, q * 4 + j, :], pr.c("ident"))
                mm.then_inc(sub_tr, 1)
            pe.sem_inc(wt_done, 2)
            pe.sem_inc(out, 2)

            def turn(k, s, q):
                pe.wait_ge(wt_done, k * NQ + q + 1)
                for j in range(4):
                    mm = nc.tensor.transpose(ps_t[q % 2][:, j, :], raw[s][:, q * 4 + j, :], pr.c("ident"))
                mm.then_inc(turned, 1)

            def multiply(k, s, q):
                pe.wait_ge(wt_done, k * NQ + q + 3)
                pe.wait_ge(out, k * NQ + q + 1)
                for j in range(4):
                    mm = nc.tensor.matmul(ps_o[q % 2][:, j * P:(j + 1) * P], wt[q % 2][:, j, :], sub_tt[:, q * 4 + j, :],
                                          start=True, stop=True)
                mm.then_inc(product, 1)

            pe.wait_ge(sub_t, NQ)
            with pe.Fori(0, KD // 2) as i:
                for s in range(2):
                    k = i * 2 + s
                    pe.wait_ge(w_in[s], i * 16 + 16)
                    turn(k, s, 0)
                    for q in range(1, NQ):
                        turn(k, s, q)
                        multiply(k, s, q - 1)
                    multiply(k, s, NQ - 1)

        @block.scalar
        def _(act):
            for q in range(NQ):
                act.wait_ge(sub_tr, q + 1)
                nc.scalar.copy(sub_tt[:, q * 4:q * 4 + 4, :], ps_s[:, :, :]).then_inc(sub_t, 1)
            act.sem_inc(product, 2)
            with act.Fori(0, KD) as k:
                for q in range(NQ):
                    act.wait_ge(turned, k * NQ + q + 1)
                    act.wait_ge(product, k * NQ + q + 1)
                    nc.scalar.copy(wt[q % 2][:, :, :], ps_t[q % 2][:, :, :]).then_inc(wt_done, 1)

        @block.vector
        def _(dve):
            with dve.Fori(0, KD) as k:
                for q in range(NQ):
                    dve.wait_ge(product, k * NQ + q + 3)
                    nc.vector.tensor_copy(wsc[:, bass.ds(k, 1), q * 4 * P:(q + 1) * 4 * P].rearrange("p a n -> p (a n)"), ps_o[q % 2][:, :])\
                        .then_inc(out, 1)


def routing(pr, ht, wsc):
    nc, t = pr.nc, pr.t
    HP = 2 * HEADS
    h_done, scored, sc_out, step_s, done, exp_in, exp_done, stored, out_free, passed = (
        pr.sem(f"rt_{n}") for n in ("h", "scored", "scout", "step", "done", "expin", "exp", "stored", "outfree", "passed"))
    with ExitStack() as cx:
        sb = lambda name, shape, dt=F32: cx.enter_context(nc.sbuf_tensor(f"rt_{name}", shape, dt))
        h = [sb(f"h{s}", [P, KD, P]) for s in range(2)]
        sc, sc2 = sb("sc", [P, HP, KEYS]), sb("sc2", [P, HP, KEYS])
        top, ix = sb("top", [P, HP, TOPK]), sb("ix", [P, HP, TOPK], U32)
        ixf = sb("ixf", [P, HP, TOPK])
        cand = sb("cand", [P, HEADS, TOPK * TOPK])
        cand2 = sc2[:, :, :].rearrange("p (h e) k -> p h (e k)", e=2)
        best, ci = sb("best", [P, HEADS, TOPK]), sb("ci", [P, HEADS, TOPK], U32)
        c1, c2 = sb("c1", [P, HEADS, TOPK], U32), sb("c2", [P, HEADS, TOPK], U32)
        place = sb("place", [P, 2, HEADS, TOPK])
        hot = sb("hot", [P, 2, HEADS, TOPK, TOPK], F16)
        e12 = sb("e12", [P, 2, PICKS])
        ex, gate = sb("ex", [P, HEADS, TOPK]), sb("gate", [P, HEADS, TOPK])
        dn = sb("dn", [P, HEADS])
        ps = [cx.enter_context(nc.psum_tensor(f"rt_ps{s}", [P, HP, KEYS], F32)) for s in range(2)]
        block = cx.enter_context(nc.Block("routing"))

        def tiles(eng, tile):
            with eng.Fori(0, PT // 2) as i:
                for s in range(2):
                    tile(i * 2 + s, s, i, P)
            tile(PT, 0, PT // 2, NS)

        @block.tensor
        def _(pe):
            def tile(n, s, i, rows):
                pe.wait_ge(h_done, n + 1)
                pe.wait_ge(sc_out, n + 1)
                for a in range(0, HP, 4):
                    for k in range(KD):
                        mm = nc.tensor.matmul(ps[s][0:rows, a:a + 4, :].rearrange("p a k -> p (a k)"), h[s][:, k, 0:rows],
                                              wsc[:, k, a * KEYS:(a + 4) * KEYS], start=(k == 0), stop=(k == KD - 1))
                mm.then_inc(scored, 1)
            tiles(pe, tile)

        @block.scalar
        def _(act):
            act.sem_inc(sc_out, 2)
            act.sem_inc(scored, 2)

            def fetch(n, s, rows):
                act.wait_ge(scored, n + 1)
                nc.scalar.copy(h[s][:, :, 0:rows], ht[:, :, bass.ds(n * P, rows)]).then_inc(h_done, 1)

            def tile(n, s, i, rows):
                act.wait_ge(scored, n + 3)
                act.wait_ge(done, n + 1)
                nc.scalar.copy(sc[0:rows, :, :], ps[s][0:rows, :, :]).then_inc(sc_out, 1)
                if not (isinstance(n, int) and n >= PT - 2):
                    fetch(n + 2, s, P)
                elif n == PT - 2:
                    fetch(PT, s, NS)
                act.wait_ge(exp_in, n + 1)
                nc.scalar.activation(ex[0:rows], ex[0:rows], ACT.Exp).then_inc(exp_done, 1)

            fetch(0, 0, P)
            fetch(1, 1, P)
            with act.Fori(0, PT // 2 - 1) as i:
                for s in range(2):
                    tile(i * 2 + s, s, i, P)
            for n in range(PT - 2, PT + 1):
                tile(n, n % 2, 0, P if n < PT else NS)

        @block.vector
        def _(dve):
            step = Ordered(dve, step_s)
            V = nc.vector
            dve.sem_inc(done, 1)
            STEPS = 4 + 4 + 10

            def tile(n, s, i, rows):
                r = slice(0, rows)
                step.turn(n, STEPS, 0)

                def top16(src, work, values, index, count):
                    dve.sem_inc(passed, 1)
                    for j in range(count):
                        last = V.max(values[r, j, 0:8], src[r, j, :])
                    step(last)
                    dve.sem_inc(passed, 1)
                    for j in range(count):
                        V.max_index(index[r, j, 0:8], values[r, j, 0:8], src[r, j, :])
                        last = V.match_replace(work[r, j, :], values[r, j, 0:8], src[r, j, :], NEG)
                    step(last)
                    dve.sem_inc(passed, 1)
                    for j in range(count):
                        last = V.max(values[r, j, 8:16], work[r, j, :])
                    step(last)
                    dve.sem_inc(passed, 1)
                    for j in range(count):
                        last = V.max_index(index[r, j, 8:16], values[r, j, 8:16], work[r, j, :])
                    step(last)

                dve.wait_ge(sc_out, n + 3)
                top16(sc, sc2, top, ix, HP)
                step(V.tensor_copy(ixf[r], ix[r]))
                halves = top[r].rearrange("p (h e) k -> p h e k", e=2)
                grid = [rows, HEADS, TOPK, TOPK]
                as_grid = lambda x: x.rearrange("p h (a b) -> p h a b", b=TOPK)
                step(V.tensor_tensor(as_grid(cand[r]), halves[:, :, 0].unsqueeze(3).broadcast_to(grid),
                                     halves[:, :, 1].unsqueeze(2).broadcast_to(grid), ALU.add))
                top16(cand, cand2, best, ci, HEADS)
                step(V.tensor_single_scalar(c1[r], ci[r], 4, ALU.logical_shift_right))
                step(V.tensor_single_scalar(c2[r], ci[r], TOPK - 1, ALU.bitwise_and))
                step(V.tensor_copy(place[r, 0], c1[r]))
                step(V.tensor_copy(place[r, 1], c2[r]))
                numbers = ixf[r].rearrange("p (h e) k -> p e h k", e=2)
                for e in range(2):
                    for b in range(TOPK):
                        last = V.scalar_tensor_tensor(hot[r, e, :, :, b], place[r, e], float(b),
                                                      numbers[:, e, :, b].unsqueeze(2).broadcast_to([rows, HEADS, TOPK]),
                                                      ALU.is_equal, ALU.mult)
                step(last)
                dve.wait_ge(out_free, n + 1)
                step(V.tensor_reduce(e12[r].rearrange("p e k -> p (e k)"), hot[r].rearrange("p e h k b -> p (e h k) b"), AX, ALU.add))
                V.tensor_tensor(ex[r], best[r], best[r, :, 0:1].broadcast_to([rows, HEADS, TOPK]), ALU.subtract)\
                    .then_inc(exp_in, 1)
                dve.wait_ge(exp_done, n + 1)
                step(V.tensor_reduce(dn[r, :], ex[r], AX, ALU.add))
                step(V.reciprocal(dn[r, :], dn[r, :]))
                V.tensor_tensor(gate[r], ex[r], dn[r].unsqueeze(2).broadcast_to([rows, HEADS, TOPK]), ALU.mult)\
                    .then_inc(done, 1)
                assert step.n == STEPS, step.n
            tiles(dve, tile)

        @block.gpsimd
        def _(pool):
            pool.sem_inc(out_free, 1)

            def tile(n, s, i, rows):
                pool.wait_ge(done, n + 2)
                pool.dma_start(t["e1"][bass.ds(n * P, rows), :], e12[0:rows, 0, :]).then_inc(stored, 16)
                pool.dma_start(t["e2"][bass.ds(n * P, rows), :], e12[0:rows, 1, :]).then_inc(stored, 16)
                pool.dma_start(t["gate"][bass.ds(n * P, rows), :], gate[0:rows].rearrange("p h k -> p (h k)"))\
                    .then_inc(stored, 16)
                pool.wait_ge(stored, n * 48 + 48)
                pool.sem_inc(out_free, 1)
            tiles(pool, tile)


def scatter_gates(pr):
    nc, t = pr.nc, pr.t
    BT = 8
    ON_POOL = 2
    turned, pk_done, passed, few_done, hot, pool_hot, product, evac, tile_free = (pr.sem(f"sg_{n}") for n in (
        "turned", "pk", "passed", "few", "hot", "poolhot", "product", "evac", "tilefree"))
    in_ = [pr.sem(f"sg_in{s}") for s in range(2)]
    stored = [pr.sem(f"sg_stored{s}") for s in range(2)]
    with ExitStack() as cx:
        sb = lambda name, shape, dt=F32: cx.enter_context(nc.sbuf_tensor(f"sg_{name}", shape, dt))
        raw = [sb(f"raw{s}", [P, 3, PICKS]) for s in range(2)]
        pk = [sb(f"pk{s}", [P, 3, P]) for s in range(2)]
        few = [sb(f"few{s}", [P, 2, ON_POOL]) for s in range(2)]
        a = [sb(f"a{s}", [P, BT, P]) for s in range(2)]
        b_ = [[sb(f"b{s}{b}", [P, P]) for b in range(BT)] for s in range(2)]
        stage = [sb(f"stage{s}", [P, P, 64]) for s in range(2)]
        ps_t = cx.enter_context(nc.psum_tensor("sg_pst", [P, 4, P], F32))
        ps = [cx.enter_context(nc.psum_tensor(f"sg_ps{s}", [P, BT, P], F32)) for s in range(2)]
        block = cx.enter_context(nc.Block("scatter_gates"))
        NG = HALF // BT

        @block.sync
        def _(sp):
            def load(n, s, rows):
                sp.wait_ge(tile_free, n + 1)
                for c, name in enumerate(("e1", "e2", "gate")):
                    sp.dma_start(raw[s][0:rows, c, :], t[name][bass.ds(n * P, rows), :]).then_inc(in_[s], 16)

            with sp.Fori(0, PT // 2) as i:
                for s in range(2):
                    load(i * 2 + s, s, P)
            load(PT, 0, NS)

        @block.tensor
        def _(pe):
            pe.sem_inc(tile_free, 2)

            def turn(n, s, i, rows):
                pe.wait_ge(in_[s], i * 48 + 48)
                pe.wait_ge(pk_done, n + 1)
                for c in range(3):
                    mm = nc.tensor.transpose(ps_t[:, c, 0:rows], raw[s][0:rows, c, :], pr.c("ident")[0:rows, 0:rows])
                mm.then_inc(turned, 1)

            def half(m):
                with pe.Fori(0, NG // 2) as j:
                    for s in range(2):
                        k = m * NG + j * 2 + s
                        pe.wait_ge(hot, k + 3)
                        pe.wait_ge(pool_hot, k + 3)
                        pe.wait_ge(evac, k + 1)
                        for b in range(BT):
                            mm = nc.tensor.matmul(ps[s][:, b, :], a[s][:, b, :], b_[s][b][:, :], start=True, stop=True)
                        mm.then_inc(product, 1)

            with pe.Fori(0, PT // 2) as i:
                for s in range(2):
                    turn(i * 2 + s, s, i, P)
                    for e in range(2):
                        half((i * 2 + s) * 2 + e)
            turn(PT, 0, PT // 2, NS)
            half(2 * PT)

        @block.vector
        def _(dve):
            dve.sem_inc(pk_done, 1)
            dve.sem_inc(hot, 2)
            dve.sem_inc(product, 2)

            def half(m, s, e):
                with dve.Fori(0, NG // 2) as j:
                    for g in range(2):
                        k = m * NG + j * 2 + g
                        dve.wait_ge(product, k + 1)
                        dve.sem_inc(passed, 1)
                        for b in range(BT - ON_POOL):
                            col = lambda c: pk[s][:, c, bass.ds(j * (2 * BT) + (e * HALF + g * BT + b), 1)]
                            nc.vector.tensor_scalar(b_[g][b][:, :], pr.c("iota128"), col(1), col(2), ALU.is_equal, ALU.mult)
                        e1 = pk[s][:, 0, bass.ds(j * (2 * BT) + (e * HALF + g * BT), BT)]
                        nc.vector.tensor_tensor(a[g][:, :, :], pr.c("iota128").unsqueeze(1).broadcast_to([P, BT, P]),
                                                e1.unsqueeze(2).broadcast_to([P, BT, P]), ALU.is_equal).then_inc(hot, 1)

            def tile(n, s, rows):
                dve.wait_ge(turned, n + 1)
                nc.vector.tensor_copy(pk[s][:, :, 0:rows], ps_t[:, 0:3, 0:rows]).then_inc(pk_done, 1)
                dve.sem_inc(tile_free, 1)
                dve.wait_ge(pk_done, n + 2)
                dve.sem_inc(passed, 1)
                for e in range(rows // HALF):
                    half(n * 2 + e, s, e)

            with dve.Fori(0, PT // 2) as i:
                for s in range(2):
                    tile(i * 2 + s, s, P)
            tile(PT, 0, NS)

        @block.gpsimd
        def _(pool):
            pool.sem_inc(pool_hot, 2)

            def half(m, s, e):
                with pool.Fori(0, NG // 2) as j:
                    for g in range(2):
                        k = m * NG + j * 2 + g
                        pool.wait_ge(product, k + 1)
                        pool.sem_inc(passed, 1)
                        cols = bass.ds(j * (2 * BT) + (e * HALF + g * BT + BT - ON_POOL), ON_POOL)
                        nc.gpsimd.tensor_copy(few[g][:, :, :], pk[s][:, 1:3, cols]).then_inc(few_done, 1)
                        pool.wait_ge(few_done, k + 1)
                        pool.sem_inc(passed, 1)
                        for b in range(BT - ON_POOL, BT):
                            scalar = lambda c: few[g][:, c, b - BT + ON_POOL:b - BT + ON_POOL + 1]
                            ins = nc.gpsimd.tensor_scalar(b_[g][b][:, :], pr.c("iota128"), scalar(0), scalar(1), ALU.is_equal, ALU.mult)
                        ins.then_inc(pool_hot, 1)

            def tile(n, s, rows):
                pool.wait_ge(pk_done, n + 2)
                pool.sem_inc(passed, 1)
                for e in range(rows // HALF):
                    half(n * 2 + e, s, e)

            with pool.Fori(0, PT // 2) as i:
                for s in range(2):
                    tile(i * 2 + s, s, P)
            tile(PT, 0, NS)

        @block.scalar
        def _(act):
            act.sem_inc(evac, 2)

            def half(m, e, i):
                act.wait_ge(stored[e], i * 16)
                act.sem_inc(passed, 1)
                with act.Fori(0, NG // 2) as j:
                    for s in range(2):
                        k = m * NG + j * 2 + s
                        act.wait_ge(product, k + 3)
                        out = stage[e][:, :, bass.ds(j * (2 * BT) + s * BT, BT)]
                        nc.scalar.copy(out, ps[s][:, :, :].rearrange("p t e -> p e t")).then_inc(evac, 1)
                act.wait_ge(evac, m * NG + NG + 2)
                act.dma_start(t["gate_all"][:, bass.ds(m, 1)].rearrange("p a e t -> p (a e) t"), stage[e][:, :, :])\
                    .then_inc(stored[e], 16)

            with act.Fori(0, PT) as i:
                for e in range(2):
                    half(i * 2 + e, e, i)
            half(2 * PT, 0, PT)
            act.wait_ge(stored[0], PT * 16 + 16)
            act.wait_ge(stored[1], PT * 16)


def experts(pr, h_hi, h_lo, acc, acc_t):
    nc, t = pr.nc, pr.t
    EB = 4
    NGR = KEYS // EB
    UNITS = [(m, a) for m in range(PT) for a in range(2)] + ["sample"]
    SHARE = (range(0, 4), range(4, 8), range(8, 12), range(12, 17))
    YB = 3
    more = lambda eb, n: not isinstance(eb, int) or eb + n < KEYS
    two = lambda name: [pr.sem(f"ex_{name}{s}") for s in range(2)]
    u_in, g_in = two("uin"), two("gin")
    v_in = pr.sem("ex_vin")
    (u_hi_done, u_lo_done, u_tr, ut_hi, ut_lo, acted, gelu_done, w_done, w_hi_done, w_lo_done, v_sc, v_hi_done, v_lo_done,
     y_done, added, ready, zeroed, passed) = (pr.sem(f"ex_{n}") for n in (
         "uhi", "ulo", "utr", "uthi", "utlo", "acted", "gelu", "w", "whi", "wlo", "vsc", "vhi", "vlo", "y", "added", "ready", "zeroed",
         "passed"))
    with ExitStack() as cx:
        sb = lambda name, shape, dt=F32: cx.enter_context(nc.sbuf_tensor(f"ex_{name}", shape, dt))
        ident = sb("ident", [P, P], F16)
        u = [sb(f"u{s}", [P, D]) for s in range(2)]
        u_hi, u_lo = ([sb(f"{n}{s}", [P, KD, P], F16) for s in range(2)] for n in ("uhi", "ulo"))
        ut_h, ut_l = ([sb(f"{n}{s}", [P, KD, P], F16) for s in range(2)] for n in ("uth", "utl"))
        gate = [sb(f"gate{s}", [P, TOK]) for s in range(2)]
        wa = sb("wa", [P, TOK])
        w_hi, w_lo = ([sb(f"{n}{s}", [P, TOK], F16) for s in range(2 * EB)] for n in ("whi", "wlo"))
        v = sb("v", [P, D])
        v_hi, v_lo = ([sb(f"{n}{s}", [P, D], F16) for s in range(2 * EB)] for n in ("vhi", "vlo"))
        ps_a = cx.enter_context(nc.psum_tensor("ex_psa", [P, 3 * 512], F32))
        ps_t = [cx.enter_context(nc.psum_tensor(f"ex_pst{s}", [P, KD, P], F16)) for s in range(2)]
        ps_y = [cx.enter_context(nc.psum_tensor(f"ex_psy{s}", [P, 512], F32)) for s in range(YB)]
        block = cx.enter_context(nc.Block("experts"))
        gates = t["gate_all"].rearrange("p m e t -> e p m t")
        rows_of = lambda table, eb: t[table][0].rearrange("(a b) d -> b a d", b=KEYS)[eb]

        def run(eng, half):
            half(0, None, 0)
            with eng.Fori(0, NGR // 2 - 1) as i:
                half(i * 2 + 1, i * 2, 1)
                half(i * 2 + 2, i * 2 + 1, 0)
            half(NGR - 1, NGR - 2, 1)
            half(None, NGR - 1, 0)

        @block.sync
        def _(sp):
            def half(g1, g2, p):
                if g1 is None:
                    return
                for b in range(EB):
                    eb, s = g1 * EB + b, b % 2
                    sp.wait_ge(u_lo_done, eb + 1)
                    sp.dma_start(u[s][:, :], rows_of("peer_u", eb)).then_inc(u_in[s], 16)
                    sp.wait_ge(w_done, eb + 1)
                    sp.dma_start(gate[s][:, :].rearrange("p (m t) -> p m t", t=HALF), gates[eb]).then_inc(g_in[s], 16)
                    sp.wait_ge(v_lo_done, eb + 1)
                    sp.dma_start(v[:, :], rows_of("peer_v", eb)).then_inc(v_in, 16)

            run(sp, half)

        @block.gpsimd
        def _(pool):
            nc.gpsimd.memset(acc[:, :, :], 0.0).then_inc(zeroed, 1)
            nc.gpsimd.memset(acc_t[:, :, :], 0.0).then_inc(zeroed, 1)
            pool.sem_inc(v_lo_done, 1)

            def half(g1, g2, p):
                if g1 is None:
                    return
                for b in range(EB):
                    eb, k = g1 * EB + b, EB * p + b
                    pool.wait_ge(v_in, eb * 16 + 16)
                    pool.sem_inc(passed, 1)
                    nc.gpsimd.tensor_scalar(v[:, :], v[:, :], SPLIT, None, ALU.mult).then_inc(v_sc, 1)
                    pool.wait_ge(v_sc, eb + 1)
                    pool.sem_inc(passed, 1)
                    if not (isinstance(g1, int) and g1 < 2):
                        pool.wait_ge(y_done, (g1 - 1) * len(UNITS))
                        pool.sem_inc(passed, 1)
                    nc.gpsimd.tensor_copy(v_hi[k][:, :], v[:, :]).then_inc(v_hi_done, 1)
                    pool.wait_ge(v_hi_done, eb + 1)
                    nc.gpsimd.tensor_tensor(v_lo[k][:, :], v[:, :], v_hi[k][:, :], ALU.subtract).then_inc(v_lo_done, 1)

            run(pool, half)

        @block.scalar
        def _(act):
            act.sem_inc(gelu_done, 1)

            def split(eb, s):
                act.wait_ge(u_in[s], (eb - s) * 8 + 16)
                act.wait_ge(u_tr, eb + 1)
                nc.scalar.activation(u_hi[s][:, :, :], u[s][:, :].rearrange("p (k d) -> p k d", k=KD), ACT.Copy, scale=SPLIT)\
                    .then_inc(u_hi_done, 1)

            def turned(eb, s):
                act.wait_ge(u_tr, eb + 3)
                act.wait_ge(acted, eb + 1)
                nc.scalar.copy(ut_h[s][:, :, :], ps_t[0][:, :, :]).then_inc(ut_hi, 1)

            def weights(eb, k, g1):
                act.wait_ge(acted, eb + 3)
                act.wait_ge(w_lo_done, eb + 1)
                nc.scalar.activation(wa[:, :], ps_a[:, 0:TOK], ACT.Gelu_apprx_tanh, scale=1.0 / SPLIT).then_inc(gelu_done, 1)
                act.wait_ge(w_done, eb + 3)
                if not (isinstance(g1, int) and g1 < 2):
                    act.wait_ge(y_done, (g1 - 1) * len(UNITS))
                nc.scalar.activation(w_hi[k][:, :], wa[:, :], ACT.Copy).then_inc(w_hi_done, 1)

            def half(g1, g2, p):
                for b in range(EB) if g1 is not None else ():
                    eb = g1 * EB + b
                    if more(eb, 1):
                        turned(eb + 1, 1 - b % 2)
                    if more(eb, 2):
                        split(eb + 2, b % 2)
                    weights(eb, EB * p + b, g1)

            split(0, 0)
            split(1, 1)
            turned(0, 0)
            run(act, half)

        @block.vector
        def _(dve):
            V = nc.vector
            V.tensor_copy(ident[:, :], pr.c("ident")).then_inc(ready, 1)
            dve.wait_ge(ready, 1)
            dve.sem_inc(u_lo_done, 2)
            dve.sem_inc(w_done, 2)
            dve.sem_inc(w_lo_done, 1)
            dve.sem_inc(added, YB)

            def split(eb, s):
                dve.wait_ge(u_hi_done, eb + 1)
                V.scalar_tensor_tensor(u_lo[s][:, :, :].rearrange("p k d -> p (k d)"), u[s][:, :], SPLIT,
                                       u_hi[s][:, :, :].rearrange("p k d -> p (k d)"), ALU.mult, ALU.subtract)\
                    .then_inc(u_lo_done, 1)

            def turned(eb, s):
                dve.wait_ge(u_tr, eb + 3)
                dve.wait_ge(acted, eb + 1)
                V.tensor_copy(ut_l[s][:, :, :], ps_t[1][:, :, :]).then_inc(ut_lo, 1)

            def half(g1, g2, p):
                for b in range(EB):
                    if g1 is not None:
                        eb, s, k = g1 * EB + b, b % 2, EB * p + b
                        if more(eb, 1):
                            turned(eb + 1, 1 - s)
                        if more(eb, 2):
                            split(eb + 2, s)
                        dve.wait_ge(gelu_done, eb + 2)
                        dve.wait_ge(g_in[s], (eb - s) * 8 + 16)
                        V.scalar_tensor_tensor(wa[:, :], wa[:, :], WSCALE, gate[s][:, :], ALU.mult, ALU.mult).then_inc(w_done, 1)
                        dve.wait_ge(w_hi_done, eb + 1)
                        V.tensor_tensor(w_lo[k][:, :], wa[:, :], w_hi[k][:, :], ALU.subtract).then_inc(w_lo_done, 1)
                    for n in SHARE[b] if g2 is not None else ():
                        dve.wait_ge(y_done, g2 * len(UNITS) + n + 1)
                        if UNITS[n] == "sample":
                            part = acc_t[:, :, :].rearrange("p k t -> p (k t)")
                        else:
                            m, a = UNITS[n]
                            part = acc[:, m, a * 512:(a + 1) * 512]
                        V.tensor_tensor(part, part, ps_y[n % YB][:, :], ALU.add).then_inc(added, 1)

            split(0, 0)
            split(1, 1)
            turned(0, 0)
            dve.wait_ge(zeroed, 2)
            run(dve, half)

        @block.tensor
        def _(pe):
            pe.wait_ge(ready, 1)
            pe.sem_inc(u_tr, 2)
            pe.sem_inc(acted, 2)

            def turn(eb, s):
                pe.wait_ge(u_lo_done, eb + 3)
                pe.wait_ge(u_hi_done, eb + 1)
                pe.wait_ge(ut_hi, eb)
                pe.wait_ge(ut_lo, eb)
                for part, src in enumerate((u_hi, u_lo)):
                    for k in range(KD):
                        mm = nc.tensor.transpose(ps_t[part][:, k, :], src[s][:, k, :], ident[:, :])
                mm.then_inc(u_tr, 1)

            def products(eb, s):
                pe.wait_ge(ut_hi, eb + 1)
                pe.wait_ge(ut_lo, eb + 1)
                pe.wait_ge(gelu_done, eb + 1)
                mms = [(x, h, k) for k in range(KD) for x, h in ((ut_h, h_hi), (ut_h, h_lo), (ut_l, h_hi))]
                for j, (x, h, k) in enumerate(mms):
                    for c in range(0, TOK, 512):
                        e = min(c + 512, TOK)
                        mm = nc.tensor.matmul(ps_a[:, c:e], x[s][:, k, :], h[:, k, c:e],
                                              start=(j == 0), stop=(j == len(mms) - 1))
                mm.then_inc(acted, 1)

            def unit(g2, n, q):
                pe.wait_ge(added, g2 * len(UNITS) + n + (2 if n < 2 else 1))
                mms = [(w, v_, EB * q + b) for b in range(EB) for w, v_ in ((w_hi, v_hi), (w_hi, v_lo), (w_lo, v_hi))]
                for c in range(KD) if UNITS[n] == "sample" else (None,):
                    for j, (w, v_, k) in enumerate(mms):
                        if c is None:
                            m, a = UNITS[n]
                            out, x, y = ps_y[n % YB][:, :], w[k][:, m * P:(m + 1) * P], v_[k][:, a * 512:(a + 1) * 512]
                        else:
                            out, x, y = ps_y[n % YB][:, c * NS:(c + 1) * NS], v_[k][:, c * P:(c + 1) * P], w[k][:, SEQ:TOK]
                        mm = nc.tensor.matmul(out, x, y, start=(j == 0), stop=(j == len(mms) - 1))
                mm.then_inc(y_done, 1)

            def half(g1, g2, p):
                for b in range(EB):
                    if g1 is not None:
                        eb = g1 * EB + b
                        if more(eb, 1):
                            turn(eb + 1, 1 - b % 2)
                        products(eb, b % 2)
                    if g2 is not None and b == 0:
                        pe.wait_ge(w_lo_done, (g2 + 1) * EB + 1)
                        pe.wait_ge(v_lo_done, (g2 + 1) * EB + 1)
                    for n in SHARE[b] if g2 is not None else ():
                        unit(g2, n, 1 - p)

            pe.wait_ge(u_lo_done, 3)
            pe.wait_ge(u_hi_done, 1)
            for part, src in enumerate((u_hi, u_lo)):
                for k in range(KD):
                    mm = nc.tensor.transpose(ps_t[part][:, k, :], src[0][:, k, :], ident[:, :])
            mm.then_inc(u_tr, 1)
            run(pe, half)


def output_norm(pr, acc, acc_t):
    nc, t = pr.nc, pr.t
    turned = pr.sem("on_turned")
    base_in, xg, x2, ssq, ms, ln, rstd, newton, y_ready, stored, o_free = (pr.sem(f"on_{n}") for n in (
        "base", "xg", "x2", "ssq", "ms", "ln", "rstd", "newton", "y", "stored", "ofree"))
    x_in = [pr.sem(f"on_in{s}") for s in range(2)]
    with ExitStack() as cx:
        sb = lambda name, shape: cx.enter_context(nc.sbuf_tensor(f"on_{name}", shape, F32))
        x = [sb(f"x{s}", [P, D]) for s in range(2)]
        y = [sb(f"y{s}", [P, D]) for s in range(2)]
        o = [sb(f"o{s}", [P, D]) for s in range(2)]
        st = [sb(f"st{s}", [P, 8]) for s in range(2)]
        g2, fg, junk = [sb(f"g2{s}", [P, D]) for s in range(2)], sb("fg", [P, D]), sb("junk", [P, D])
        ps_x = cx.enter_context(nc.psum_tensor("on_psx", [P, D], F32))
        block = cx.enter_context(nc.Block("output_norm"))

        def tiles(eng, *steps):
            with eng.Fori(0, PT // 2) as i:
                for step in steps:
                    for s in range(2):
                        step(i * 2 + s, s, i, P)
            for step in steps:
                step(PT, 0, PT // 2, NS)

        @block.sync
        def _(sp):
            for r, (a, n) in enumerate(((0, P), (P, NS))):
                sp.dma_start(g2[r][0:n, :], t["modrep"][a:a + n, 5 * D:6 * D]).then_inc(base_in, 16)
            sp.dma_start(fg[:, :], t["final_norm_g"].partition_broadcast(P)).then_inc(base_in, 16)

            def tile(n, s, i, rows):
                sp.wait_ge(x2, n + 1)
                sp.dma_start(x[s][0:rows, :], t["x1"][bass.ds(n * P, rows), :]).then_inc(x_in[s], 16)
            tiles(sp, tile)

        @block.tensor
        def _(pe):
            for k in range(KD):
                tr = nc.tensor.transpose(ps_x[0:NS, k * P:(k + 1) * P], acc_t[:, k, :], pr.c("ident"))
            tr.then_inc(turned, 1)

        @block.vector
        def _(dve):
            V = nc.vector
            dve.sem_inc(x2, 2)
            dve.wait_ge(base_in, 48)

            def residual(n, s, i, rows):
                r = slice(0, rows)
                dve.wait_ge(x_in[s], i * 16 + 16)
                if rows == P:
                    part = acc[:, bass.ds(n, 1), :].rearrange("p a d -> p (a d)")
                else:
                    dve.wait_ge(turned, 1)
                    part = ps_x[r, :]
                V.scalar_tensor_tensor(y[s][r, :], part, 1.0 / (SPLIT * WSCALE), g2[0 if rows == P else 1][r, :],
                                       ALU.mult, ALU.mult).then_inc(xg, 1)
                dve.wait_ge(xg, n + 1)
                V.tensor_tensor(y[s][r, :], y[s][r, :], x[s][r, :], ALU.add).then_inc(x2, 1)

            def mean(n, s, i, rows):
                r = slice(0, rows)
                dve.wait_ge(ssq, n + 1)
                V.tensor_scalar(st[s][r, 1:2], st[s][r, 0:1], 1.0 / D, EPS, ALU.mult, ALU.add).then_inc(ms, 1)

            def scale(n, s, i, rows):
                r = slice(0, rows)
                dve.wait_ge(rstd, n + 1)
                step = Ordered(dve, newton)
                step.turn(n, 3, 0)
                step(V.scalar_tensor_tensor(st[s][r, 4:5], st[s][r, 3:4], st[s][r, 1:2], st[s][r, 3:4], ALU.mult, ALU.mult))
                step(V.tensor_scalar(st[s][r, 4:5], st[s][r, 4:5], -0.5, 1.5, ALU.mult, ALU.add))
                step(V.tensor_tensor(st[s][r, 5:6], st[s][r, 3:4], st[s][r, 4:5], ALU.mult))
                dve.wait_ge(o_free, n + 1)
                V.scalar_tensor_tensor(o[s][r, :], y[s][r, :], st[s][r, 5:6], fg[r, :], ALU.mult, ALU.mult).then_inc(y_ready, 1)
            tiles(dve, residual, mean, scale)

        @block.scalar
        def _(act):
            def squares(n, s, i, rows):
                r = slice(0, rows)
                act.wait_ge(x2, n + 3)
                nc.scalar.activation(junk[r, :], y[s][r, :], ACT.Square, accum_out=st[s][r, 0:1]).then_inc(ssq, 1)
                act.wait_ge(ssq, n + 1)

            def root(n, s, i, rows):
                r = slice(0, rows)
                act.wait_ge(ms, n + 1)
                nc.scalar.activation(st[s][r, 2:3], st[s][r, 1:2], ACT.Ln).then_inc(ln, 1)
                act.wait_ge(ln, n + 1)
                nc.scalar.activation(st[s][r, 3:4], st[s][r, 2:3], ACT.Exp, scale=-0.5).then_inc(rstd, 1)
            tiles(act, squares, root)

        @block.gpsimd
        def _(pool):
            pool.sem_inc(o_free, 2)

            def tile(n, s, i, rows):
                pool.wait_ge(y_ready, n + 1)
                whole = t["y_prompt"][0] if rows == P else t["y_sample"].rearrange("b t d -> (b t) d")
                dst = whole[bass.ds(n * P, P), :] if rows == P else whole
                pool.dma_start(dst, o[s][0:rows, :]).then_inc(stored, 16)
                pool.wait_ge(stored, n * 16 + 16)
                pool.sem_inc(o_free, 1)
            tiles(pool, tile)


def peer(pr):
    nc, t = pr.nc, pr.t
    with nc.sbuf_tensor("h_hi", [P, KD, TOK], F16) as h_hi, nc.sbuf_tensor("h_lo", [P, KD, TOK], F16) as h_lo:
        with nc.sbuf_tensor("ht2", [P, KD, TOK], F32) as ht:
            norm_modulate(pr, "n2", t["x1"][0:SEQ, :], t["x1"][SEQ:TOK, :], t["norm2_g"][0], 4, 3, h_hi, h_lo, ht)
            pr.clear_semaphores()
            with nc.sbuf_tensor("wsc", [P, KD, 2 * HEADS * KEYS], F32) as wsc:
                score_weights(pr, wsc)
                routing(pr, ht, wsc)
        pr.clear_semaphores()
        scatter_gates(pr)
        pr.clear_semaphores()
        with nc.sbuf_tensor("acc", [P, PT, D], F32) as acc, nc.sbuf_tensor("acc_t", [P, KD, NS], F32) as acc_t:
            experts(pr, h_hi, h_lo, acc, acc_t)
            output_norm(pr, acc, acc_t)


STAGES = (conditioning, mixer_input, attention_prompt, attention_sample, attention_merge, recurrence, mixer_merge,
          mixer_output, peer)


def build(nc, t, scratch_kind="Internal", stages=None):
    with ExitStack() as ctx:
        pr = Program(nc, t, ctx, scratch_kind)
        load_constants(pr)
        for n, stage in enumerate(STAGES):
            if stages is None or n in stages:
                stage(pr)
                pr.clear_semaphores()


_INS = ["x_prompt", "x_sample", "cache_k0", "cache_v0", "cache_k1", "cache_v1", "cache_k2", "cache_v2", "state_hgrn",
        "c_prompt", "c_sample", "ada_w", "ada_b", "norm1_g", "w_in", "w_att_branch", "w_hg_branch", "w_out",
        "hg_lower_bound", "hg_norm_g", "norm2_g", "peer_wq", "peer_subkeys", "peer_u", "peer_v", "final_norm_g"]
_OUTS = [("y_prompt", (1, 1024, 1024)), ("y_sample", (8, 8, 1024)),
         ("k0_p", (1, 1, 128, 4, 64)), ("v0_p", (1, 1, 128, 4, 64)), ("k1_p", (1, 1, 512, 4, 64)),
         ("v1_p", (1, 1, 512, 4, 64)), ("k2_p", (1, 1, 1024, 4, 64)), ("v2_p", (1, 1, 1024, 4, 64)),
         ("hgrn_p", (1, 1, 4, 128, 128)),
         ("k0_s", (1, 8, 128, 4, 64)), ("v0_s", (1, 8, 128, 4, 64)), ("k1_s", (1, 8, 512, 4, 64)),
         ("v1_s", (1, 8, 512, 4, 64)), ("k2_s", (1, 8, 1024, 4, 64)), ("v2_s", (1, 8, 1024, 4, 64)),
         ("hgrn_s", (1, 8, 4, 128, 128))]


def kernel(**inputs):
    import concourse.bacc as _bacc
    from concourse.bass_utils import run_bass_kernel_spmd as _run

    nc = _bacc.Bacc("TRN2", target_bir_lowering=False, num_devices=1)
    arrays, t = {"in_const_dram": CONST}, {}
    for name in _INS:
        arrays[f"in_{name}_dram"] = np.ascontiguousarray(inputs[name])
    for name, a in arrays.items():
        t[name[3:-5]] = nc.dram_tensor(name, a.shape, mybir.dt.from_np(a.dtype), kind="ExternalInput").ap()
    for name, shape in _OUTS:
        t[name] = nc.dram_tensor(f"out_{name}_dram", shape, F32, kind="ExternalOutput").ap()
    build(nc, t)
    r = _run(nc, [arrays], core_ids=[0])
    return tuple(r.results[0][f"out_{name}_dram"] for name, _ in _OUTS)
```
